# Optimizing a Trainium2 kernel written in Bass

```python
import numpy as np
import jax
import jax.numpy as jnp
from jax import lax

D_MODEL = 2048
BATCH = 1
SEQ = 512
DEPTH = 1

GRID_W = 64
CTX_LEN = 256
EPS = 1e-6
NEG_INF = -1e30

NA_HEADS = 16
NA_HEAD_DIM = 64
NA_WIDTH = NA_HEADS * NA_HEAD_DIM
NA_WIN_H = 8
NA_WIN_W = 16
NA_QBLOCK_W = 16
NA_BAND_W = NA_QBLOCK_W + NA_WIN_W
NA_SCALE = NA_HEAD_DIM ** -0.5

MLA_HEADS = 8
MLA_NOPE_DIM = 128
MLA_ROPE_DIM = 64
MLA_V_DIM = 128
MLA_WIDTH = MLA_HEADS * MLA_V_DIM
MLA_Q_RANK = 768
MLA_KV_RANK = 512
MLA_Q_BLOCK = 128
MLA_SCALE = (MLA_NOPE_DIM + MLA_ROPE_DIM) ** -0.5
ROPE_THETA = 10000.0

PEER_HEADS = 8
PEER_N_KEYS = 128
PEER_N_EXPERTS = PEER_N_KEYS * PEER_N_KEYS
PEER_KEY_DIM = 256
PEER_TOPK = 16
PEER_TOKEN_BLOCK = 128

IN_SPLITS = (NA_WIDTH, NA_WIDTH, NA_WIDTH, MLA_Q_RANK, MLA_KV_RANK, MLA_ROPE_DIM, D_MODEL, D_MODEL)
IN_COLS = sum(IN_SPLITS)

kernel_name = 'hybrid_natten_mla_peer_dit_block'

def _rms(x, g):
    xf = x.astype(jnp.float32)
    y = xf * lax.rsqrt(jnp.mean(xf * xf, axis=-1, keepdims=True) + EPS)
    return (y * g.astype(jnp.float32)).astype(x.dtype)

def _modulate(h, shift, scale):
    return h * (1 + scale) + shift

def _split_in(p):
    return jnp.split(p, np.cumsum(IN_SPLITS)[:-1].tolist(), axis=-1)

def _heads(t, n):
    return t.reshape(t.shape[0], t.shape[1], n, -1)

def _axial_rope(n_tokens):
    t = jnp.arange(n_tokens)
    row = (t // GRID_W).astype(jnp.float32)
    col = (t % GRID_W).astype(jnp.float32)
    quarter = MLA_ROPE_DIM // 4
    inv_freq = ROPE_THETA ** (-jnp.arange(quarter, dtype=jnp.float32) / quarter)
    ang = jnp.concatenate([row[:, None] * inv_freq, col[:, None] * inv_freq], axis=-1)
    return jnp.cos(ang), jnp.sin(ang)

def _rope(x, cos, sin):
    xf = x.astype(jnp.float32)
    half = xf.shape[-1] // 2
    x1, x2 = xf[..., :half], xf[..., half:]
    return jnp.concatenate([x1 * cos - x2 * sin, x1 * sin + x2 * cos], axis=-1).astype(x.dtype)

def _neighbourhood_attention(q, k, v, kc, vc, rpb):
    b, s, h, dh = q.shape
    rows = s // GRID_W
    kh = min(NA_WIN_H, rows)
    nqb = GRID_W // NA_QBLOCK_W
    nk = kh * NA_BAND_W
    qcol = np.arange(GRID_W).reshape(nqb, NA_QBLOCK_W)
    band_start = np.clip(np.arange(nqb) * NA_QBLOCK_W - NA_WIN_W // 2, 0, GRID_W - NA_BAND_W)
    band_cols = band_start[:, None] + np.arange(NA_BAND_W)
    win_start = np.clip(qcol - NA_WIN_W // 2, 0, GRID_W - NA_WIN_W)
    off = band_cols[:, None, :] - win_start[:, :, None]
    col_ok = (off >= 0) & (off < NA_WIN_W)
    mask = np.broadcast_to(col_ok[:, :, None, :], (nqb, NA_QBLOCK_W, kh, NA_BAND_W)).reshape(nqb, NA_QBLOCK_W, nk)
    dx_idx = np.clip(band_cols[:, None, :] - qcol[:, :, None] + NA_WIN_W - 1, 0, 2 * NA_WIN_W - 2)
    kg = k.reshape(b, rows, GRID_W, h, dh)
    vg = v.reshape(b, rows, GRID_W, h, dh)
    qg = q.reshape(b, rows, nqb, NA_QBLOCK_W, h, dh).swapaxes(0, 1)

    def row_block(args):
        r, qr = args
        r0 = jnp.clip(r - NA_WIN_H // 2, 0, rows - kh)
        kb = lax.dynamic_slice_in_dim(kg, r0, kh, axis=1)[:, :, band_cols]
        vb = lax.dynamic_slice_in_dim(vg, r0, kh, axis=1)[:, :, band_cols]
        kb = kb.transpose(0, 2, 1, 3, 4, 5).reshape(b, nqb, nk, h, dh)
        vb = vb.transpose(0, 2, 1, 3, 4, 5).reshape(b, nqb, nk, h, dh)
        dy_idx = r0 + jnp.arange(kh) - r + NA_WIN_H - 1
        bias = rpb[:, dy_idx[:, None, None, None], dx_idx[None]]
        bias = bias.transpose(2, 0, 3, 1, 4).reshape(nqb, h, NA_QBLOCK_W, nk)
        s_lat = jnp.einsum('bjqhd,bjkhd->bjhqk', qr, kb).astype(jnp.float32) * NA_SCALE + bias.astype(jnp.float32)
        s_lat = jnp.where(mask[None, :, None], s_lat, NEG_INF)
        s_ctx = jnp.einsum('bjqhd,blhd->bjhql', qr, kc).astype(jnp.float32) * NA_SCALE
        p = jax.nn.softmax(jnp.concatenate([s_lat, s_ctx], axis=-1), axis=-1).astype(v.dtype)
        return (jnp.einsum('bjhqk,bjkhd->bjqhd', p[..., :nk], vb)
                + jnp.einsum('bjhql,blhd->bjqhd', p[..., nk:], vc))

    out = lax.map(row_block, (jnp.arange(rows), qg))
    return out.swapaxes(0, 1).reshape(b, s, h * dh)

def _na_context(q, k, v):
    s = jnp.einsum('bqhd,bkhd->bhqk', q, k).astype(jnp.float32) * NA_SCALE
    p = jax.nn.softmax(s, axis=-1).astype(v.dtype)
    return jnp.einsum('bhqk,bkhd->bqhd', p, v).reshape(q.shape[0], q.shape[1], -1)

def _mla_queries(cq, g_q, w_q_b, rope):
    q = _heads(_rms(cq, g_q) @ w_q_b, MLA_HEADS)
    q_nope, q_pe = q[..., :MLA_NOPE_DIM], q[..., MLA_NOPE_DIM:]
    if rope is not None:
        q_pe = _rope(q_pe, rope[0][:, None], rope[1][:, None])
    return q_nope, q_pe

def _mla_keys(ckv, kpe, g_kv, w_kv_b, rope):
    kv = _heads(_rms(ckv, g_kv) @ w_kv_b, MLA_HEADS)
    k_nope, val = kv[..., :MLA_NOPE_DIM], kv[..., MLA_NOPE_DIM:]
    if rope is not None:
        kpe = _rope(kpe, rope[0], rope[1])
    return k_nope, kpe, val

def _mla_attend(qn, qp, kn, kp, v):
    s = jnp.einsum('bqhn,bkhn->bhqk', qn, kn) + jnp.einsum('bqhr,bkr->bhqk', qp, kp)
    p = jax.nn.softmax(s.astype(jnp.float32) * MLA_SCALE, axis=-1).astype(v.dtype)
    return jnp.einsum('bhqk,bkhv->bqhv', p, v)

def _mla_latent(qn, qp, kn, kp, v):
    b, s = qn.shape[0], qn.shape[1]
    nb = s // MLA_Q_BLOCK
    qn_b = qn.reshape(b, nb, MLA_Q_BLOCK, MLA_HEADS, MLA_NOPE_DIM).swapaxes(0, 1)
    qp_b = qp.reshape(b, nb, MLA_Q_BLOCK, MLA_HEADS, MLA_ROPE_DIM).swapaxes(0, 1)
    out = lax.map(lambda a: _mla_attend(a[0], a[1], kn, kp, v), (qn_b, qp_b))
    return out.swapaxes(0, 1).reshape(b, s, MLA_WIDTH)

def _merge(oa, ob, ga, gb, lp):
    y = jax.nn.sigmoid(ga) * (oa @ lp['w_branch_a']) + jax.nn.sigmoid(gb) * (ob @ lp['w_branch_b'])
    return y @ lp['w_out']

def _token_mixing(h, hc, lp, rope, with_ctx_out):
    qa, ka, va, cq, ckv, kpe, ga, gb = _split_in(h @ lp['w_in'])
    qac, kac, vac, cqc, ckvc, kpec, gac, gbc = _split_in(hc @ lp['w_in'])
    kac_h, vac_h = _heads(kac, NA_HEADS), _heads(vac, NA_HEADS)
    oa = _neighbourhood_attention(_heads(qa, NA_HEADS), _heads(ka, NA_HEADS), _heads(va, NA_HEADS),
                                  kac_h, vac_h, lp['na_rpb'])
    qn, qp = _mla_queries(cq, lp['mla_g_q'], lp['mla_w_q_b'], rope)
    kn, kp, vb = _mla_keys(ckv, kpe, lp['mla_g_kv'], lp['mla_w_kv_b'], rope)
    knc, kpc, vbc = _mla_keys(ckvc, kpec, lp['mla_g_kv'], lp['mla_w_kv_b'], None)
    ob = _mla_latent(qn, qp, jnp.concatenate([kn, knc], axis=1), jnp.concatenate([kp, kpc], axis=1),
                     jnp.concatenate([vb, vbc], axis=1))
    y = _merge(oa, ob, ga, gb, lp)
    if not with_ctx_out:
        return y, None
    oac = _na_context(_heads(qac, NA_HEADS), kac_h, vac_h)
    qnc, qpc = _mla_queries(cqc, lp['mla_g_q'], lp['mla_w_q_b'], None)
    obc = _mla_attend(qnc, qpc, knc, kpc, vbc).reshape(hc.shape[0], hc.shape[1], MLA_WIDTH)
    yc = _merge(oac, obc, gac, gbc, lp)
    return y, yc

def _peer(h, lp):
    b, s, d = h.shape
    t = b * s
    hf = h.reshape(t, d)
    q = (hf @ lp['peer_w_query']).reshape(t, PEER_HEADS, 2, PEER_KEY_DIM // 2)
    sc = jnp.einsum('thpk,hpnk->thpn', q, lp['peer_subkeys']).astype(jnp.float32)
    v1, i1 = lax.top_k(sc[:, :, 0], PEER_TOPK)
    v2, i2 = lax.top_k(sc[:, :, 1], PEER_TOPK)
    cand_s = (v1[..., :, None] + v2[..., None, :]).reshape(t, PEER_HEADS, PEER_TOPK * PEER_TOPK)
    cand_i = (i1[..., :, None] * PEER_N_KEYS + i2[..., None, :]).reshape(t, PEER_HEADS, PEER_TOPK * PEER_TOPK)
    top_s, pos = lax.top_k(cand_s, PEER_TOPK)
    idx = jnp.take_along_axis(cand_i, pos, axis=-1)
    gate = jax.nn.softmax(top_s, axis=-1).astype(h.dtype)
    u, v = lp['peer_u'], lp['peer_v']
    nb = t // PEER_TOKEN_BLOCK

    def blk(args):
        hb, ib, gb = args
        act = jax.nn.gelu(jnp.einsum('td,thkd->thk', hb, u[ib]), approximate=False)
        return jnp.einsum('thk,thkd->td', gb * act, v[ib])

    out = lax.map(blk, (hf.reshape(nb, PEER_TOKEN_BLOCK, d),
                        idx.reshape(nb, PEER_TOKEN_BLOCK, PEER_HEADS, PEER_TOPK),
                        gate.reshape(nb, PEER_TOKEN_BLOCK, PEER_HEADS, PEER_TOPK)))
    return out.reshape(b, s, d)

def _layer(x, xc, c, c_ctx, lp, rope, update_ctx):
    mod = (jax.nn.silu(c) @ lp['w_ada'] + lp['b_ada'])[:, None, :]
    modc = jax.nn.silu(c_ctx) @ lp['w_ada'] + lp['b_ada']
    sh1, sc1, gt1, sh2, sc2, gt2 = jnp.split(mod, 6, axis=-1)
    shc1, scc1, gtc1, shc2, scc2, gtc2 = jnp.split(modc, 6, axis=-1)
    h = _modulate(_rms(x, lp['g_pre_mix']), sh1, sc1)
    hc = _modulate(_rms(xc, lp['g_pre_mix']), shc1, scc1)
    y, yc = _token_mixing(h, hc, lp, rope, update_ctx)
    x = x + gt1 * _rms(y, lp['g_post_mix'])
    h2 = _modulate(_rms(x, lp['g_pre_ffn']), sh2, sc2)
    x = x + gt2 * _rms(_peer(h2, lp), lp['g_post_ffn'])
    if update_ctx:
        xc = xc + gtc1 * _rms(yc, lp['g_post_mix'])
        h2c = _modulate(_rms(xc, lp['g_pre_ffn']), shc2, scc2)
        xc = xc + gtc2 * _rms(_peer(h2c, lp), lp['g_post_ffn'])
    return x, xc

def setup_inputs(seed: int = 0) -> dict:
    key = jax.random.key(seed)
    ks = jax.random.split(key, 24)
    f32 = jnp.float32
    L = DEPTH

    def nrm(k, shape, scale):
        return jax.random.normal(k, shape, f32) * scale

    def gain(k, shape):
        return 1.0 + 0.1 * jax.random.normal(k, shape, f32)

    return {
        'x': nrm(ks[0], (BATCH, SEQ, D_MODEL), 1.0),
        'c': nrm(ks[1], (BATCH, D_MODEL), 1.0),
        'ctx': nrm(ks[2], (BATCH, CTX_LEN, D_MODEL), 1.0),
        'c_ctx': nrm(ks[3], (D_MODEL,), 1.0),
        'w_ada': nrm(ks[4], (L, D_MODEL, 6 * D_MODEL), 0.5 * D_MODEL ** -0.5),
        'b_ada': nrm(ks[5], (L, 6 * D_MODEL), 0.01),
        'g_pre_mix': gain(ks[6], (L, D_MODEL)),
        'g_post_mix': gain(ks[7], (L, D_MODEL)),
        'g_pre_ffn': gain(ks[8], (L, D_MODEL)),
        'g_post_ffn': gain(ks[9], (L, D_MODEL)),
        'w_in': nrm(ks[10], (L, D_MODEL, IN_COLS), D_MODEL ** -0.5),
        'na_rpb': nrm(ks[11], (L, NA_HEADS, 2 * NA_WIN_H - 1, 2 * NA_WIN_W - 1), 0.1),
        'mla_g_q': gain(ks[12], (L, MLA_Q_RANK)),
        'mla_w_q_b': nrm(ks[13], (L, MLA_Q_RANK, MLA_HEADS * (MLA_NOPE_DIM + MLA_ROPE_DIM)), MLA_Q_RANK ** -0.5),
        'mla_g_kv': gain(ks[14], (L, MLA_KV_RANK)),
        'mla_w_kv_b': nrm(ks[15], (L, MLA_KV_RANK, MLA_HEADS * (MLA_NOPE_DIM + MLA_V_DIM)), MLA_KV_RANK ** -0.5),
        'w_branch_a': nrm(ks[16], (L, NA_WIDTH, D_MODEL), NA_WIDTH ** -0.5),
        'w_branch_b': nrm(ks[17], (L, MLA_WIDTH, D_MODEL), MLA_WIDTH ** -0.5),
        'w_out': nrm(ks[18], (L, D_MODEL, D_MODEL), D_MODEL ** -0.5),
        'peer_w_query': nrm(ks[19], (L, D_MODEL, PEER_HEADS * PEER_KEY_DIM), D_MODEL ** -0.5),
        'peer_subkeys': nrm(ks[20], (L, PEER_HEADS, 2, PEER_N_KEYS, PEER_KEY_DIM // 2), (PEER_KEY_DIM // 2) ** -0.5),
        'peer_u': nrm(ks[21], (L, PEER_N_EXPERTS, D_MODEL), D_MODEL ** -0.5),
        'peer_v': nrm(ks[22], (L, PEER_N_EXPERTS, D_MODEL), (PEER_HEADS * PEER_TOPK) ** -0.5),
    }

def reference(x, c, ctx, c_ctx, w_ada, b_ada, g_pre_mix, g_post_mix, g_pre_ffn, g_post_ffn, w_in, na_rpb,
              mla_g_q, mla_w_q_b, mla_g_kv, mla_w_kv_b, w_branch_a, w_branch_b, w_out,
              peer_w_query, peer_subkeys, peer_u, peer_v):
    rope = _axial_rope(x.shape[1])
    xc = ctx
    for l in range(DEPTH):
        lp = {
            'w_ada': w_ada[l], 'b_ada': b_ada[l],
            'g_pre_mix': g_pre_mix[l], 'g_post_mix': g_post_mix[l],
            'g_pre_ffn': g_pre_ffn[l], 'g_post_ffn': g_post_ffn[l],
            'w_in': w_in[l], 'na_rpb': na_rpb[l],
            'mla_g_q': mla_g_q[l], 'mla_w_q_b': mla_w_q_b[l],
            'mla_g_kv': mla_g_kv[l], 'mla_w_kv_b': mla_w_kv_b[l],
            'w_branch_a': w_branch_a[l], 'w_branch_b': w_branch_b[l], 'w_out': w_out[l],
            'peer_w_query': peer_w_query[l], 'peer_subkeys': peer_subkeys[l],
            'peer_u': peer_u[l], 'peer_v': peer_v[l],
        }
        x, xc = _layer(x, xc, c, c_ctx, lp, rope, l < DEPTH - 1)
    return x


_drawn_inputs = setup_inputs


def setup_inputs(seed=0):
    import zlib

    import numpy as np

    out = dict(_drawn_inputs(seed))
    spreads = {}
    factors = {}
    for name, (base, spread) in spreads.items():
        noise = np.random.default_rng([zlib.crc32(name.encode()), seed]).standard_normal(out[name].shape)
        drawn = base * np.exp(spread * noise) if base else spread * noise
        out[name] = jnp.asarray(drawn.astype(out[name].dtype))
    for name, factor in factors.items():
        out[name] = (out[name] * factor).astype(out[name].dtype)
    return out
```

```python
import numpy as np
import concourse.bass as bass
from concourse import mybir

F32 = mybir.dt.float32
F32R = mybir.dt.float32r
U32 = mybir.dt.uint32
ALU = mybir.AluOpType
ACT = mybir.ActivationFunctionType
AX = mybir.AxisListType

P = 128
D = 2048
KD = D // P
T = 512
C = 256
TC = T + C
ROWS = 8
GRID_W = 64
EPS = 1e-6
MLA_SCALE = float((128 + 64) ** -0.5)
NA_SCALE = 0.125

RING = 4
UW = 1024
BOTH_BLOCKS = 21
LAT_BLOCKS = 46
N_BOTH = 0
N_LAT = N_BOTH + 2 * BOTH_BLOCKS
N_KN = N_LAT + 2 * LAT_BLOCKS
N_V = N_KN + 4
N_QB = N_V + 4
N_MERGE = N_QB + 12
N_OUT = N_MERGE + 32
N_QUERY = N_OUT + 32
N_MAIN = N_QUERY + 32
GROUPS = 32
N_END = N_MAIN + GROUPS * 16
B_CKV, B_KPE, B_KA, B_VA = 0, 4, 5, 13
L_CQ, L_QA, L_GA, L_GB = 0, 6, 14, 30
BAND = [0, 64, 192, 256]
SHIFT = [0, 1, 1, 2]
V_CHUNKS = [0, 128, 64, 192, 320, 256, 384, 512, 640]
V_OF = [(0, 1), (2, 3), (3, 4), (5, 6)]
CHOICE_STEPS = 2 * 4 * 5 + 1 + 1 + 4 * 5 + 3 + 2 * 3 + 2 + 1
VEC_B, VEC_PRE, VEC_POST, VEC_PREF, VEC_POSTF, VEC_GQ, VEC_GKV = 0, 96, 112, 128, 144, 160, 166
NVEC = 170
TCH = 64
NA_UNITS = 64
DX = 63


def dram(ap, offset, pattern):
    return bass.AP(tensor=ap.tensor, offset=offset, ap=pattern)


def v(base, g=None, per=0):
    return base if g is None else g * per + base


def build(nc, a):
    sb_at = [16512]

    def place(spec, at):
        out = {}
        for name, shape, dt in spec:
            n = 4 * int(np.prod(shape[1:]))
            out[name] = nc.alloc_sbuf_tensor_at(name, shape, dt, offset=at)
            at += (n + 31) // 32 * 32
        assert at <= nc.sbuf_usable_end, (spec[0][0], at)
        return out, at

    m = {}

    def region(at, *spec):
        got, end = place(spec, at)
        m.update(got)
        return end

    END = region(sb_at[0],
                 ("w_raw", [P, RING, UW], F32), ("w_hi", [P, RING, UW], F32R), ("w_lo", [P, RING, UW], F32R),
                 ("ones", [P, P], F32), ("ident", [P, P], F32), ("iota", [P, P], F32),
                 ("vecs", [P, NVEC], F32), ("cvec", [P, KD * 2], F32), ("csig", [P, KD * 2], F32),
                 ("csilu", [P, KD * 2], F32), ("c1", [P, KD], F32),
                 ("mod1", [P, 32, 2], F32), ("scale1", [P, KD, 2], F32), ("mod2", [P, 64], F32),
                 ("scale2", [P, KD], F32), ("gate1", [P, KD], F32), ("gate2", [P, KD], F32),
                 ("eps", [P, 1], F32), ("nmax", [P, 4], F32), ("nm0", [P, 4], F32), ("rsum", [P, 4], F32), ("rinv", [P, 4], F32))
    e = region(END, ("h_hi", [P, KD, TC], F32R), ("xin", [P, KD, TC], F32))
    region(END + 4 * KD * TC, ("h_lo", [P, KD, TC], F32R))
    e1 = region(e, ("ada_sum", [P, 8192], F32), ("ada_raw", [P, 2, 2048], F32), ("stage", [P, 2, TC], F32))
    region(e, ("ada1_raw", [P, 4, 2048], F32))
    region(e + 32768, ("sq", [P, 2, TC], F32), ("rs", [P, TC], F32), ("sqr", [P, TC], F32),
           ("xsum", [P, TC], F32))
    region(END, ("mrow", [P, 4096], F32))
    oa_end = region(END, ("oa_hi", [P, 8, T], F32R), ("oa_lo", [P, 8, T], F32R))
    ob_end = region(oa_end, ("ob_hi", [P, 8, T], F32R), ("ob_lo", [P, 8, T], F32R))
    region(END,
           ("cq", [P, 6, T], F32), ("ckv", [P, 4, TC], F32), ("kpe", [P, TC], F32),
           ("cq_hi", [P, 6, T], F32R), ("cq_lo", [P, 6, T], F32R),
           ("ckv_hi", [P, 4, TC], F32R), ("ckv_lo", [P, 4, TC], F32R),
           ("rotm", [P, P], F32), ("cos", [P, T], F32), ("sin", [P, T], F32),
           ("sq3", [P, 2, TC], F32), ("sqr3", [P, TC], F32), ("rs3", [P, TC], F32),
           ("mst", [P, 2, TC], F32), ("rope_t", [P, T], F32), ("bpre", [P, DX * 8], F32))
    region(oa_end,
           ("na_q", [P, T], F32), ("na_k", [P, TC], F32), ("na_v", [P, TC], F32),
           ("qz_hi", [P, 4, T], F32R), ("qz_lo", [P, 4, T], F32R),
           ("k_hi", [P, 2, TC], F32R), ("k_lo", [P, 2, TC], F32R),
           ("v_hi", [P, 2, 9, P], F32R), ("v_lo", [P, 2, 9, P], F32R),
           ("na_p", [P, 2, T], F32), ("pt_hi", [P, 2, T], F32R), ("pt_lo", [P, 2, T], F32R),
           ("bm", [P, 4, 256], F32), ("mask", [P, 4, 256], F32))
    region(ob_end,
           ("ml_q", [P, T], F32), ("ml_k", [P, TC], F32), ("ml_v", [P, 6, P], F32), ("ml_qp", [P, T], F32),
           ("mq_hi", [P, 2, T], F32R), ("mq_lo", [P, 2, T], F32R),
           ("mk_hi", [P, 2, TC], F32R), ("mk_lo", [P, 2, TC], F32R),
           ("mv_hi", [P, 2, 6, P], F32R), ("mv_lo", [P, 2, 6, P], F32R),
           ("mqp_hi", [P, 2, T], F32R), ("mqp_lo", [P, 2, T], F32R),
           ("ml_kp", [P, TC], F32), ("kp_hi", [P, TC], F32R), ("kp_lo", [P, TC], F32R),
           ("ml_p", [P, 2, TC], F32), ("mpt_hi", [P, 6, T], F32R))
    region(ob_end - 0 + 4 * (T * 2 + TC + 768) + 4 * (4 * T + 4 * TC + 4 * 768 + 4 * T + 3 * TC + 2 * TC + 6 * T),
           ("mpt_lo", [P, 6, T], F32R))
    y_end = region(ob_end, ("y_hi", [P, KD, T], F32R), ("y_lo", [P, KD, T], F32R))
    region(y_end, ("sg", [P, 2, 2, T], F32), ("yb", [P, 2, T], F32))
    z_end = region(END, ("z", [P, KD, T], F32), ("x1", [P, KD, T], F32))
    assert z_end <= ob_end
    region(y_end, ("zsq", [P, 2, T], F32), ("ssum", [P, T], F32), ("rs2", [P, T], F32), ("sqr2", [P, T], F32))
    h2_end = region(END, ("h2_hi", [P, KD, T], F32R), ("h2_lo", [P, KD, T], F32R))
    q_end = region(h2_end, ("sel", [P, 3, 4, P], F32),
           ("sk_hi", [P, 16, P], F32R), ("sk_lo", [P, 16, P], F32R), ("sk_raw", [P, 16, P], F32),
           ("q_hi", [P, 2, T], F32R), ("q_lo", [P, 2, T], F32R),
           ("sc", [P, 2, 4, P], F32), 
           ("topv", [P, 2, 4, 16], F32), ("topi", [P, 2, 4, 16], U32), ("topif", [P, 2, 4, 16], F32),
           ("cand", [P, 4, 256], F32), ("cand2", [P, 4, 256], F32),
           ("tv", [P, 4, 16], F32), ("tpos", [P, 4, 16], U32), ("tab", [P, 2, 4, 16], U32),
           ("tabf", [P, 2, 4, 16], F32), ("eqb", [P, 4, 16, 16], F32), ("eqc", [P, 4, 16, 16], F32),
           ("te", [P, 4, 16], F32), ("tex", [P, 4, 16], F32), ("tsum", [P, 4], F32), ("tinv", [P, 4], F32))
    region(h2_end, ("sel_keep", [P, 3, 4, P], F32), ("selT", [P, 3, T], F32), ("selw", [P, 2, 3, 8], F32),
           ("oh1", [P, 2, 8, P], F32), ("oh2", [P, 2, 8, P], F32), ("gst", [P, 2, P, TCH], F32))
    region(h2_end, ("acc", [P, KD, T], F32), ("ew_hi", [P, 8, T], F32R), ("ew_lo", [P, 8, T], F32R),
           ("eact", [P, 2, T], F32), ("eg", [P, 2, T], F32), ("ew", [P, 2, T], F32))
    region(END, ("fx", [P, KD, T], F32), ("fsq", [P, 2, T], F32), ("fsum", [P, T], F32), ("frs", [P, T], F32),
           ("fsqr", [P, T], F32))

    M = type("M", (), m)
    ps = nc.alloc_psum_tensor("ps", [P, 8, 512], F32)
    psf = ps[:, :, :].rearrange("p b n -> p (b n)")

    S = {}

    def sem(name):
        if name not in S:
            S[name] = nc.alloc_semaphore(name)
        return S[name]

    w_ld = [sem(f"w_loaded{i}") for i in range(RING)]
    w_hi_done, w_lo_done, unit_done = sem("w_hi_done"), sem("w_lo_done"), sem("unit_done")
    consts_ld, x_ld, silu_ld = sem("consts_loaded"), sem("x_loaded"), sem("c_loaded")
    ada1_ld = [sem(f"ada1_loaded{i}") for i in range(4)]
    ada1_used, csig_ok, csilu_ok, sq_ok, sq_sum, ss_ok = (sem(n) for n in (
        "ada1_used", "c_sigmoid_ready", "c_silu_ready", "squares_ready", "squares_added", "square_sum_ready"))
    rt_ok, rs_ok, rows_ok, h_raw, h_hi_ok, h_ok, cols_ok = (sem(n) for n in (
        "root_ready", "rs_ready", "mod_rows_ready", "h_ready_f32", "h_hi_ready", "h_ready", "mod_columns_ready"))
    dve0 = sem("dve_step")
    bpre_z, bpre_ld, br_st, bf_st = sem("bias_cleared"), sem("bias_loaded"), sem("bias_rows_stored"), sem("bias_stored")
    p2_ev, ada2_used = sem("proj_evacuated"), sem("ada2_used")
    p2_st = [sem(f"proj_stored{i}") for i in range(2)]
    ada2_ld = [sem(f"ada2_loaded{i}") for i in range(2)]
    ada_zero, mod2_ps, mod2_ok = sem("ada_sum_cleared"), sem("mod2_product_ready"), sem("mod2_ready")

    (pre_ld, pre_sq, pre_n, pre_hi, pre_ok, pre_ev, kp_rot, kp_ok, kp_st,
     rope_raw, rope_rot, rope_step) = (sem("pre_" + n) for n in (
         "loaded", "squares", "normed", "hi", "ready", "evacuated", "key_rotated", "key_ready", "key_stored", "rope_copied", "rope_rotated", "rope_step"))
    pre_used, kn_mm, ml_m0 = sem("pre_squares_used"), sem("pre_product_ready"), sem("ml_max_raw")
    pre_st = [sem(f"pre_stored{i}") for i in range(2)]
    (na_ld, na_s, na_add, na_max, na_exp, na_rinv, na_p, na_t, na_pthi, na_pt, na_pv, na_ohi, na_o,
     na_qkhi, na_split, na_vt, na_vhi, na_vlo, na_zero, bm_ok, mask_ld) = (sem("na_" + n) for n in (
         "loaded", "scores", "biased", "max", "exp", "rinv", "probs", "transposed", "pt_hi", "pt_lo", "pv", "out_hi",
         "out", "qk_hi", "qk_lo", "v_transposed", "v_hi", "v_lo", "zeroed", "bias_masked", "mask_loaded"))
    bm_ld = [sem(f"na_bias_loaded{i}") for i in range(4)]
    (ml_ld, ml_kpld, ml_kphi, ml_kplo, ml_zero, ml_s, ml_max, ml_pt, ml_pv,
     ml_ohi, ml_o, ml_hi, ml_lo) = (sem("ml_" + n) for n in (
         "loaded", "kp_loaded", "kp_hi", "kp_lo", "zeroed", "scores", "max", "pt_lo", "pv", "out_hi", "out", "prep_hi", "prep_lo"))
    (mg_sig, mg_part, mg_y, mg_yhi, mg_ylo, z_sq, z_cp, z_add, zn, x1_ok,      x1_st, h2_raw, h2_hi_ok, h2_ok) = (sem(n) for n in (
         "gates_ready", "branch_gated", "merged", "y_hi_ready", "y_lo_ready", "z_squares", "z_copied", "z_squares_added",
         "z_normed", "x1_ready", "x1_stored", "h2_f32", "h2_hi_ready", "h2_ready"))
    mg_ld = [sem(f"gates_loaded{i}") for i in range(2)]
    (sk_ld, sk_h, sk_ok, q_h, q_l, s_mm, sc_cp, acc_zero, tk, te_ok, tex_ok, sel_t, selT_ok, selw_ok, oh1_ok,
     oh2_ok, g_mm, g_ev) = (sem(n) for n in (
         "subkeys_loaded", "subkeys_hi", "subkeys_ready", "query_hi", "query_lo", "key_scores", "key_scores_copied",
         "sum_cleared", "topk_step", "top_scores_ready", "top_exp_ready", "choice_transposed",
         "choice_columns_ready", "token_columns_ready", "onehot1_ready", "onehot2_ready", "gates_product",
         "gates_copied"))
    g_st = [sem(f"gates_stored{i}") for i in range(2)]
    waited_dve, waited_pool = sem("waited_dve"), sem("waited_pool")
    (m_gelu, m_w, m_hi, m_lo, m_v, m_acc) = (sem("ffn_" + n) for n in (
        "gelu", "weighted", "weighted_hi", "weighted_lo", "product", "added"))
    m_eg = [sem(f"ffn_gates_loaded{i}") for i in range(2)]

    block = nc.Block()
    block.__enter__()

    @block.sync
    def _(sp):
        def load_unit(n, g=None, per=0):
            if g is not None or n >= RING:
                sp.wait_ge(w_lo_done, v(n - RING + 1, g, per))
            src = a["wall"][n] if g is None else a["wall"][bass.ds(g * per + n, 1)].rearrange("a p n -> p (a n)")
            sp.dma_start(M.w_raw[:, n % RING, :], src).then_inc(w_ld[n % RING], 16)

        sp.dma_start(M.cvec[:, :], a["cvec"]).then_inc(silu_ld, 16)
        sp.dma_start(M.vecs[:, :], a["vecs"]).then_inc(consts_ld, 16)
        for i, name in enumerate(("ones", "ident", "iota")):
            sp.dma_start(m[name][:, :], a["consts"][i]).then_inc(consts_ld, 16)
        for s in range(4):
            sp.dma_start(M.ada1_raw[:, s, :], a["ada1"][s]).then_inc(ada1_ld[s], 16)
        sp.dma_start(M.xin[:, :, 0:T], a["xT"]).then_inc(x_ld, 16)
        sp.dma_start(M.xin[:, :, T:TC], a["ctxT"]).then_inc(x_ld, 16)
        with sp.Fori(1, 8) as g:
            for s in range(4):
                sp.wait_ge(ada1_used, v(s - 3, g, 4))
                sp.dma_start(M.ada1_raw[:, s, :], a["ada1"][bass.ds(g * 4 + s, 1)].rearrange("a p n -> p (a n)")
                             ).then_inc(ada1_ld[s], 16)
        for n in range(2 * RING):
            load_unit(n)
        sp.wait_ge(h_ok, KD)

        def p2_block(b, ctx, bg, g=None, ada=None):
            ub, up = (b * 2, None if g is None else 8) if ctx else (N_LAT + b * 2, None if g is None else 8)
            if ada is not None:
                sp.wait_ge(ada2_used, v(ada + 3, g, 4))
                kk, q = (ada // 4, ada % 4)
                src = a["ada2"][kk, q] if g is None else a["ada2"][bass.ds(g + kk, 1), q].rearrange("a p n -> p (a n)")
                sp.dma_start(M.ada_raw[:, ada % 2, :], src).then_inc(ada2_ld[ada % 2], 16)
            for j in range(2):
                load_unit(ub + 8 + j, g, 8)
            sp.wait_ge(p2_ev, v(bg + 3, g, 4))
            dst = a["projB"] if ctx else a["projL"]
            dst = dst[b] if g is None else dst[bass.ds(g * 4 + b, 1)].rearrange("a p n -> p (a n)")
            sp.dma_start(dst, M.stage[:, bg % 2, 0:TC if ctx else T]).then_inc(p2_st[bg % 2], 16)

        with sp.Fori(0, 5) as g:
            for s in range(4):
                p2_block(s, True, s, g, ada=s)
        p2_block(20, True, 20)
        with sp.Fori(0, 11) as g:
            for s in range(4):
                p2_block(s, False, 21 + s, g, ada=20 + s)
        for b in (44, 45):
            p2_block(b, False, 21 + b)
        for s in range(2):
            sp.wait_ge(p2_st[s], 16 * ((67 + 1 - s) // 2 + 1))

        sp.wait_ge(unit_done, N_KN)
        sp.dma_start(M.ckv[:, :, :], a["projB"][B_CKV:B_CKV + 4].rearrange("b p t -> p b t")).then_inc(pre_ld, 16)
        sp.dma_start(M.kpe[:, :], a["projB"][B_KPE]).then_inc(pre_ld, 16)
        sp.dma_start(M.rotm[:, :], a["consts"][3]).then_inc(pre_ld, 16)
        sp.dma_start(M.cos[:, :], a["rope"][0]).then_inc(pre_ld, 16)
        sp.dma_start(M.sin[:, :], a["rope"][1]).then_inc(pre_ld, 16)
        sp.dma_start(M.cq[:, :, :], a["projL"][L_CQ:L_CQ + 6].rearrange("b p t -> p b t")).then_inc(pre_ld, 16)
        sp.wait_ge(bpre_z, 1)
        for r in range(ROWS):
            sp.dma_start(M.bpre[16 * r:16 * r + 16, 128:128 + 31 * 8].rearrange("h (x y) -> h x y", y=8),
                         a["rpb"][:, :, 7 - r:15 - r]).then_inc(bpre_ld, 16)
        sp.wait_ge(bpre_ld, 16 * ROWS)
        sp.dma_start(a["bias_rows"].rearrange("r h n -> (r h) n")[:, 0:DX * 8], M.bpre[:, :]).then_inc(br_st, 16)
        sp.wait_ge(br_st, 16)
        for o in range(3):
            for h in range(16):
                src = dram(a["bias_rows"], h * 512 + (31 - 8 * o) * 8, [[16 * 512, ROWS], [-8, 16], [1, 256]])
                sp.dma_start(a["bias"][o, h].rearrange("(c r) k -> r c k", r=ROWS), src).then_inc(bf_st, 16)

        def pre_store(e, dst, g=None, per=0, w=T):
            sp.wait_ge(pre_ev, v(e + 3, g, per))
            sp.dma_start(dst, M.mst[:, e % 2, 0:w]).then_inc(pre_st[e % 2], 16)

        for b in range(8):
            if b % 2 == 0:
                load_unit(N_KN + b // 2 + 8)
            pre_store(b, a["knT"][b], w=TC)
        for u in range(4):
            for t in range(6):
                pre_store(8 + 6 * u + t, a["vmla"][t, :, 256 * u:256 * (u + 1)], w=256)
            load_unit(N_V + u + 8)
        with sp.Fori(0, 2) as g:
            for s in range(4):
                load_unit(N_QB + 8 + s, g, 4)
                pre_store(32 + s, a["qT"][bass.ds(g * 4 + s, 1)].rearrange("a p n -> p (a n)"), g, 4)
        sp.wait_ge(kp_ok, 1)
        sp.dma_start(a["kp"], M.kpe[:, :]).then_inc(kp_st, 16)
        for s in range(4):
            load_unit(N_QB + 16 + s)
            pre_store(40 + s, a["qT"][8 + s])
        for s in range(2):
            sp.wait_ge(pre_st[s], 16 * 23)
        sp.wait_ge(kp_st, 16)
        sp.wait_ge(bf_st, 16 * 48)

        sp.dma_start(M.mask[:, :, :], a["maskc"]).then_inc(mask_ld, 16)

        def na_prep(b, g=None):
            srcs = [a[name][blk + b] if g is None else a[name][bass.ds(g * 2 + (b + blk), 1)].rearrange("a p n -> p (a n)")
                    for name, blk in (("projL", L_QA), ("projB", B_KA), ("projB", B_VA))]
            for i, (dst, src) in enumerate(zip((M.na_q, M.na_k, M.na_v), srcs)):
                if i == 0 and (g is not None or b):
                    sp.wait_ge(na_split, v(b, g, 2))
                if i == 2 and (g is not None or b):
                    sp.wait_ge(na_vt, v(3 * b, g, 6))
                sp.dma_start(dst[:, :], src).then_inc(na_ld, 16)

        def na_bias(u, g=None):
            h, j = u // 4, u % 4
            src = a["bias"][SHIFT[j], h] if g is None else a["bias"][SHIFT[j], bass.ds(g * 4 + h, 1)].rearrange("a p n -> p (a n)")
            sp.wait_ge(na_max, v(u + 1, g, 16))
            sp.dma_start(M.bm[:, u % 4, :], src).then_inc(bm_ld[u % 4], 16)

        na_prep(0)
        with sp.Fori(0, 3) as g:
            for s in range(2):
                for u in range(8):
                    na_bias(8 * s + u, g)
                    if u == 1:
                        na_prep(s + 1, g)
        for s in range(2):
            for u in range(8):
                na_bias(48 + 8 * s + u)
                if u == 1 and s == 0:
                    na_prep(7)

        sp.wait_ge(na_o, 16 + 2)
        sp.dma_start(M.ml_kp[:, :], a["kp"]).then_inc(ml_kpld, 16)

        def ml_prep(h, g=None):
            z = 64 * (h % 2)
            def at(x, n):
                return x[n] if g is None else x[bass.ds(g * 2 + n, 1)].rearrange("a p n -> p (a n)")
            qp = a["qT"][8 + h // 2, z:z + 64] if g is None else a["qT"][bass.ds(g + (8 + h // 2), 1), z:z + 64].rearrange("a p n -> p (a n)")
            vm = a["vmla"].rearrange("t p (h n) -> h p t n", n=P)
            vm = vm[h] if g is None else vm[bass.ds(g * 2 + h, 1)].rearrange("a p t n -> p (a t) n")
            q, k = at(a["qT"], h), at(a["knT"], h)
            if g is not None or h:
                sp.wait_ge(ml_lo, v(h, g, 2))
            sp.dma_start(M.ml_q[:, :], q).then_inc(ml_ld, 16)
            sp.dma_start(M.ml_k[:, :], k).then_inc(ml_ld, 16)
            sp.dma_start(M.ml_v[:, :, :], vm).then_inc(ml_ld, 16)
            sp.dma_start(M.ml_qp[z:z + 64, :], qp).then_inc(ml_ld, 16)

        ml_prep(0)
        with sp.Fori(0, 3) as g:
            for s in range(2):
                ml_prep(s + 1, g)
        ml_prep(7)

        sp.wait_ge(ml_o, 8 + 2)

        def mg_block(n, g=None):
            srcs = [a["projL"][bass.ds(g * 2 + (n + blk), 1)].rearrange("a p n -> p (a n)") for blk in (L_GA, L_GB)]
            sp.wait_ge(mg_y, v(n + 1, g, 2))
            for i in range(2):
                sp.dma_start(M.sg[:, n % 2, i, :], srcs[i]).then_inc(mg_ld[n % 2], 16)
            for j in range(2):
                load_unit(N_MERGE + 2 * n + 8 + j, g, 4)

        with sp.Fori(0, 8) as g:
            for n in range(2):
                mg_block(n, g)
        sp.wait_ge(unit_done, N_OUT)
        sp.dma_start(M.x1[:, :, :], a["xT"]).then_inc(x_ld, 16)
        with sp.Fori(0, 8) as g:
            for j in range(4):
                load_unit(N_OUT + 8 + j, g, 4)
        for q in range(4):
            sp.wait_ge(x1_ok, 4 * q + 4)
            sp.dma_start(a["x1s"][:, 4 * q:4 * q + 4, :], M.x1[:, 4 * q:4 * q + 4, :]).then_inc(x1_st, 16)

        sp.wait_ge(unit_done, N_QUERY)
        sp.dma_start(M.sk_raw[:, :, :], a["subk"]).then_inc(sk_ld, 16)
        with sp.Fori(0, 8) as g:
            for j in range(4):
                load_unit(N_QUERY + 8 + j, g, 4)
        def store_gates(s, g):
            sp.wait_ge(g_ev, v(16 * (s + 1) + 4, g, 32))
            sp.dma_start(a["gates"][bass.ds(g * 2 + s, 1)].rearrange("a p n -> p (a n)"),
                         M.gst[:, s, :, :].rearrange("p e t -> p (e t)")).then_inc(g_st[s], 16)

        with sp.Fori(0, T // TCH // 2) as g:
            for s in range(2):
                store_gates(s, g)
        for s in range(2):
            sp.wait_ge(g_st[s], 16 * (T // TCH // 2 + 1))

        gates_by_block = a["gates"].rearrange("c p (e t) -> e p c t", t=TCH)

        def exp_block(b, n, g=None):
            src = gates_by_block[b] if g is None else gates_by_block[bass.ds(g * 8 + b, 1)].rearrange("a p c t -> p (a c) t")
            sp.wait_ge(m_w, v(b + 1, g, 8))
            sp.dma_start(M.eg[:, b % 2, :].rearrange("p (c t) -> p c t", t=TCH), src).then_inc(m_eg[b % 2], 16)
            for j in range(2):
                load_unit(n + j + 8, g, 32)

        def out_units(n, g=None, count=8):
            for j in range(count):
                load_unit(n + j + 8, g, 32)

        for b in range(4):
            exp_block(b, N_MAIN + 2 * b)
        with sp.Fori(0, GROUPS // 2 - 1) as g:
            for r in range(2):
                for q in range(4):
                    exp_block(4 + 4 * r + q, N_MAIN + 8 + 16 * r + 2 * q, g)
                out_units(N_MAIN + 16 + 16 * r, g)
        for q in range(4):
            exp_block(4 * GROUPS - 4 + q, N_END - 24 + 2 * q)
        out_units(N_END - 16)
        sp.wait_ge(m_lo, 4 * GROUPS)
        sp.dma_start(M.fx[:, :, :], a["x1s"]).then_inc(x_ld, 16)
        for q in range(4):
            sp.wait_ge(x1_ok, KD + 4 * q + 4)
            sp.dma_start(a["out"][:, 4 * q:4 * q + 4, :], M.fx[:, 4 * q:4 * q + 4, :]).then_inc(x1_st, 16)
        sp.wait_ge(x1_st, 64 + 64)
        sp.wait_ge(x1_st, 64)

    @block.scalar
    def _(act):
        def w_hi(n, g=None, per=0):
            act.wait_ge(w_ld[n % RING], v(16 * (n // RING + 1), g, 16 * (per // RING)))
            if g is not None or n >= RING:
                act.wait_ge(unit_done, v(n - RING + 1, g, per))
            act.activation(M.w_hi[:, n % RING, :], M.w_raw[:, n % RING, :], ACT.Copy).then_inc(w_hi_done, 1)

        act.wait_ge(silu_ld, 16)
        act.activation(M.csig[:, :], M.cvec[:, :], ACT.Sigmoid).then_inc(csig_ok, 1)
        act.wait_ge(x_ld, 32)
        for k in range(KD):
            if k >= 2:
                act.wait_ge(sq_sum, k)
            act.activation(M.sq[:, k % 2, :], M.xin[:, k, :], ACT.Square).then_inc(sq_ok, 1)
        for half in range(2):
            act.wait_ge(ada1_used, 16 * (half + 1))
            act.activation(M.mrow[0:2, 2048 * half:2048 * (half + 1)], psf[0:2, 2048 * half:2048 * (half + 1)],
                           ACT.Copy).then_inc(rows_ok, 1)
        act.wait_ge(ss_ok, 1)
        act.wait_ge(dve0, 1)
        act.activation(M.sqr[:, 0:T], ps[:, 1, :], ACT.Sqrt, bias=M.eps[:, 0:1], scale=1.0 / D)
        act.activation(M.sqr[:, T:TC], ps[:, 2, 0:C], ACT.Sqrt, bias=M.eps[:, 0:1], scale=1.0 / D).then_inc(rt_ok, 1)
        for n in range(RING):
            w_hi(n)
        act.wait_ge(dve0, 6)
        for k in range(KD):
            if k == 0:
                act.wait_ge(rs_ok, 1 + KD)
            act.activation(M.h_hi[:, k, 0:T], M.xin[:, k, 0:T], ACT.Identity,
                           bias=M.mod1[:, k, 0:1], scale=M.scale1[:, k, 0:1])
            act.activation(M.h_hi[:, k, T:TC], M.xin[:, k, T:TC], ACT.Identity,
                           bias=M.mod1[:, k, 1:2], scale=M.scale1[:, k, 1:2]).then_inc(h_hi_ok, 1)
        with act.Fori(0, 5) as g:
            for s in range(8):
                w_hi(N_BOTH + RING + s, g, 8)
        for j in range(2):
            w_hi(N_BOTH + 40 + RING + j)
        with act.Fori(0, 11) as g:
            for s in range(8):
                w_hi(N_LAT + RING + s, g, 8)
        for j in range(4):
            w_hi(N_LAT + 88 + RING + j)

        act.wait_ge(pre_ld, 96)
        for i in range(10):
            src, w = (M.ckv[:, i, :], TC) if i < 4 else (M.cq[:, i - 4, :], T)
            if i >= 2:
                act.wait_ge(pre_used, i - 1)
            act.activation(M.sq3[:, i % 2, 0:w], src, ACT.Square).then_inc(pre_sq, 1)
            if i == 5:
                act.wait_ge(pre_used, 4)
                act.activation(M.sqr3[:, 0:T], ps[:, 0, :], ACT.Sqrt, bias=M.eps[:, 0:1], scale=1.0 / 512)
                act.activation(M.sqr3[:, T:TC], ps[:, 1, 0:C], ACT.Sqrt, bias=M.eps[:, 0:1], scale=1.0 / 512
                               ).then_inc(rt_ok, 1)
        act.wait_ge(pre_used, 10)
        act.wait_ge(rs_ok, 17 + 1)
        act.activation(M.sqr3[:, 0:T], ps[:, 2, :], ACT.Sqrt, bias=M.eps[:, 0:1], scale=1.0 / 768).then_inc(rt_ok, 1)
        for i in range(10):
            act.wait_ge(pre_n, i + 1)
            if i < 4:
                act.activation(M.ckv_hi[:, i, :], M.ckv[:, i, :], ACT.Copy).then_inc(pre_hi, 1)
            else:
                act.activation(M.cq_hi[:, i - 4, :], M.cq[:, i - 4, :], ACT.Copy).then_inc(pre_hi, 1)
        for n in range(8):
            w_hi(N_KN + RING + n)
        with act.Fori(0, 3) as g:
            for s in range(4):
                w_hi(N_QB + RING + s, g, 4)

        def na_prep(b, slot, g=None):
            act.wait_ge(na_ld, v(48 * (b + 1), g, 96))
            if g is not None or b:
                act.wait_ge(na_pv, v(8 * b, g, 16))
            else:
                act.wait_ge(na_zero, 1)
            for p in range(2):
                z = slice(64 * p, 64 * p + 64)
                act.activation(M.qz_hi[z, 2 * slot + p, :], M.na_q[z, :], ACT.Copy, scale=NA_SCALE)
            act.activation(M.k_hi[:, slot, :], M.na_k[:, :], ACT.Copy).then_inc(na_qkhi, 1)

        def na_vals(b, slot, part, g=None):
            n = 4 if part < 2 else 1
            act.wait_ge(na_vt, v(3 * b + part + 1, g, 6))
            if g is not None or b:
                act.wait_ge(na_pv, v(8 * b, g, 16))
            act.activation(M.v_hi[:, slot, 4 * part:4 * part + n, :],
                           ps[:, 6 + part % 2, 0:n * P].rearrange("p (c n) -> p c n", n=P), ACT.Copy).then_inc(na_vhi, 1)

        def na_exp_(u, g=None):
            act.wait_ge(na_max, v(u + 1 + 4, g, 16))
            act.activation(M.na_p[:, u % 2, :], ps[:, u % 2, :], ACT.Exp, bias=M.nmax[:, u % 4:u % 4 + 1],
                           accum_out=M.rsum[:, u % 4:u % 4 + 1]).then_inc(na_exp, 1)

        def na_out(h, g=None):
            z = slice(64 * (h % 2), 64 * (h % 2) + 64)
            act.wait_ge(na_pv, v(4 * h + 4 + 8, g, 16))
            dst = M.oa_hi[z, h // 2, :] if g is None else M.oa_hi[z, bass.ds(g * 2 + h // 2, 1), :].rearrange("p a n -> p (a n)")
            act.activation(dst, ps[z, 4 + h % 2, :], ACT.Copy).then_inc(na_ohi, 1)

        def na_pair(s, g=None, last=False, base=0):
            for u in range(8):
                uu = base + 8 * s + u
                b = uu // 8
                if not last:
                    if u == 1:
                        na_prep(b + 1, (s + 1) % 2, g)
                    if u in (3, 5, 7):
                        na_vals(b + 1, (s + 1) % 2, (u - 3) // 2, g)
                act.wait_ge(na_t, v(uu + 1, g, 16))
                act.wait_ge(na_pv, v(uu + 7, g, 16))
                act.activation(M.pt_hi[:, u % 2, :], ps[:, 2 + u % 2, :], ACT.Copy).then_inc(na_pthi, 1)
                if not (last and u >= 6):
                    na_exp_(uu + 2, g)
                if u == 5:
                    na_out(2 * b, g)
            na_out(2 * b + 1, g)

        na_prep(0, 0)
        for part in range(3):
            na_vals(0, 0, part)
        na_exp_(0)
        na_exp_(1)
        with act.Fori(0, 3) as g:
            for s in range(2):
                na_pair(s, g)
        na_pair(0, base=48)
        na_pair(1, base=48, last=True)

        def ml_prep(h, part, g=None):
            s, z = h % 2, slice(64 * (h % 2), 64 * (h % 2) + 64)
            if part == 0:
                act.wait_ge(ml_ld, v(64 * (h + 1), g, 128))
                if g is not None or h:
                    act.wait_ge(ml_pv, v(h, g, 2))
                act.activation(M.mq_hi[:, s, :], M.ml_q[:, :], ACT.Copy)
                act.activation(M.mqp_hi[z, s, :], M.ml_qp[z, :], ACT.Copy).then_inc(ml_hi, 1)
            elif part == 1:
                act.activation(M.mk_hi[:, s, :], M.ml_k[:, :], ACT.Copy).then_inc(ml_hi, 1)
            else:
                act.activation(M.mv_hi[:, s, :, :], M.ml_v[:, :, :], ACT.Copy).then_inc(ml_hi, 1)

        def ml_exp_(u, g=None):
            act.wait_ge(ml_max, v(u + 1, g, 8))
            b = 1024 * (u % 2)
            act.activation(M.ml_p[:, u % 2, :], psf[:, b:b + TC], ACT.Exp, bias=M.nmax[:, u % 4:u % 4 + 1],
                           scale=MLA_SCALE, accum_out=M.rsum[:, u % 4:u % 4 + 1]).then_inc(na_exp, 1)

        def ml_head(s, g=None, base=0, last=False):
            h = base + s
            for q in range(4):
                u = 4 * h + q
                if q < 3 and not last:
                    ml_prep(h + 1, q, g)
                act.wait_ge(na_t, v(NA_UNITS + u + 1, g, 8))
                if q == 0:
                    act.wait_ge(ml_pv, v(h + 1, g, 2))
                act.activation(M.mpt_hi[:, :, P * q:P * (q + 1)],
                               psf[:, 2048:2048 + TC].rearrange("p (c n) -> p c n", n=P), ACT.Copy).then_inc(na_pthi, 1)
                if not (last and q >= 2):
                    ml_exp_(u + 2, g)
            act.wait_ge(ml_pv, v(h + 2, g, 2))
            dst = M.ob_hi[:, h, :] if g is None else M.ob_hi[:, bass.ds(g * 2 + s, 1), :].rearrange("p a n -> p (a n)")
            act.activation(dst, ps[:, 6 + s, :], ACT.Copy).then_inc(ml_ohi, 1)

        act.wait_ge(ml_kpld, 16)
        act.activation(M.kp_hi[:, :], M.ml_kp[:, :], ACT.Copy).then_inc(ml_kphi, 1)
        act.wait_ge(ml_zero, 1)
        for part in range(3):
            ml_prep(0, part)
        ml_exp_(0)
        ml_exp_(1)
        with act.Fori(0, 3) as g:
            for s in range(2):
                ml_head(s, g)
        ml_head(0, base=6)
        ml_head(1, base=6, last=True)

        with act.Fori(0, 8) as g:
            for n in range(2):
                act.wait_ge(mg_ld[n], v(32, g, 32))
                act.activation(M.sg[:, n, :, :], M.sg[:, n, :, :], ACT.Sigmoid).then_inc(mg_sig, 1)
                w_hi(N_MERGE + 2 * n + RING, g, 4)
                w_hi(N_MERGE + 2 * n + 1 + RING, g, 4)
                act.wait_ge(mg_y, v(n + 1 + 2, g, 2))
                act.activation(M.y_hi[:, bass.ds(g * 2 + n, 1), :].rearrange("p a n -> p (a n)"), M.yb[:, n, :],
                               ACT.Copy).then_inc(mg_yhi, 1)
        with act.Fori(0, 8) as g:
            for n in range(2):
                w_hi(N_OUT + 2 * n + RING, g, 4)
                w_hi(N_OUT + 2 * n + 1 + RING, g, 4)
                act.wait_ge(unit_done, v(N_OUT + 2 * n + 2, g, 4))
                act.wait_ge(z_add, v(n + 1, g, 2))
                act.activation(M.zsq[:, n, :], ps[:, 4 + n, :], ACT.Square).then_inc(z_sq, 1)
        act.wait_ge(ss_ok, 1 + 1)
        act.activation(M.sqr2[:, :], ps[:, 6, :], ACT.Sqrt, bias=M.eps[:, 0:1], scale=1.0 / D).then_inc(rt_ok, 1)
        for k in range(KD):
            act.wait_ge(x1_ok, k + 1)
            if k >= 2:
                act.wait_ge(z_add, KD + 2 + k - 1)
            act.activation(M.zsq[:, k % 2, :], M.x1[:, k, :], ACT.Square).then_inc(z_sq, 1)
        act.wait_ge(ss_ok, 2 + 1)
        act.activation(M.sqr2[:, :], ps[:, 7, :], ACT.Sqrt, bias=M.eps[:, 0:1], scale=1.0 / D).then_inc(rt_ok, 1)

        for k in range(KD):
            act.wait_ge(h2_raw, k + 1)
            act.activation(M.h2_hi[:, k, :], M.x1[:, k, :], ACT.Copy).then_inc(h2_hi_ok, 1)
        act.wait_ge(sk_ld, 16)
        act.activation(M.sk_hi[:, :, :], M.sk_raw[:, :, :], ACT.Copy).then_inc(sk_h, 1)
        def choice_exp(h, g=None):
            act.wait_ge(te_ok, v(h + 1, g, 1))
            act.activation(M.tex[:, :, :], M.te[:, :, :], ACT.Exp).then_inc(tex_ok, 1)

        def choice_head(g=None, first=False):
            for p in range(2):
                w_hi(N_QUERY + 2 * p + RING, g, 4)
                w_hi(N_QUERY + 2 * p + 1 + RING, g, 4)
                act.wait_ge(unit_done, v(N_QUERY + 2 * p + 2, g, 4))
                act.wait_ge(s_mm, v(p + 1, g, 2))
                act.activation(M.q_hi[:, p, :], ps[:, p, :], ACT.Copy).then_inc(q_h, 1)
            for p in range(2):
                act.wait_ge(s_mm, v(p + 1 + 2, g, 2))
                if not first:
                    act.wait_ge(tk, v(20 * (p + 1) - CHOICE_STEPS, g, CHOICE_STEPS))
                act.activation(M.sc[:, p, :, :], ps[:, 2 + p, :].rearrange("p (t n) -> p t n", n=P), ACT.Copy
                               ).then_inc(sc_cp, 1)
            if not first:
                choice_exp(-1, g)

        choice_head(first=True)
        with act.Fori(1, 8) as g:
            choice_head(g)
        choice_exp(7)
        for x in range(3):
            act.wait_ge(sel_t, x + 1)
            act.activation(M.selT[:, x, :], ps[:, x, :], ACT.Copy).then_inc(selT_ok, 1)
        with act.Fori(0, T // TCH // 2) as g:
            for s in range(2):
                act.wait_ge(g_st[s], v(16, g, 16))
                with act.Fori(0, 4) as j:
                    for i in range(4):
                        act.wait_ge(g_mm, g * 16 + j * 2 + (8 * s + i // 2 + 3))
                        dst = M.gst[:, s, :, :].rearrange("p e t -> p t e")
                        act.activation(dst[:, bass.ds(j * 16 + 4 * i, 4), :],
                                       ps[:, i, :].rearrange("p (t e) -> p t e", e=P), ACT.Copy).then_inc(g_ev, 1)

        def exp_block(b, n, g=None, ahead=True):
            if ahead:
                for j in range(2):
                    w_hi(n + j + RING, g, 32)
            act.wait_ge(unit_done, v(n + 2, g, 32))
            act.wait_ge(m_w, v(b + 1, g, 8))
            act.activation(M.eact[:, b % 2, :], ps[:, b % 2, :], ACT.Gelu).then_inc(m_gelu, 1)
            act.wait_ge(m_w, v(b + 1 + 2, g, 8))
            act.activation(M.ew_hi[:, b % 8, :], M.ew[:, b % 2, :], ACT.Copy).then_inc(m_hi, 1)

        def out_units(n, g=None, count=8):
            for j in range(count):
                w_hi(n + j + RING, g, 32)

        for s in range(2):
            act.wait_ge(g_st[s], 16 * (T // TCH // 2 + 1))
        for b in range(4):
            exp_block(b, N_MAIN + 2 * b)
        with act.Fori(0, GROUPS // 2 - 1) as g:
            for r in range(2):
                for q in range(4):
                    exp_block(4 + 4 * r + q, N_MAIN + 8 + 16 * r + 2 * q, g)
                out_units(N_MAIN + 16 + 16 * r, g)
        for q in range(4):
            exp_block(4 * GROUPS - 4 + q, N_END - 24 + 2 * q)
        out_units(N_END - 16)
        out_units(N_END - 8, count=4)
        for k in range(KD):
            act.wait_ge(m_acc, 16 * GROUPS + k + 1)
            if k >= 2:
                act.wait_ge(z_add, 2 * KD + 3 + k)
            act.activation(M.fsq[:, k % 2, :], M.acc[:, k, :], ACT.Square).then_inc(z_sq, 1)
        act.wait_ge(ss_ok, 3 + 1)
        act.activation(M.fsqr[:, :], ps[:, 6, :], ACT.Sqrt, bias=M.eps[:, 0:1], scale=1.0 / D).then_inc(rt_ok, 1)

    @block.gpsimd
    def _(pool):
        def w_lo(n, g=None, per=0):
            pool.wait_ge(w_hi_done, v(n + 1, g, per))
            pool.tensor_tensor(M.w_lo[:, n % RING, :], M.w_raw[:, n % RING, :],
                               M.w_hi[:, n % RING, :].bitcast(F32), ALU.subtract).then_inc(w_lo_done, 1)

        for n in range(RING):
            w_lo(n)
        pool.wait_ge(ada1_used, 32)
        pool.memset(M.ada_sum[:, :], 0.0).then_inc(ada_zero, 1)
        with pool.Fori(0, (N_KN - 2) // 4) as g:
            for s in range(4):
                w_lo(RING + s, g, 4)
        for n in range(RING + N_KN - 2, RING + N_KN):
            w_lo(n)

        pool.wait_ge(unit_done, N_KN)
        pool.wait_ge(mod2_ps, 1)
        pool.memset(M.bpre[:, :], 0.0).then_inc(bpre_z, 1)
        for n in range(N_KN + RING, N_QB + RING):
            w_lo(n)
        with pool.Fori(0, 3) as g:
            for s in range(4):
                w_lo(N_QB + RING + s, g, 4)

        for s in range(2):
            pool.wait_ge(pre_st[s], 16 * 23)
        pool.wait_ge(unit_done, N_MERGE)
        pool.memset(M.qz_hi[:, :, :].bitcast(F32), 0.0)
        pool.memset(M.qz_lo[:, :, :].bitcast(F32), 0.0).then_inc(na_zero, 1)
        pool.wait_ge(mask_ld, 16)

        def na_mask(u, g=None):
            pool.wait_ge(bm_ld[u % 4], v(16 * (u // 4 + 1), g, 64))
            pool.tensor_tensor(M.bm[:, u % 4, :], M.bm[:, u % 4, :], M.mask[:, u % 4, :], ALU.add).then_inc(bm_ok, 1)

        def na_norm(u, g=None):
            pool.wait_ge(na_rinv, v(u + 1, g, 16))
            pool.tensor_tensor(M.na_p[:, u % 2, :], M.na_p[:, u % 2, :],
                               M.rinv[:, u % 4:u % 4 + 1].to_broadcast([P, T]), ALU.mult).then_inc(na_p, 1)

        for u in range(3):
            na_mask(u)
        na_norm(0)
        with pool.Fori(0, 3) as g:
            for u in range(16):
                na_norm(u + 1, g)
                na_mask(u + 3, g)
        for u in range(48, 64):
            if u + 1 < 64:
                na_norm(u + 1)
            if u + 3 < 64:
                na_mask(u + 3)

        pool.wait_ge(na_o, 16 + 2)
        pool.memset(M.mqp_hi[:, :, :].bitcast(F32), 0.0)
        pool.memset(M.mqp_lo[:, :, :].bitcast(F32), 0.0).then_inc(ml_zero, 1)

        def ml_norm(u, g=None):
            pool.wait_ge(na_rinv, v(NA_UNITS + u + 1, g, 8))
            pool.tensor_tensor(M.ml_p[:, u % 2, :], M.ml_p[:, u % 2, :],
                               M.rinv[:, u % 4:u % 4 + 1].to_broadcast([P, TC]), ALU.mult).then_inc(na_p, 1)

        ml_norm(0)
        with pool.Fori(0, 3) as g:
            for u in range(8):
                ml_norm(u + 1, g)
        for u in range(25, 32):
            ml_norm(u)

        with pool.Fori(0, 16) as g:
            for s in range(4):
                w_lo(N_MERGE + RING + s, g, 4)
        pool.wait_ge(rs_ok, 19 + 1)
        for k in range(KD):
            pool.tensor_tensor(M.z[:, k, :], M.z[:, k, :], M.rs2[:, :], ALU.mult).then_inc(zn, 1)

        pool.wait_ge(rs_ok, 20 + 1)
        for k in range(KD):
            pool.tensor_tensor(M.z[:, k, :], M.x1[:, k, :], M.rs2[:, :], ALU.mult).then_inc(zn, 1)
        with pool.Fori(0, 8) as g:
            for s in range(4):
                w_lo(N_QUERY + RING + s, g, 4)
        pool.wait_ge(selT_ok, 3)
        with pool.Fori(0, T // 16) as g:
            for s in range(2):
                pool.wait_ge(oh1_ok, v(s + 1, g, 2))
                pool.tensor_copy(M.selw[:, s, :, :], M.selT[:, :, bass.ds(g * 16 + 8 * s, 8)]).then_inc(selw_ok, 1)
                pool.wait_ge(selw_ok, v(s + 1, g, 2))
                pool.wait_ge(g_mm, v(s + 1, g, 2))
                pool.sem_inc(waited_pool, 1)
                for i in range(8):
                    last = pool.tensor_scalar(M.oh2[:, s, i, :], M.iota[:, :], M.selw[:, s, 1, i:i + 1], None, ALU.is_equal)
                last.then_inc(oh2_ok, 1)

        for s in range(2):
            pool.wait_ge(g_st[s], 16 * (T // TCH // 2 + 1))
        pool.wait_ge(g_mm, T // 8 + 2)
        pool.wait_ge(oh1_ok, T // 8 + 2)
        pool.memset(M.acc[:, :, :], 0.0).then_inc(acc_zero, 1)
        with pool.Fori(0, (N_END - N_MAIN - RING - 4) // 8) as g:
            for s in range(8):
                w_lo(N_MAIN + RING + s, g, 8)
        for n in range(N_END - 4, N_END):
            w_lo(n)
        pool.wait_ge(rs_ok, 21 + 1)
        for k in range(KD):
            pool.tensor_tensor(M.acc[:, k, :], M.acc[:, k, :], M.frs[:, :], ALU.mult).then_inc(zn, 1)

    @block.vector
    def _(dve):
        dve.sem_inc(ada2_used, 4)
        dve.sem_inc(p2_ev, 2)
        for s in range(2):
            dve.sem_inc(p2_st[s], 16)
        for s_, n in ((pre_st[0], 16), (pre_st[1], 16), (pre_ev, 2), (na_s, 8), (na_max, 4), (na_pt, 2), (na_pv, 8),
                      (na_o, 2), (ml_pt, 1), (ml_o, 2), (ml_pv, 1), (mg_y, 2), (z_add, 2),
                      (q_l, 2), (sc_cp, 2), (s_mm, 2), (g_ev, 4), (g_mm, 2), (oh1_ok, 2), (g_st[0], 16),
                      (g_st[1], 16), (m_gelu, 2), (m_w, 2), (m_acc, 16)):
            dve.sem_inc(s_, n)
        dve.memset(M.eps[:, :], EPS).then_inc(dve0, 1)
        dve.wait_ge(csig_ok, 1)
        dve.tensor_tensor(M.csilu[:, :], M.cvec[:, :], M.csig[:, :], ALU.mult).then_inc(csilu_ok, 1)
        dve.wait_ge(csilu_ok, 1)
        dve.tensor_copy(M.c1[:, :], M.csilu[:, :].rearrange("p (k c) -> p k c", c=2)[:, :, 0]).then_inc(dve0, 1)
        dve.memset(M.xsum[:, :], 0.0).then_inc(sq_sum, 1)
        for k in range(KD):
            dve.wait_ge(sq_ok, k + 1)
            dve.wait_ge(sq_sum, k + 1)
            dve.tensor_tensor(M.xsum[:, :], M.xsum[:, :], M.sq[:, k % 2, :], ALU.add).then_inc(sq_sum, 1)
        dve.wait_ge(rt_ok, 1)
        dve.reciprocal(M.rs[:, :], M.sqr[:, :]).then_inc(rs_ok, 1)
        dve.wait_ge(rs_ok, 1)
        for k in range(KD):
            dve.tensor_tensor(M.xin[:, k, :], M.xin[:, k, :], M.rs[:, :], ALU.mult).then_inc(rs_ok, 1)
        dve.wait_ge(cols_ok, 2)
        dve.wait_ge(consts_ld, 64)
        for c in range(2):
            dve.tensor_tensor(M.mod1[:, :, c], ps[:, 0, 0:64].rearrange("p (n c) -> p n c", c=2)[:, :, c],
                              M.vecs[:, VEC_B:VEC_B + 32], ALU.add).then_inc(dve0, 1)
        dve.wait_ge(dve0, 4)
        for c in range(2):
            dve.scalar_tensor_tensor(M.scale1[:, :, c], M.mod1[:, KD:2 * KD, c], 1.0,
                                     M.vecs[:, VEC_PRE:VEC_PRE + KD], ALU.add, ALU.mult).then_inc(dve0, 1)
        dve.wait_ge(dve0, 6)
        dve.wait_ge(rs_ok, 1 + KD)
        for k in range(KD):
            dve.wait_ge(h_hi_ok, k + 1)
            for c, (t0, t1) in enumerate(((0, T), (T, TC))):
                dve.tensor_scalar(M.xin[:, k, t0:t1], M.xin[:, k, t0:t1], M.scale1[:, k, c:c + 1],
                                  M.mod1[:, k, c:c + 1], ALU.mult, ALU.add).then_inc(h_raw, 1)
            dve.wait_ge(h_raw, 2 * k + 2)
            dve.tensor_tensor(M.h_lo[:, k, :], M.xin[:, k, :], M.h_hi[:, k, :].bitcast(F32),
                              ALU.subtract).then_inc(h_ok, 1)

        def p2_block(bg, ctx, g=None, ada=None):
            dve.wait_ge(unit_done, v(2 * bg + 2, g, 8))
            dve.wait_ge(p2_st[bg % 2], v(16 * (bg // 2 + 1), g, 32))
            if ctx:
                dve.tensor_copy(M.stage[:, bg % 2, T:TC], ps[:, 2 + bg % 2, 0:C])
            dve.tensor_copy(M.stage[:, bg % 2, 0:T], ps[:, bg % 2, :]).then_inc(p2_ev, 1)
            if ada is not None:
                kk, q = ada // 4, ada % 4
                part = M.ada_sum[:, q * 2048:(q + 1) * 2048]
                dve.wait_ge(ada2_ld[ada % 2], v(16 * (ada // 2 + 1), g, 32))
                dve.wait_ge(ada2_used, v(ada + 1, g, 4))
                sc = M.c1[:, bass.ds(g + kk, 1)]
                dve.scalar_tensor_tensor(part, M.ada_raw[:, ada % 2, :], sc, part, ALU.mult, ALU.add
                                         ).then_inc(ada2_used, 1)

        dve.wait_ge(ada_zero, 1)
        with dve.Fori(0, 5) as g:
            for s in range(4):
                p2_block(s, True, g, ada=s)
        p2_block(20, True)
        with dve.Fori(0, 11) as g:
            for s in range(4):
                p2_block(21 + s, False, g, ada=20 + s)
        for b in (44, 45):
            p2_block(21 + b, False)

        dve.wait_ge(mod2_ps, 1)
        dve.tensor_tensor(M.mod2[:, :], ps[:, 7, 0:64], M.vecs[:, VEC_B + 32:VEC_B + 96], ALU.add).then_inc(mod2_ok, 1)
        dve.wait_ge(mod2_ok, 1)
        dve.tensor_tensor(M.gate1[:, :], M.mod2[:, 0:KD], M.vecs[:, VEC_POST:VEC_POST + KD], ALU.mult)
        dve.scalar_tensor_tensor(M.scale2[:, :], M.mod2[:, 2 * KD:3 * KD], 1.0, M.vecs[:, VEC_PREF:VEC_PREF + KD],
                                 ALU.add, ALU.mult)
        dve.tensor_tensor(M.gate2[:, :], M.mod2[:, 3 * KD:4 * KD], M.vecs[:, VEC_POSTF:VEC_POSTF + KD],
                          ALU.mult).then_inc(mod2_ok, 1)

        dve.wait_ge(rt_ok, 1 + 1)
        dve.reciprocal(M.rs3[:, :], M.sqr3[:, :]).then_inc(rs_ok, 1)
        dve.wait_ge(rs_ok, 17 + 1)
        for i in range(10):
            x, w, gg = (M.ckv[:, i, :], TC, VEC_GKV + i) if i < 4 else (M.cq[:, i - 4, :], T, VEC_GQ + i - 4)
            if i == 4:
                dve.wait_ge(rt_ok, 1 + 2)
                dve.wait_ge(pre_n, 4)
                dve.reciprocal(M.rs3[:, 0:T], M.sqr3[:, 0:T]).then_inc(rs_ok, 1)
                dve.wait_ge(rs_ok, 17 + 2)
            dve.scalar_tensor_tensor(x, x, M.vecs[:, gg:gg + 1], M.rs3[:, 0:w], ALU.mult, ALU.mult).then_inc(pre_n, 1)
        for i in range(10):
            x, hi, lo = ((M.ckv, M.ckv_hi, M.ckv_lo) if i < 4 else (M.cq, M.cq_hi, M.cq_lo))
            k = i if i < 4 else i - 4
            dve.wait_ge(pre_hi, i + 1)
            dve.tensor_tensor(lo[:, k, :], x[:, k, :], hi[:, k, :].bitcast(F32), ALU.subtract).then_inc(pre_ok, 1)

        def rope(x, rot, tmp, step, at, done):
            dve.tensor_tensor(tmp, rot, M.sin[:, :], ALU.mult).then_inc(step, 1)
            dve.tensor_tensor(x, x, M.cos[:, :], ALU.mult).then_inc(step, 1)
            dve.wait_ge(step, at + 2)
            dve.tensor_tensor(x, x, tmp, ALU.add).then_inc(done, 1)

        dve.wait_ge(kp_rot, 1)
        dve.wait_ge(pre_ld, 96)
        rope(M.kpe[:, 0:T], ps[:, 3, :], M.rope_t[:, :], rope_step, 0, kp_ok)

        def pre_evac(e, done, w=T, ctx=False, g=None, per=0, inc=pre_ev):
            dve.wait_ge(done[0], done[1])
            dve.wait_ge(pre_st[e % 2], v(16 * (e // 2 + 1), g, 16 * (per // 2)))
            if ctx:
                dve.tensor_copy(M.mst[:, e % 2, T:TC], ps[:, 6 + e % 2, 0:C])
            dve.tensor_copy(M.mst[:, e % 2, 0:w], ps[:, 4 + e % 2, 0:w]).then_inc(inc, 1)

        for b in range(8):
            pre_evac(b, (unit_done, N_KN + b // 2 + 1) if b % 2 else (kn_mm, b // 2 + 1), ctx=True)
        for t in range(24):
            pre_evac(8 + t, (unit_done, N_V + t // 6 + 1) if t % 6 == 5 else (kn_mm, 4 + t // 6 * 5 + t % 6 + 1), w=256)
        with dve.Fori(0, 2) as g:
            for s in range(4):
                pre_evac(32 + s, (unit_done, v(N_QB + s + 1, g, 4)), g=g, per=4)
        for s in range(4):
            e = 40 + s
            pre_evac(e, (unit_done, N_QB + 8 + s + 1), inc=rope_raw)
            dve.wait_ge(rope_rot, s + 1)
            rope(M.mst[:, e % 2, 0:T], ps[:, 2 + s % 2, :], M.rope_t[:, :], rope_step, 2 + 2 * s, pre_ev)

        def na_prep(b, slot, g=None):
            dve.wait_ge(na_qkhi, v(b + 1, g, 2))
            for p in range(2):
                z = slice(64 * p, 64 * p + 64)
                dve.scalar_tensor_tensor(M.qz_lo[z, 2 * slot + p, :], M.na_q[z, :], NA_SCALE,
                                         M.qz_hi[z, 2 * slot + p, :].bitcast(F32), ALU.mult, ALU.subtract)
            dve.tensor_tensor(M.k_lo[:, slot, :], M.na_k[:, :], M.k_hi[:, slot, :].bitcast(F32),
                              ALU.subtract).then_inc(na_split, 1)

        def na_vals(b, slot, part, g=None):
            n = 4 if part < 2 else 1
            dve.wait_ge(na_vhi, v(3 * b + part + 1, g, 6))
            dve.tensor_tensor(M.v_lo[:, slot, 4 * part:4 * part + n, :],
                              ps[:, 6 + part % 2, 0:n * P].rearrange("p (c n) -> p c n", n=P),
                              M.v_hi[:, slot, 4 * part:4 * part + n, :].bitcast(F32), ALU.subtract).then_inc(na_vlo, 1)

        def na_max_(u, g=None):
            dve.wait_ge(na_s, v(u + 1 + 8, g, 16))
            dve.wait_ge(bm_ok, v(u + 1, g, 16))
            dve.tensor_tensor(ps[:, u % 2, 0:256], ps[:, u % 2, 0:256], M.bm[:, u % 4, :], ALU.add).then_inc(na_add, 1)
            dve.wait_ge(na_add, v(u + 1, g, 16))
            dve.tensor_reduce(M.nmax[:, u % 4:u % 4 + 1], ps[:, u % 2, :], AX.X, ALU.max, negate=True).then_inc(na_max, 1)

        def na_rinv_(u, g=None):
            dve.wait_ge(na_exp, v(u + 1, g, 16))
            dve.reciprocal(M.rinv[:, u % 4:u % 4 + 1], M.rsum[:, u % 4:u % 4 + 1]).then_inc(na_rinv, 1)

        def na_out(h, g=None):
            z = slice(64 * (h % 2), 64 * (h % 2) + 64)
            dve.wait_ge(na_ohi, v(h + 1, g, 4))
            def at(x):
                return x[z, h // 2, :] if g is None else x[z, bass.ds(g * 2 + h // 2, 1), :].rearrange("p a n -> p (a n)")
            dve.tensor_tensor(at(M.oa_lo), ps[z, 4 + h % 2, :], at(M.oa_hi).bitcast(F32), ALU.subtract).then_inc(na_o, 1)

        def na_pair(s, g=None, last=False, base=0):
            for u in range(8):
                uu = base + 8 * s + u
                b = uu // 8
                if not (last and u == 7):
                    na_rinv_(uu + 1, g)
                if not last:
                    if u == 1:
                        na_prep(b + 1, (s + 1) % 2, g)
                    if u in (3, 5, 7):
                        na_vals(b + 1, (s + 1) % 2, (u - 3) // 2, g)
                dve.wait_ge(na_pthi, v(uu + 1, g, 16))
                dve.tensor_tensor(M.pt_lo[:, u % 2, :], ps[:, 2 + u % 2, :], M.pt_hi[:, u % 2, :].bitcast(F32),
                                  ALU.subtract).then_inc(na_pt, 1)
                if not (last and u >= 6):
                    na_max_(uu + 2, g)
                if u == 5:
                    na_out(2 * b, g)
            na_out(2 * b + 1, g)

        na_prep(0, 0)
        for part in range(3):
            na_vals(0, 0, part)
        na_max_(0)
        na_max_(1)
        na_rinv_(0)
        with dve.Fori(0, 3) as g:
            for s in range(2):
                na_pair(s, g)
        na_pair(0, base=48)
        na_pair(1, base=48, last=True)

        def ml_prep(h, part, g=None):
            s, z = h % 2, slice(64 * (h % 2), 64 * (h % 2) + 64)
            dve.wait_ge(ml_hi, v(3 * h + part + 1, g, 6))
            if part == 0:
                dve.tensor_tensor(M.mq_lo[:, s, :], M.ml_q[:, :], M.mq_hi[:, s, :].bitcast(F32), ALU.subtract)
                dve.tensor_tensor(M.mqp_lo[z, s, :], M.ml_qp[z, :], M.mqp_hi[z, s, :].bitcast(F32), ALU.subtract)
            elif part == 1:
                dve.tensor_tensor(M.mk_lo[:, s, :], M.ml_k[:, :], M.mk_hi[:, s, :].bitcast(F32), ALU.subtract)
            else:
                dve.tensor_tensor(M.mv_lo[:, s, :, :], M.ml_v[:, :, :], M.mv_hi[:, s, :, :].bitcast(F32),
                                  ALU.subtract).then_inc(ml_lo, 1)

        def ml_max_(u, g=None):
            dve.wait_ge(ml_s, v(u + 1, g, 8))
            b = 1024 * (u % 2)
            dve.tensor_reduce(M.nm0[:, u % 4:u % 4 + 1], psf[:, b:b + TC], AX.X, ALU.max, negate=True).then_inc(ml_m0, 1)
            dve.wait_ge(ml_m0, v(u + 1, g, 8))
            dve.tensor_scalar(M.nmax[:, u % 4:u % 4 + 1], M.nm0[:, u % 4:u % 4 + 1], MLA_SCALE, None,
                              ALU.mult).then_inc(ml_max, 1)

        def ml_rinv_(u, g=None):
            dve.wait_ge(na_exp, v(NA_UNITS + u + 1, g, 8))
            dve.reciprocal(M.rinv[:, u % 4:u % 4 + 1], M.rsum[:, u % 4:u % 4 + 1]).then_inc(na_rinv, 1)

        def ml_head(s, g=None, base=0, last=False):
            h = base + s
            for q in range(4):
                u = 4 * h + q
                if not (last and q == 3):
                    ml_rinv_(u + 1, g)
                if q < 3 and not last:
                    ml_prep(h + 1, q, g)
                dve.wait_ge(na_pthi, v(NA_UNITS + u + 1, g, 8))
                dve.tensor_tensor(M.mpt_lo[:, :, P * q:P * (q + 1)],
                                  psf[:, 2048:2048 + TC].rearrange("p (c n) -> p c n", n=P),
                                  M.mpt_hi[:, :, P * q:P * (q + 1)].bitcast(F32), ALU.subtract).then_inc(ml_pt, 1)
                if not (last and q >= 2):
                    ml_max_(u + 2, g)
            dve.wait_ge(ml_ohi, v(h + 1, g, 2))
            def at(x):
                return x[:, h, :] if g is None else x[:, bass.ds(g * 2 + s, 1), :].rearrange("p a n -> p (a n)")
            dve.tensor_tensor(at(M.ob_lo), ps[:, 6 + s, :], at(M.ob_hi).bitcast(F32), ALU.subtract).then_inc(ml_o, 1)

        dve.wait_ge(ml_kphi, 1)
        dve.tensor_tensor(M.kp_lo[:, :], M.ml_kp[:, :], M.kp_hi[:, :].bitcast(F32), ALU.subtract).then_inc(ml_kplo, 1)
        dve.wait_ge(ml_zero, 1)
        for part in range(3):
            ml_prep(0, part)
        ml_max_(0)
        ml_max_(1)
        ml_rinv_(0)
        with dve.Fori(0, 3) as g:
            for s in range(2):
                ml_head(s, g)
        ml_head(0, base=6)
        ml_head(1, base=6, last=True)

        with dve.Fori(0, 8) as g:
            for n in range(2):
                dve.wait_ge(unit_done, v(N_MERGE + 2 * n + 2, g, 4))
                dve.wait_ge(mg_sig, v(n + 1, g, 2))
                for i in range(2):
                    dve.tensor_tensor(M.sg[:, n, i, :], ps[:, 2 * n + i, :], M.sg[:, n, i, :], ALU.mult).then_inc(mg_part, 1)
                dve.wait_ge(mg_part, v(2 * n + 2, g, 4))
                dve.tensor_tensor(M.yb[:, n, :], M.sg[:, n, 0, :], M.sg[:, n, 1, :], ALU.add).then_inc(mg_y, 1)
                dve.wait_ge(mg_yhi, v(n + 1, g, 2))
                y = bass.ds(g * 2 + n, 1)
                dve.tensor_tensor(M.y_lo[:, y, :].rearrange("p a n -> p (a n)"), M.yb[:, n, :],
                                  M.y_hi[:, y, :].rearrange("p a n -> p (a n)").bitcast(F32),
                                  ALU.subtract).then_inc(mg_ylo, 1)
        dve.memset(M.ssum[:, :], 0.0).then_inc(z_cp, 1)
        with dve.Fori(0, 8) as g:
            for n in range(2):
                dve.wait_ge(z_sq, v(n + 1, g, 2))
                dve.tensor_copy(M.z[:, bass.ds(g * 2 + n, 1), :].rearrange("p a n -> p (a n)"), ps[:, 4 + n, :]
                                ).then_inc(z_cp, 1)
                dve.wait_ge(z_add, v(n + 2, g, 2))
                dve.wait_ge(z_cp, v(n + 2, g, 2))
                dve.tensor_tensor(M.ssum[:, :], M.ssum[:, :], M.zsq[:, n, :], ALU.add).then_inc(z_add, 1)
        dve.wait_ge(rt_ok, 3 + 1)
        dve.reciprocal(M.rs2[:, :], M.sqr2[:, :]).then_inc(rs_ok, 1)
        dve.memset(M.ssum[:, :], 0.0).then_inc(z_add, 1)
        dve.wait_ge(x_ld, 32 + 16)
        for k in range(KD + 1):
            if k < KD:
                dve.wait_ge(zn, k + 1)
                dve.scalar_tensor_tensor(M.x1[:, k, :], M.z[:, k, :], M.gate1[:, k:k + 1], M.x1[:, k, :],
                                         ALU.mult, ALU.add).then_inc(x1_ok, 1)
            if k:
                dve.wait_ge(z_sq, KD + k)
                dve.wait_ge(z_add, KD + 2 + k)
                dve.tensor_tensor(M.ssum[:, :], M.ssum[:, :], M.zsq[:, (k - 1) % 2, :], ALU.add).then_inc(z_add, 1)

        dve.wait_ge(rt_ok, 4 + 1)
        dve.reciprocal(M.rs2[:, :], M.sqr2[:, :]).then_inc(rs_ok, 1)
        dve.wait_ge(x1_st, 64)
        for k in range(KD + 1):
            if k < KD:
                dve.wait_ge(zn, KD + k + 1)
                dve.tensor_scalar(M.x1[:, k, :], M.z[:, k, :], M.scale2[:, k:k + 1], M.mod2[:, KD + k:KD + k + 1],
                                  ALU.mult, ALU.add).then_inc(h2_raw, 1)
            if k:
                dve.wait_ge(h2_hi_ok, k)
                dve.tensor_tensor(M.h2_lo[:, k - 1, :], M.x1[:, k - 1, :], M.h2_hi[:, k - 1, :].bitcast(F32),
                                  ALU.subtract).then_inc(h2_ok, 1)
        dve.wait_ge(sk_h, 1)
        dve.tensor_tensor(M.sk_lo[:, :, :], M.sk_raw[:, :, :], M.sk_hi[:, :, :].bitcast(F32), ALU.subtract).then_inc(sk_ok, 1)

        step = [0, None]

        def done(ins):
            ins.then_inc(tk, 1)
            step[0] += 1

        def after():
            h = step[1]
            if h is LAST:
                dve.wait_ge(tk, 7 * CHOICE_STEPS + step[0])
            else:
                dve.wait_ge(tk, v(step[0] - CHOICE_STEPS, h, CHOICE_STEPS))
                dve.sem_inc(waited_dve, 1)

        LAST = "last"

        def top16(vals, idx, src, tmp):
            for t in range(4):
                done(dve.max(vals[:, t, 0:8], src[:, t, :]))
            after()
            for t in range(4):
                done(dve.max_index(idx[:, t, 0:8], vals[:, t, 0:8], src[:, t, :]))
                done(dve.match_replace(tmp[:, t, :], vals[:, t, 0:8], src[:, t, :], -3.0e38))
            after()
            for t in range(4):
                done(dve.max(vals[:, t, 8:16], tmp[:, t, :]))
            after()
            for t in range(4):
                done(dve.max_index(idx[:, t, 8:16], vals[:, t, 8:16], tmp[:, t, :]))
            after()

        def choice_first(h):
            step[0], step[1] = 0, h
            for p in range(2):
                dve.wait_ge(sc_cp, 14 + p + 1 + 2 if h is LAST else v(p + 1, h, 2))
                dve.sem_inc(waited_dve, 1)
                top16(M.topv[:, p, :, :], M.topi[:, p, :, :], M.sc[:, p, :, :], M.cand2[:, :, 0:P])

        def choice_second(h):
            done(dve.tensor_copy(M.topif[:, :, :, :], M.topi[:, :, :, :]))
            done(dve.tensor_tensor(M.cand[:, :, :].rearrange("p t (a b) -> p t a b", b=16),
                                   M.topv[:, 0, :, :].unsqueeze(3).to_broadcast([P, 4, 16, 16]),
                                   M.topv[:, 1, :, :].unsqueeze(2).to_broadcast([P, 4, 16, 16]), ALU.add)); after()
            top16(M.tv[:, :, :], M.tpos[:, :, :], M.cand[:, :, :], M.cand2[:, :, :])
            dve.tensor_tensor(M.te[:, :, :], M.tv[:, :, :], M.tv[:, :, 0:1].to_broadcast([P, 4, 16]),
                              ALU.subtract).then_inc(te_ok, 1)
            done(dve.tensor_scalar(M.tab[:, 0, :, :], M.tpos[:, :, :], 4, None, ALU.logical_shift_right))
            done(dve.tensor_scalar(M.tab[:, 1, :, :], M.tpos[:, :, :], 15, None, ALU.bitwise_and)); after()
            done(dve.tensor_copy(M.tabf[:, :, :, :], M.tab[:, :, :, :])); after()
            at = slice(7 * 16, 8 * 16) if h is LAST else bass.ds(h * 16 - 16, 16)
            for x in range(2):
                done(dve.tensor_tensor(M.eqb[:, :, :, :], M.tabf[:, x, :, :].unsqueeze(3).to_broadcast([P, 4, 16, 16]),
                                       M.iota[:, 0:16].unsqueeze(1).unsqueeze(1).to_broadcast([P, 4, 16, 16]),
                                       ALU.is_equal)); after()
                done(dve.tensor_tensor(M.eqc[:, :, :, :], M.eqb[:, :, :, :],
                                       M.topif[:, x, :, :].unsqueeze(2).to_broadcast([P, 4, 16, 16]), ALU.mult)); after()
                done(dve.tensor_reduce(M.sel[:, x, :, at], M.eqc[:, :, :, :], AX.X, ALU.add)); after()
            dve.wait_ge(tex_ok, 8 if h is LAST else v(0, h, 1))
            done(dve.tensor_reduce(M.tsum[:, :], M.tex[:, :, :], AX.X, ALU.add)); after()
            done(dve.reciprocal(M.tinv[:, :], M.tsum[:, :])); after()
            done(dve.tensor_tensor(M.sel[:, 2, :, at], M.tex[:, :, :], M.tinv[:, :].unsqueeze(2).to_broadcast([P, 4, 16]),
                                   ALU.mult))
            assert step[0] == CHOICE_STEPS, step[0]

        def query_lo(p, g=None):
            dve.wait_ge(q_h, v(p + 1, g, 2))
            dve.tensor_tensor(M.q_lo[:, p, :], ps[:, p, :], M.q_hi[:, p, :].bitcast(F32), ALU.subtract).then_inc(q_l, 1)

        query_lo(0)
        query_lo(1)
        with dve.Fori(1, 8) as g:
            query_lo(0, g)
            choice_first(g)
            query_lo(1, g)
            choice_second(g)
        choice_first(LAST)
        choice_second(LAST)

        with dve.Fori(0, T // 16) as g:
            for s in range(2):
                dve.wait_ge(selw_ok, v(s + 1, g, 2))
                dve.wait_ge(g_mm, v(s + 1, g, 2))
                for i in range(8):
                    last = dve.tensor_scalar(M.oh1[:, s, i, :], M.iota[:, :], M.selw[:, s, 0, i:i + 1],
                                             M.selw[:, s, 2, i:i + 1], ALU.is_equal, ALU.mult)
                last.then_inc(oh1_ok, 1)

        def exp_block(b, g=None):
            dve.wait_ge(m_gelu, v(b + 1 + 2, g, 8))
            dve.wait_ge(m_eg[b % 2], v(16 * (b // 2 + 1), g, 64))
            dve.tensor_tensor(M.ew[:, b % 2, :], M.eact[:, b % 2, :], M.eg[:, b % 2, :], ALU.mult).then_inc(m_w, 1)
            dve.wait_ge(m_hi, v(b + 1, g, 8))
            dve.tensor_tensor(M.ew_lo[:, b % 8, :], M.ew[:, b % 2, :], M.ew_hi[:, b % 8, :].bitcast(F32),
                              ALU.subtract).then_inc(m_lo, 1)

        def out_blocks(i, n, g=None):
            for k in range(KD):
                if k % 2:
                    dve.wait_ge(unit_done, v(n + k // 2 + 1, g, 32))
                else:
                    dve.wait_ge(m_v, v((i + k) // 2 + 1, g, 16))
                dve.wait_ge(m_acc, v(i + k + 1, g, 32))
                dve.tensor_tensor(M.acc[:, k, :], M.acc[:, k, :], ps[:, 2 + k % 4, :], ALU.add).then_inc(m_acc, 1)

        dve.wait_ge(acc_zero, 1)
        for b in range(4):
            exp_block(b)
        with dve.Fori(0, GROUPS // 2 - 1) as g:
            for r in range(2):
                for q in range(4):
                    exp_block(4 + 4 * r + q, g)
                out_blocks(16 * r, N_MAIN + 16 + 16 * r, g)
        for q in range(4):
            exp_block(4 * GROUPS - 4 + q)
        out_blocks(16 * (GROUPS - 2), N_END - 16)
        out_blocks(16 * (GROUPS - 1), N_END - 8)
        dve.memset(M.fsum[:, :], 0.0).then_inc(z_add, 1)
        for k in range(KD):
            dve.wait_ge(z_sq, 2 * KD + k + 1)
            dve.wait_ge(z_add, 2 * KD + 3 + k + 1)
            dve.tensor_tensor(M.fsum[:, :], M.fsum[:, :], M.fsq[:, k % 2, :], ALU.add).then_inc(z_add, 1)
        dve.wait_ge(rt_ok, 5 + 1)
        dve.reciprocal(M.frs[:, :], M.fsqr[:, :]).then_inc(rs_ok, 1)
        dve.wait_ge(x_ld, 48 + 16)
        for k in range(KD):
            dve.wait_ge(zn, 2 * KD + k + 1)
            dve.scalar_tensor_tensor(M.fx[:, k, :], M.acc[:, k, :], M.gate2[:, k:k + 1], M.fx[:, k, :],
                                     ALU.mult, ALU.add).then_inc(x1_ok, 1)

    @block.tensor
    def _(pe):
        def mm3(out, stat, mov, first, last):
            pe.matmul(out, stat[0], mov[0], start=first, stop=False)
            pe.matmul(out, stat[0], mov[1], start=False, stop=False)
            return pe.matmul(out, stat[1], mov[0], start=False, stop=last)

        def w_at(n, k, w=P):
            return M.w_hi[:, n % RING, k * w:(k + 1) * w], M.w_lo[:, n % RING, k * w:(k + 1) * w]

        def w_ready(n, g=None, per=0):
            pe.wait_ge(w_lo_done, v(n + 1, g, per))

        pe.wait_ge(csilu_ok, 1)

        for half in range(2):
            for k0 in range(4):
                for s in range(4):
                    k = 4 * k0 + s
                    pe.wait_ge(ada1_ld[s], 16 * (4 * half + k0 + 1))
                    for b in range(4):
                        last = pe.matmul(ps[0:2, 4 * half + b, :], M.csilu[:, 2 * k:2 * k + 2],
                                         M.ada1_raw[:, s, 512 * b:512 * (b + 1)], start=(k == 0), stop=(k == KD - 1))
                    last.then_inc(ada1_used, 1)
            if half == 0:
                pe.wait_ge(consts_ld, 64)
        for half in range(2):
            pe.wait_ge(rows_ok, half + 1)
            for n in range(KD):
                last = pe.matmul(ps[:, 0, 32 * half + 2 * n:32 * half + 2 * n + 2],
                                 M.mrow[0:2, (KD * half + n) * P:(KD * half + n + 1) * P], M.ident[0:2, 0:2],
                                 start=True, stop=True)
            last.then_inc(cols_ok, 1)
            if half == 0:
                pe.wait_ge(sq_sum, KD + 1)
                pe.matmul(ps[:, 1, :], M.ones[:, :], M.xsum[:, 0:T], start=True, stop=True)
                pe.matmul(ps[:, 2, 0:C], M.ones[:, :], M.xsum[:, T:TC], start=True, stop=True).then_inc(ss_ok, 1)

        pe.wait_ge(h_ok, KD)

        def p2_block(bg, ctx, g=None):
            pe.wait_ge(p2_ev, v(bg + 1, g, 4))
            for u in range(2):
                w_ready(2 * bg + u, g, 8)
                for j in range(8):
                    k, w = 8 * u + j, w_at(2 * bg + u, j)
                    f, z = k == 0, k == KD - 1
                    last = mm3(ps[:, bg % 2, :], w, (M.h_hi[:, k, 0:T], M.h_lo[:, k, 0:T]), f, z)
                    if ctx:
                        last = mm3(ps[:, 2 + bg % 2, 0:C], w, (M.h_hi[:, k, T:TC], M.h_lo[:, k, T:TC]), f, z)
                last.then_inc(unit_done, 1)

        with pe.Fori(0, 5) as g:
            for s in range(4):
                p2_block(s, True, g)
        p2_block(20, True)
        with pe.Fori(0, 11) as g:
            for s in range(4):
                p2_block(21 + s, False, g)
        for b in (44, 45):
            p2_block(21 + b, False)

        pe.wait_ge(ada2_used, 64 + 4)
        for j in range(64):
            last = pe.matmul(ps[:, 7, j:j + 1], M.ada_sum[:, j * P:(j + 1) * P], M.ones[:, 0:1], start=True, stop=True)
        last.then_inc(mod2_ps, 1)

        pe.wait_ge(p2_ev, 67 + 2)
        for i in range(10):
            pe.wait_ge(pre_sq, i + 1)
            if i < 4:
                pe.matmul(ps[:, 0, :], M.ones[:, :], M.sq3[:, i % 2, 0:T], start=(i == 0), stop=(i == 3))
                pe.matmul(ps[:, 1, 0:C], M.ones[:, :], M.sq3[:, i % 2, T:TC], start=(i == 0), stop=(i == 3)
                          ).then_inc(pre_used, 1)
            else:
                pe.matmul(ps[:, 2, :], M.ones[:, :], M.sq3[:, i % 2, 0:T], start=(i == 4), stop=(i == 9)
                          ).then_inc(pre_used, 1)
        pe.matmul(ps[:, 3, :], M.rotm[:, :], M.kpe[:, 0:T], start=True, stop=True).then_inc(kp_rot, 1)
        pe.wait_ge(pre_ok, 4)
        for b in range(8):
            n = N_KN + b // 2
            w_ready(n)
            pe.wait_ge(pre_ev, b + 1)
            for k in range(4):
                w = w_at(n, 4 * (b % 2) + k)
                mm3(ps[:, 4 + b % 2, :], w, (M.ckv_hi[:, k, 0:T], M.ckv_lo[:, k, 0:T]), k == 0, k == 3)
                last = mm3(ps[:, 6 + b % 2, 0:C], w, (M.ckv_hi[:, k, T:TC], M.ckv_lo[:, k, T:TC]), k == 0, k == 3)
            last.then_inc(unit_done if b % 2 else kn_mm, 1)
        for u in range(4):
            n = N_V + u
            w_ready(n)
            for t in range(6):
                e = 8 + 6 * u + t
                pe.wait_ge(pre_ev, e + 1)
                for k in range(4):
                    last = mm3(ps[:, 4 + e % 2, 0:256],
                               (M.ckv_hi[:, k, t * P:(t + 1) * P], M.ckv_lo[:, k, t * P:(t + 1) * P]),
                               (M.w_hi[:, n % RING, 256 * k:256 * (k + 1)], M.w_lo[:, n % RING, 256 * k:256 * (k + 1)]),
                               k == 0, k == 3)
                last.then_inc(unit_done if t == 5 else kn_mm, 1)
        pe.wait_ge(pre_ok, 10)

        def qb_block(s, base=0, g=None):
            n = N_QB + base + s
            w_ready(n, g, 4)
            pe.wait_ge(pre_ev, v(33 + base + s, g, 4))
            for k in range(6):
                last = mm3(ps[:, 4 + s % 2, :], w_at(n, k), (M.cq_hi[:, k, :], M.cq_lo[:, k, :]), k == 0, k == 5)
            last.then_inc(unit_done, 1)

        with pe.Fori(0, 2) as g:
            for s in range(4):
                qb_block(s, 0, g)
        for s in range(4):
            qb_block(s, 8)
            pe.wait_ge(rope_raw, s + 1)
            pe.matmul(ps[:, 2 + s % 2, :], M.rotm[:, :], M.mst[:, s % 2, 0:T], start=True, stop=True).then_inc(rope_rot, 1)

        pe.wait_ge(pre_ev, 44 + 2)
        def na_vt_(b, part, g=None):
            if part == 0:
                pe.wait_ge(na_ld, v(48 * (b + 1), g, 96))
            if g is not None or 3 * b + part >= 2:
                need = 3 * b + part - (1 if part == 2 else (1 if part == 0 else 2))
                pe.wait_ge(na_vlo, v(need, g, 6))
            for i in range(4 if part < 2 else 1):
                t = V_CHUNKS[4 * part + i]
                last = pe.transpose(ps[:, 6 + part % 2, i * P:(i + 1) * P], M.na_v[:, t:t + P], M.ident[:, :])
            last.then_inc(na_vt, 1)

        def na_s_(u, slot, g=None):
            h, j = u // 4, u % 4
            if u % 8 == 0:
                pe.wait_ge(na_split, v(u // 8 + 1, g, 2))
            if g is not None or u >= 2:
                pe.wait_ge(na_exp, v(u - 1, g, 16))
            qq = tuple(q[:, 2 * slot + h % 2, j * P:(j + 1) * P] for q in (M.qz_hi, M.qz_lo))
            mm3(ps[:, u % 2, 0:256], qq, tuple(k[:, slot, BAND[j]:BAND[j] + 256] for k in (M.k_hi, M.k_lo)), True, True)
            mm3(ps[:, u % 2, 256:512], qq, tuple(k[:, slot, T:TC] for k in (M.k_hi, M.k_lo)), True, True
                ).then_inc(na_s, 1)

        def na_pv_(u, slot, g=None):
            h, j = u // 4, u % 4
            if u % 8 == 0:
                pe.wait_ge(na_vlo, v(3 * (u // 8 + 1), g, 6))
            pe.wait_ge(na_pt, v(u + 1 + 2, g, 16))
            if j == 0:
                pe.wait_ge(na_o, v(h + 1, g, 4))
            for c in range(4):
                ch = V_OF[j][c] if c < 2 else 5 + c
                last = mm3(ps[:, 4 + h % 2, j * P:(j + 1) * P],
                           (M.v_hi[:, slot, ch, :], M.v_lo[:, slot, ch, :]),
                           (M.pt_hi[:, u % 2, c * P:(c + 1) * P], M.pt_lo[:, u % 2, c * P:(c + 1) * P]), c == 0, c == 3)
            last.then_inc(na_pv, 1)

        def na_pair(s, g=None, last=False, base=0):
            for u in range(8):
                uu = base + 8 * s + u
                pe.wait_ge(na_p, v(uu + 1, g, 16))
                pe.wait_ge(na_pt, v(uu + 1, g, 16))
                for c in range(4):
                    t = pe.transpose(ps[:, 2 + u % 2, c * P:(c + 1) * P], M.na_p[:, u % 2, c * P:(c + 1) * P],
                                     M.ident[:, :])
                t.then_inc(na_t, 1)
                if not (last and u >= 6):
                    na_s_(uu + 2, s if u < 6 else (s + 1) % 2, g)
                if u:
                    na_pv_(uu - 1, s, g)
                if not last and u in (2, 4, 6):
                    na_vt_(uu // 8 + 1, (u - 2) // 2, g)
            na_pv_(uu, s, g)

        for part in range(3):
            na_vt_(0, part)
        na_s_(0, 0)
        na_s_(1, 0)
        with pe.Fori(0, 3) as g:
            for s in range(2):
                na_pair(s, g)
        na_pair(0, base=48)
        na_pair(1, base=48, last=True)

        pe.wait_ge(ml_kplo, 1)
        pe.wait_ge(na_o, 16 + 2)

        def ml_s_(u, g=None):
            h, q = u // 4, u % 4
            if q == 0:
                pe.wait_ge(ml_lo, v(h + 1, g, 2))
            if g is not None or u >= 2:
                pe.wait_ge(na_exp, v(NA_UNITS + u - 1, g, 8))
            s = h % 2
            cols = slice(q * P, (q + 1) * P)
            for t0, t1, bank in ((0, T, 2 * (u % 2)), (T, TC, 2 * (u % 2) + 1)):
                out = ps[:, bank, 0:t1 - t0]
                mm3(out, (M.mq_hi[:, s, cols], M.mq_lo[:, s, cols]), (M.mk_hi[:, s, t0:t1], M.mk_lo[:, s, t0:t1]), True, False)
                last = mm3(out, (M.mqp_hi[:, s, cols], M.mqp_lo[:, s, cols]), (M.kp_hi[:, t0:t1], M.kp_lo[:, t0:t1]),
                           False, True)
            last.then_inc(ml_s, 1)

        def ml_head(s, g=None, base=0, last=False):
            h = base + s
            for q in range(4):
                u = 4 * h + q
                pe.wait_ge(na_p, v(NA_UNITS + u + 1, g, 8))
                pe.wait_ge(ml_pt, v(u + 1, g, 8))
                for c in range(6):
                    t = pe.transpose(psf[:, 2048 + c * P:2048 + (c + 1) * P], M.ml_p[:, u % 2, c * P:(c + 1) * P],
                                     M.ident[:, :])
                t.then_inc(na_t, 1)
                if not (last and q >= 2):
                    ml_s_(u + 2, g)
            pe.wait_ge(ml_pt, v(4 * h + 4 + 1, g, 8))
            pe.wait_ge(ml_o, v(h + 1, g, 2))
            for c in range(6):
                t = mm3(ps[:, 6 + s, :], (M.mv_hi[:, s, c, :], M.mv_lo[:, s, c, :]),
                        (M.mpt_hi[:, c, :], M.mpt_lo[:, c, :]), c == 0, c == 5)
            t.then_inc(ml_pv, 1)

        ml_s_(0)
        ml_s_(1)
        with pe.Fori(0, 3) as g:
            for s in range(2):
                ml_head(s, g)
        ml_head(0, base=6)
        ml_head(1, base=6, last=True)

        pe.wait_ge(ml_o, 8 + 2)
        with pe.Fori(0, 8) as g:
            for n in range(2):
                pe.wait_ge(mg_y, v(n + 1, g, 2))
                for i, (hi, lo) in enumerate(((M.oa_hi, M.oa_lo), (M.ob_hi, M.ob_lo))):
                    w_ready(N_MERGE + 2 * n + i, g, 4)
                    for k in range(8):
                        last = mm3(ps[:, 2 * n + i, :], w_at(N_MERGE + 2 * n + i, k), (hi[:, k, :], lo[:, k, :]),
                                   k == 0, k == 7)
                    last.then_inc(unit_done, 1)
        pe.wait_ge(mg_ylo, KD)

        def block16(n, bank, xh, xl, g, per):
            for k in range(KD):
                if k % 8 == 0:
                    w_ready(n + k // 8, g, per)
                last = mm3(ps[:, bank, :], w_at(n + k // 8, k % 8), (xh[:, k, :], xl[:, k, :]), k == 0, k == KD - 1)
                if k % 8 == 7:
                    last.then_inc(unit_done, 1)

        with pe.Fori(0, 8) as g:
            for n in range(2):
                pe.wait_ge(z_add, v(n + 1, g, 2))
                block16(N_OUT + 2 * n, 4 + n, M.y_hi, M.y_lo, g, 4)
        pe.wait_ge(z_add, KD + 2)
        pe.matmul(ps[:, 6, :], M.ones[:, :], M.ssum[:, :], start=True, stop=True).then_inc(ss_ok, 1)
        pe.wait_ge(z_add, KD + 2 + KD + 1)
        pe.matmul(ps[:, 7, :], M.ones[:, :], M.ssum[:, :], start=True, stop=True).then_inc(ss_ok, 1)

        pe.wait_ge(h2_ok, KD)
        pe.wait_ge(sk_ok, 1)

        with pe.Fori(0, 8) as g:
            for p in range(2):
                pe.wait_ge(q_l, v(p + 1, g, 2))
                block16(N_QUERY + 2 * p, p, M.h2_hi, M.h2_lo, g, 4)
            for p in range(2):
                pe.wait_ge(q_l, v(p + 1 + 2, g, 2))
                pe.wait_ge(sc_cp, v(p + 1, g, 2))
                keys = tuple(k[:, bass.ds(g * 2 + p, 1), :].rearrange("p a n -> p (a n)") for k in (M.sk_hi, M.sk_lo))
                for t in range(4):
                    last = mm3(ps[:, 2 + p, t * P:(t + 1) * P],
                               (M.q_hi[:, p, t * P:(t + 1) * P], M.q_lo[:, p, t * P:(t + 1) * P]), keys, True, True)
                last.then_inc(s_mm, 1)
        pe.wait_ge(tk, 8 * CHOICE_STEPS)
        for x in range(3):
            for t in range(4):
                last = pe.transpose(ps[:, x, t * P:(t + 1) * P], M.sel[:, x, t, :], M.ident[:, :])
            last.then_inc(sel_t, 1)
        pe.wait_ge(selT_ok, 3)
        with pe.Fori(0, T // 16) as g:
            for s in range(2):
                pe.wait_ge(oh1_ok, v(s + 1 + 2, g, 2))
                pe.wait_ge(oh2_ok, v(s + 1, g, 2))
                for i in range(8):
                    if i % 4 == 0:
                        pe.wait_ge(g_ev, v(2 * s + i // 4 + 1, g, 4))
                    last = pe.matmul(ps[:, 2 * s + i // 4, P * (i % 4):P * (i % 4 + 1)], M.oh2[:, s, i, :],
                                     M.oh1[:, s, i, :], start=True, stop=True)
                last.then_inc(g_mm, 1)

        def exp_block(b, n, g=None):
            pe.wait_ge(m_gelu, v(b + 1, g, 8))
            block16(n, b % 2, M.h2_hi, M.h2_lo, g, 32)

        def out_blocks(i, n, grp, g=None):
            pe.wait_ge(m_lo, v(i // 4 + 4, g, 8))
            for k in range(KD):
                if k % 2 == 0:
                    w_ready(n + k // 2, g, 32)
                pe.wait_ge(m_acc, v(i + k - 4 + 1 + 16, g, 32))
                for c in range(4):
                    last = mm3(ps[:, 2 + k % 4, :], w_at(n + k // 2, 4 * (k % 2) + c),
                               (M.ew_hi[:, 4 * grp + c, :], M.ew_lo[:, 4 * grp + c, :]), c == 0, c == 3)
                last.then_inc(unit_done if k % 2 else m_v, 1)

        pe.wait_ge(g_ev, T // 4 + 4)
        for b in range(4):
            exp_block(b, N_MAIN + 2 * b)
        with pe.Fori(0, GROUPS // 2 - 1) as g:
            for r in range(2):
                for q in range(4):
                    exp_block(4 + 4 * r + q, N_MAIN + 8 + 16 * r + 2 * q, g)
                out_blocks(16 * r, N_MAIN + 16 + 16 * r, r, g)
        for q in range(4):
            exp_block(4 * GROUPS - 4 + q, N_END - 24 + 2 * q)
        out_blocks(16 * (GROUPS - 2), N_END - 16, 0)
        out_blocks(16 * (GROUPS - 1), N_END - 8, 1)
        pe.wait_ge(z_add, 2 * KD + 3 + KD + 1)
        pe.matmul(ps[:, 6, :], M.ones[:, :], M.fsum[:, :], start=True, stop=True).then_inc(ss_ok, 1)

    block.__exit__(None, None, None)


SCRATCH = {
    "projB": (BOTH_BLOCKS, P, TC), "projL": (LAT_BLOCKS, P, T), "bias_rows": (ROWS, 16, 512),
    "bias": (3, 16, P, 256), "qT": (12, P, T), "knT": (8, P, TC), "vmla": (6, P, 1024), "kp": (P, TC), "x1s": (P, KD, T),
    "gates": (T // TCH, P, P * TCH),
}


def layout(x, c, ctx, c_ctx, w_ada, b_ada, g_pre_mix, g_post_mix, g_pre_ffn, g_post_ffn, w_in, na_rpb,
           mla_g_q, mla_w_q_b, mla_g_kv, mla_w_kv_b, w_branch_a, w_branch_b, w_out,
           peer_w_query, peer_subkeys, peer_u, peer_v):
    f = np.float32

    def cols(w):
        k, n = w.shape
        return w.reshape(k // P, P, n // P, P).transpose(2, 1, 0, 3)

    def feat(x):
        return np.ascontiguousarray(x.T.reshape(-1, P, x.shape[0]).transpose(1, 0, 2))

    w = w_in[0]
    e = np.cumsum([0, 1024, 1024, 1024, 768, 512, 64, D, D])
    qa, ka, va, cq, ckv, kpe, ga, gb = (w[:, e[i]:e[i + 1]] for i in range(8))
    w2 = np.concatenate([ckv, kpe, kpe, ka, va, cq, qa, ga, gb], axis=1)
    units = [cols(w2).reshape(-1, P, 2, UW).transpose(0, 2, 1, 3).reshape(-1, P, UW)]
    wq = mla_w_q_b[0].reshape(768, 8, 192)
    wq = np.concatenate([wq[:, :, :128].reshape(768, 1024), wq[:, :, 128:].reshape(768, 512)], axis=1)
    wkv = mla_w_kv_b[0].reshape(512, 8, 256)
    units.append(cols(wkv[:, :, :128].reshape(512, 1024)).reshape(4, 2, P, 512).transpose(0, 2, 1, 3).reshape(4, P, UW))
    units.append(wkv[:, :, 128:].reshape(4, P, 4, 256).transpose(2, 1, 0, 3).reshape(4, P, UW))
    units.append(np.concatenate([cols(wq).reshape(12, P, 768), np.zeros((12, P, 256), f)], axis=2))
    ab = np.stack([cols(w_branch_a[0]).reshape(16, P, UW), cols(w_branch_b[0]).reshape(16, P, UW)], axis=1)
    units.append(ab.reshape(32, P, UW))
    for w in (w_out[0], peer_w_query[0]):
        units.append(cols(w).reshape(-1, P, 2, UW).transpose(0, 2, 1, 3).reshape(-1, P, UW))
    u = cols(peer_u[0].T).reshape(P, P, 2, UW).transpose(0, 2, 1, 3).reshape(GROUPS, 8, P, UW)
    vv = peer_v[0].reshape(GROUPS, 4, P, 8, 2, P).transpose(0, 3, 2, 4, 1, 5).reshape(GROUPS, 8, P, UW)
    body = [u[0]]
    for g in range(1, GROUPS):
        body += [u[g], vv[g - 1]]
    body.append(vv[GROUPS - 1])
    units += body
    wall = np.concatenate(units, axis=0)
    assert wall.shape[0] == N_END, wall.shape
    wa = w_ada[0]
    tok = x[0].reshape(ROWS, GRID_W, D).transpose(1, 0, 2).reshape(T, D)
    vec = np.concatenate([b_ada[0].reshape(96, P), g_pre_mix[0].reshape(KD, P), g_post_mix[0].reshape(KD, P),
                          g_pre_ffn[0].reshape(KD, P), g_post_ffn[0].reshape(KD, P), mla_g_q[0].reshape(6, P),
                          mla_g_kv[0].reshape(4, P)], axis=0)
    t = np.arange(T)
    row, col = (t % ROWS).astype(f), (t // ROWS).astype(f)
    inv = (10000.0 ** (-np.arange(16, dtype=f) / f(16))).astype(f)
    ang = np.concatenate([row[:, None] * inv, col[:, None] * inv], axis=1).T
    cos, sin = np.cos(ang).astype(f), np.sin(ang).astype(f)
    rot = np.zeros((P, P), f)
    for b in range(2):
        for i in range(32):
            rot[64 * b + 32 + i, 64 * b + i] = -1.0
            rot[64 * b + i, 64 * b + 32 + i] = 1.0
    mask = np.zeros((P, 4, 256), f)
    for j in range(4):
        qc = 16 * j + np.arange(P) // ROWS
        kc = BAND[j] // ROWS + np.arange(256) // ROWS
        off = kc[None, :] - np.clip(qc - 8, 0, GRID_W - 16)[:, None]
        mask[:, j] = np.where((off >= 0) & (off < 16), 0.0, -1e30)
    return {
        "wall": wall,
        "ada1": np.ascontiguousarray(wa[:, :4096].reshape(KD, P, 2, 2048).transpose(2, 0, 1, 3)).reshape(32, P, 2048),
        "ada2": np.ascontiguousarray(wa[:, 4096:].reshape(KD, P, 4, 2048).transpose(0, 2, 1, 3)),
        "xT": feat(tok), "ctxT": feat(ctx[0]),
        "cvec": np.ascontiguousarray(np.stack([c[0], c_ctx], axis=1).reshape(KD, P, 2).transpose(1, 0, 2).reshape(P, 32)),
        "vecs": np.ascontiguousarray(vec.T),
        "rpb": np.ascontiguousarray(na_rpb[0].transpose(0, 2, 1)),
        "subk": np.ascontiguousarray(peer_subkeys[0].transpose(3, 0, 1, 2).reshape(P, 16, P)),
        "consts": np.stack([np.ones((P, P), f), np.eye(P, dtype=f), np.tile(np.arange(P, dtype=f), (P, 1)), rot]),
        "rope": np.stack([np.tile(cos, (4, 1)), np.tile(sin, (4, 1))]),
        "maskc": mask,
    }


def kernel(**inputs):
    from concourse.bass_utils import run_bass_kernel_spmd as run
    import concourse.bacc as bacc

    arrays = layout(**{k: np.asarray(x) for k, x in inputs.items()})
    nc = bacc.Bacc("TRN2", target_bir_lowering=False, num_devices=1)
    a = {k: nc.dram_tensor(k, x.shape, F32, kind="ExternalInput").ap() for k, x in arrays.items()}
    for k, shape in SCRATCH.items():
        a[k] = nc.dram_tensor(k, shape, F32, kind="Internal").ap()
    a["out"] = nc.dram_tensor("out", (P, KD, T), F32, kind="ExternalOutput").ap()
    build(nc, a)
    r = run(nc, [arrays], core_ids=[0]).results[0]
    o = r["out"].transpose(1, 0, 2).reshape(D, GRID_W, ROWS).transpose(2, 1, 0).reshape(1, T, D)
    return np.ascontiguousarray(o)
```

```python
import numpy as np
import concourse.bass as bass
from concourse import mybir

F32 = mybir.dt.float32
F32R = mybir.dt.float32r
U32 = mybir.dt.uint32
ALU = mybir.AluOpType
ACT = mybir.ActivationFunctionType
AX = mybir.AxisListType

P = 128
D = 2048
KD = D // P
T = 512
C = 256
TC = T + C
ROWS = 8
GRID_W = 64
EPS = 1e-6
MLA_SCALE = float((128 + 64) ** -0.5)
NA_SCALE = 0.125

RING = 4
UW = 1024
BOTH_BLOCKS = 21
LAT_BLOCKS = 46
N_BOTH = 0
N_LAT = N_BOTH + 2 * BOTH_BLOCKS
N_KN = N_LAT + 2 * LAT_BLOCKS
N_V = N_KN + 4
N_QB = N_V + 4
N_MERGE = N_QB + 12
N_OUT = N_MERGE + 32
N_QUERY = N_OUT + 32
N_MAIN = N_QUERY + 32
GROUPS = 32
N_END = N_MAIN + GROUPS * 16
B_CKV, B_KPE, B_KA, B_VA = 0, 4, 5, 13
L_CQ, L_QA, L_GA, L_GB = 0, 6, 14, 30
BAND = [0, 64, 192, 256]
SHIFT = [0, 1, 1, 2]
V_CHUNKS = [0, 128, 64, 192, 320, 256, 384, 512, 640]
V_OF = [(0, 1), (2, 3), (3, 4), (5, 6)]
CHOICE_STEPS = 2 * 4 * 5 + 2 + 4 * 5 + 3 + 2 + 2 + 3
CHOICE_SCORES = 2 * 4 * 3
CHOICE_MATCHES = 2 * 4 * 5 + 2 + 4 * 5 + 3 + 2
VEC_B, VEC_PRE, VEC_POST, VEC_PREF, VEC_POSTF, VEC_GQ, VEC_GKV = 0, 96, 112, 128, 144, 160, 166
NVEC = 170
TCH = 32
NA_UNITS = 64
DX = 63


def dram(ap, offset, pattern):
    return bass.AP(tensor=ap.tensor, offset=offset, ap=pattern)


def v(base, g=None, per=0):
    return base if g is None else g * per + base


def build(nc, a):
    sb_at = [16512]

    def place(spec, at):
        out = {}
        for name, shape, dt in spec:
            n = 4 * int(np.prod(shape[1:]))
            out[name] = nc.alloc_sbuf_tensor_at(name, shape, dt, offset=at)
            at += (n + 31) // 32 * 32
        assert at <= nc.sbuf_usable_end, (spec[0][0], at)
        return out, at

    m = {}

    def region(at, *spec):
        got, end = place(spec, at)
        m.update(got)
        return end

    END = region(sb_at[0],
                 ("w_raw", [P, RING, UW], F32), ("w_hi", [P, RING, UW], F32R), ("w_lo", [P, RING, UW], F32R),
                 ("ones", [P, P], F32), ("ident", [P, P], F32), ("iota", [P, P], F32),
                 ("vecs", [P, NVEC], F32), ("cvec", [P, KD * 2], F32), ("csig", [P, KD * 2], F32),
                 ("csilu", [P, KD * 2], F32), ("c1", [P, KD], F32),
                 ("mod1", [P, 32, 2], F32), ("scale1", [P, KD, 2], F32), ("mod2", [P, 64], F32),
                 ("scale2", [P, KD], F32), ("gate1", [P, KD], F32), ("gate2", [P, KD], F32),
                 ("eps", [P, 1], F32), ("nmax", [P, 4], F32), ("nm0", [P, 4], F32), ("rsum", [P, 4], F32), ("rinv", [P, 4], F32))
    e = region(END, ("h_hi", [P, KD, TC], F32R), ("xin", [P, KD, TC], F32))
    region(END + 4 * KD * TC, ("h_lo", [P, KD, TC], F32R))
    e1 = region(e, ("ada_sum", [P, 8192], F32), ("ada_raw", [P, 2, 2048], F32), ("stage", [P, 2, TC], F32))
    region(e, ("ada1_raw", [P, 4, 2048], F32))
    region(e + 32768, ("sq", [P, 2, TC], F32), ("rs", [P, TC], F32), ("sqr", [P, TC], F32),
           ("xsum", [P, TC], F32))
    region(END, ("mrow", [P, 4096], F32))
    oa_end = region(END, ("oa_hi", [P, 8, T], F32R), ("oa_lo", [P, 8, T], F32R))
    ob_end = region(oa_end, ("ob_hi", [P, 8, T], F32R), ("ob_lo", [P, 8, T], F32R))
    region(END,
           ("cq", [P, 6, T], F32),
           ("cq_hi", [P, 6, T], F32R), ("cq_lo", [P, 6, T], F32R),
           ("ckv_hi", [P, 4, TC], F32R), ("ckv_lo", [P, 4, TC], F32R),
           ("rotm", [P, P], F32), ("cos", [P, T], F32), ("sin", [P, T], F32),
           ("sqr3", [P, TC], F32), ("rs3", [P, TC], F32),
           ("mst", [P, 2, TC], F32), ("rope_t", [P, T], F32), ("bpre", [P, DX * 8], F32))
    region(e + 32768, ("ckv", [P, 4, TC], F32), ("kpe", [P, TC], F32))
    region(e1, ("sq3", [P, 2, TC], F32))
    region(e1 - 4 * 2 * TC, ("na_q", [P, T], F32), ("na_k", [P, TC], F32), ("na_v", [P, TC], F32))
    region(e + 32768, ("qz_hi", [P, 4, T], F32R), ("qz_lo", [P, 4, T], F32R))
    region(oa_end + 4 * 4 * P * 12,
           ("k_hi", [P, 2, TC], F32R), ("k_lo", [P, 2, TC], F32R),
           ("v_hi", [P, 2, 9, P], F32R), ("v_lo", [P, 2, 9, P], F32R),
           ("na_p", [P, 4, T], F32), ("pt_hi", [P, 2, T], F32R), ("pt_lo", [P, 2, T], F32R),
           ("bm", [P, 4, 256], F32), ("mask", [P, 4, 256], F32))
    region(ob_end,
           ("ml_q", [P, T], F32), ("ml_k", [P, TC], F32), ("ml_v", [P, 6, P], F32), ("ml_qp", [P, T], F32),
           ("mq_hi", [P, 2, T], F32R), ("mq_lo", [P, 2, T], F32R),
           ("mk_hi", [P, 2, TC], F32R), ("mk_lo", [P, 2, TC], F32R),
           ("mv_hi", [P, 2, 6, P], F32R), ("mv_lo", [P, 2, 6, P], F32R),
           ("mqp_hi", [P, 2, T], F32R), ("mqp_lo", [P, 2, T], F32R),
           ("kp_hi", [P, TC], F32R), ("kp_lo", [P, TC], F32R),
           ("ml_p", [P, 4, TC], F32), ("mpt_hi", [P, 6, T], F32R))
    ml_p_at = ob_end + 4 * (2 * T + 2 * TC + 8 * T + 8 * TC + 2 * TC)
    region(ml_p_at + 4 * (4 * TC + 6 * T), ("mpt_lo", [P, 6, T], F32R))
    region(ml_p_at + 4 * 3 * TC, ("ml_kp", [P, TC], F32))
    y_end = region(ob_end, ("y_hi", [P, KD, T], F32R), ("y_lo", [P, KD, T], F32R))
    region(y_end, ("sg", [P, 2, 2, T], F32), ("yb", [P, 2, T], F32))
    z_end = region(END, ("z", [P, KD, T], F32), ("x1", [P, KD, T], F32))
    assert z_end <= ob_end
    region(y_end, ("zsq", [P, 2, T], F32), ("ssum", [P, T], F32), ("rs2", [P, T], F32), ("sqr2", [P, T], F32))
    h2_end = region(END, ("h2_hi", [P, KD, T], F32R), ("h2_lo", [P, KD, T], F32R))
    region(h2_end, ("sel", [P, 3, 4, P], F32),
           ("sk_hi", [P, 16, P], F32R), ("sk_lo", [P, 16, P], F32R), ("sk_raw", [P, 16, P], F32),
           ("q_hi", [P, 2, T], F32R), ("q_lo", [P, 2, T], F32R),
           ("sc", [P, 2, 4, P], F32), 
           ("topv", [P, 2, 4, 16], F32), ("topi", [P, 2, 4, 16], U32), ("topif", [P, 2, 4, 16], F32),
           ("cand", [P, 4, 256], F32), ("cand2", [P, 4, 256], F32),
           ("tv", [P, 4, 16], F32), ("tpos", [P, 4, 16], U32), ("tab", [P, 2, 4, 16], U32),
           ("tabf", [P, 2, 4, 16], F32), ("eqb", [P, 2, 4, 16, 16], F32), ("eqc", [P, 2, 4, 16, 16], F32),
           ("te", [P, 4, 16], F32), ("tex", [P, 4, 16], F32), ("tsum", [P, 4], F32), ("tinv", [P, 4], F32))
    region(h2_end + 4 * 3 * 4 * P, ("selT", [P, 3, T], F32), 
           ("oh1", [P, 4, 8, P], F32), ("oh2", [P, 4, 8, P], F32), ("gst", [P, 2, P, TCH], F32))
    region(h2_end, ("acc", [P, KD, T], F32), ("ew_hi", [P, 8, T], F32R), ("ew_lo", [P, 8, T], F32R),
           ("eg", [P, 2, T], F32), ("ew", [P, 2, T], F32))
    region(nc.sbuf_usable_end // 32 * 32 - 4 * 4 * T, ("eact", [P, 4, T], F32))
    region(END, ("fx", [P, KD, T], F32), ("fsq", [P, 2, T], F32), ("fsum", [P, T], F32), ("frs", [P, T], F32),
           ("fsqr", [P, T], F32))

    M = type("M", (), m)
    ps = nc.alloc_psum_tensor("ps", [P, 8, 512], F32)
    psf = ps[:, :, :].rearrange("p b n -> p (b n)")

    S = {}

    def sem(name):
        if name not in S:
            S[name] = nc.alloc_semaphore(name)
        return S[name]

    w_ld = [sem(f"w_loaded{i}") for i in range(RING)]
    w_hi_done, w_lo_done, unit_done = sem("w_hi_done"), sem("w_lo_done"), sem("unit_done")
    consts_ld, x_ld, silu_ld = sem("consts_loaded"), sem("x_loaded"), sem("c_loaded")
    ada1_ld = [sem(f"ada1_loaded{i}") for i in range(4)]
    ada1_used, csig_ok, csilu_ok, sq_ok, sq_sum, ss_ok = (sem(n) for n in (
        "ada1_used", "c_sigmoid_ready", "c_silu_ready", "squares_ready", "squares_added", "square_sum_ready"))
    rt_ok, rs_ok, rows_ok, h_raw, h_hi_ok, h_ok, cols_ok = (sem(n) for n in (
        "root_ready", "rs_ready", "mod_rows_ready", "h_ready_f32", "h_hi_ready", "h_ready", "mod_columns_ready"))
    dve0 = sem("dve_step")
    bpre_z, bpre_ld, br_st, bf_st = sem("bias_cleared"), sem("bias_loaded"), sem("bias_rows_stored"), sem("bias_stored")
    p2_ev, ada2_used = sem("proj_evacuated"), sem("ada2_used")
    p2_st = [sem(f"proj_stored{i}") for i in range(2)]
    ada2_ld = [sem(f"ada2_loaded{i}") for i in range(2)]
    ada_zero, mod2_ps, mod2_ok = sem("ada_sum_cleared"), sem("mod2_product_ready"), sem("mod2_ready")

    (pre_ld, pre_sq, pre_n, pre_hi, pre_ok, pre_ev, kp_rot, kp_ok, kp_st,
     rope_raw, rope_rot, rope_step) = (sem("pre_" + n) for n in (
         "loaded", "squares", "normed", "hi", "ready", "evacuated", "key_rotated", "key_ready", "key_stored", "rope_copied", "rope_rotated", "rope_step"))
    pre_used, kn_mm, ml_m0 = sem("pre_squares_used"), sem("pre_product_ready"), sem("ml_max_raw")
    pre_st = [sem(f"pre_stored{i}") for i in range(2)]
    (na_ld, na_s, na_add, na_max, na_exp, na_rinv, na_p, na_t, na_pthi, na_pt, na_pv, na_ohi, na_o,
     na_qkhi, na_split, na_vt, na_vhi, na_vlo, na_zero, bm_ok, mask_ld) = (sem("na_" + n) for n in (
         "loaded", "scores", "biased", "max", "exp", "rinv", "probs", "transposed", "pt_hi", "pt_lo", "pv", "out_hi",
         "out", "qk_hi", "qk_lo", "v_transposed", "v_hi", "v_lo", "zeroed", "bias_masked", "mask_loaded"))
    bm_ld = [sem(f"na_bias_loaded{i}") for i in range(4)]
    (ml_ld, ml_kpld, ml_kphi, ml_kplo, ml_zero, ml_s, ml_max, ml_pt, ml_pv,
     ml_ohi, ml_o, ml_hi, ml_lo) = (sem("ml_" + n) for n in (
         "loaded", "kp_loaded", "kp_hi", "kp_lo", "zeroed", "scores", "max", "pt_lo", "pv", "out_hi", "out", "prep_hi", "prep_lo"))
    (mg_sig, mg_part, mg_y, mg_yhi, mg_ylo, z_sq, z_cp, z_add, zn, x1_ok,      x1_st, h2_hi_ok, h2_ok) = (sem(n) for n in (
         "gates_ready", "branch_gated", "merged", "y_hi_ready", "y_lo_ready", "z_squares", "z_copied", "z_squares_added",
         "z_normed", "x1_ready", "x1_stored", "h2_hi_ready", "h2_ready"))
    mg_ld = [sem(f"gates_loaded{i}") for i in range(2)]
    (sk_ld, sk_h, sk_ok, q_h, q_l, s_mm, sc_cp, acc_zero, tk, te_ok, tex_ok, sel_t, selT_ok, oh1_ok,
     oh2_ok, g_mm, g_ev) = (sem(n) for n in (
         "subkeys_loaded", "subkeys_hi", "subkeys_ready", "query_hi", "query_lo", "key_scores", "key_scores_copied",
         "sum_cleared", "topk_step", "top_scores_ready", "top_exp_ready", "choice_transposed",
         "choice_columns_ready", "onehot1_ready", "onehot2_ready", "gates_product",
         "gates_copied"))
    g_st = [sem(f"gates_stored{i}") for i in range(2)]
    ckv_ld = sem("ckv_loaded")
    waited_dve, oh_eq, eqc_ok = sem("waited_dve"), sem("onehot2_equal"), sem("match_keys_ready")
    zn_even = sem("even_chunks_normed")
    (m_gelu, m_w, m_hi, m_lo, m_v, m_acc) = (sem("ffn_" + n) for n in (
        "gelu", "weighted", "weighted_hi", "weighted_lo", "product", "added"))
    m_eg = [sem(f"ffn_gates_loaded{i}") for i in range(2)]

    block = nc.Block()
    block.__enter__()

    @block.sync
    def _(sp):
        def load_unit(n, g=None, per=0):
            if g is not None or n >= RING:
                sp.wait_ge(w_lo_done, v(n - RING + 1, g, per))
            src = a["wall"][n] if g is None else a["wall"][bass.ds(g * per + n, 1)].rearrange("a p n -> p (a n)")
            sp.dma_start(M.w_raw[:, n % RING, :], src).then_inc(w_ld[n % RING], 16)

        sp.dma_start(M.cvec[:, :], a["cvec"]).then_inc(silu_ld, 16)
        sp.dma_start(M.vecs[:, :], a["vecs"]).then_inc(consts_ld, 16)
        for i, name in enumerate(("ones", "ident", "iota")):
            sp.dma_start(m[name][:, :], a["consts"][i]).then_inc(consts_ld, 16)
        for s in range(4):
            sp.dma_start(M.ada1_raw[:, s, :], a["ada1"][s]).then_inc(ada1_ld[s], 16)
        sp.dma_start(M.xin[:, :, 0:T], a["xT"]).then_inc(x_ld, 16)
        sp.dma_start(M.xin[:, :, T:TC], a["ctxT"]).then_inc(x_ld, 16)
        with sp.Fori(1, 8) as g:
            for s in range(4):
                sp.wait_ge(ada1_used, v(s - 3, g, 4))
                sp.dma_start(M.ada1_raw[:, s, :], a["ada1"][bass.ds(g * 4 + s, 1)].rearrange("a p n -> p (a n)")
                             ).then_inc(ada1_ld[s], 16)
        for n in range(2 * RING):
            load_unit(n)
        sp.wait_ge(h_ok, KD)

        def p2_block(b, ctx, bg, g=None, ada=None):
            ub, up = (b * 2, None if g is None else 8) if ctx else (N_LAT + b * 2, None if g is None else 8)
            if ada is not None:
                sp.wait_ge(ada2_used, v(ada + 3, g, 4))
                kk, q = (ada // 4, ada % 4)
                src = a["ada2"][kk, q] if g is None else a["ada2"][bass.ds(g + kk, 1), q].rearrange("a p n -> p (a n)")
                sp.dma_start(M.ada_raw[:, ada % 2, :], src).then_inc(ada2_ld[ada % 2], 16)
            for j in range(2):
                load_unit(ub + 8 + j, g, 8)
            sp.wait_ge(p2_ev, v(bg + 3, g, 4))
            dst = a["projB"] if ctx else a["projL"]
            dst = dst[b] if g is None else dst[bass.ds(g * 4 + b, 1)].rearrange("a p n -> p (a n)")
            sp.dma_start(dst, M.stage[:, bg % 2, 0:TC if ctx else T]).then_inc(p2_st[bg % 2], 16)

        with sp.Fori(0, 5) as g:
            for s in range(4):
                p2_block(s, True, s, g, ada=s)
        p2_block(20, True, 20)
        with sp.Fori(0, 11) as g:
            for s in range(4):
                p2_block(s, False, 21 + s, g, ada=20 + s)
        sp.wait_ge(ada2_used, 64 + 4)
        sp.wait_ge(p2_st[0], 16 * (33 + 1))
        sp.wait_ge(p2_st[1], 16 * (32 + 1))
        sp.dma_start(M.ckv[:, :, :], a["projB"][B_CKV:B_CKV + 4].rearrange("b p t -> p b t")).then_inc(ckv_ld, 16)
        sp.dma_start(M.kpe[:, :], a["projB"][B_KPE]).then_inc(ckv_ld, 16)
        for b in (44, 45):
            p2_block(b, False, 21 + b)
        for s in range(2):
            sp.wait_ge(p2_st[s], 16 * ((67 + 1 - s) // 2 + 1))

        sp.wait_ge(unit_done, N_KN)
        sp.dma_start(M.rotm[:, :], a["consts"][3]).then_inc(pre_ld, 16)
        sp.dma_start(M.cos[:, :], a["rope"][0]).then_inc(pre_ld, 16)
        sp.dma_start(M.sin[:, :], a["rope"][1]).then_inc(pre_ld, 16)
        sp.dma_start(M.cq[:, :, :], a["projL"][L_CQ:L_CQ + 6].rearrange("b p t -> p b t")).then_inc(pre_ld, 16)

        def bias_rows():
            sp.wait_ge(bpre_z, 1)
            for r in range(ROWS):
                sp.dma_start(M.bpre[16 * r:16 * r + 16, 128:128 + 31 * 8].rearrange("h (x y) -> h x y", y=8),
                             a["rpb"][:, :, 7 - r:15 - r]).then_inc(bpre_ld, 16)
            sp.wait_ge(bpre_ld, 16 * ROWS)
            sp.dma_start(a["bias_rows"].rearrange("r h n -> (r h) n")[:, 0:DX * 8], M.bpre[:, :]).then_inc(br_st, 16)
            sp.wait_ge(br_st, 16)

        tables = [(o, h) for o in range(3) for h in range(16)]

        def bias_tables(count):
            for o, h in [tables.pop(0) for _ in range(count)]:
                src = dram(a["bias_rows"], h * 512 + (31 - 8 * o) * 8, [[16 * 512, ROWS], [-8, 16], [1, 256]])
                sp.dma_start(a["bias"][o, h].rearrange("(c r) k -> r c k", r=ROWS), src).then_inc(bf_st, 16)

        def pre_store(e, dst, g=None, per=0, w=T):
            sp.wait_ge(pre_ev, v(e + 3, g, per))
            sp.dma_start(dst, M.mst[:, e % 2, 0:w]).then_inc(pre_st[e % 2], 16)

        for b in range(8):
            if b % 2 == 0:
                load_unit(N_KN + b // 2 + 8)
            pre_store(b, a["knT"][b], w=TC)
            if b == 1:
                bias_rows()
            if b >= 2:
                bias_tables(2)
        for u in range(4):
            for t in range(6):
                pre_store(8 + 6 * u + t, a["vmla"][t, :, 256 * u:256 * (u + 1)], w=256)
                bias_tables(1)
            load_unit(N_V + u + 8)
        def na_prep(b, g=None):
            srcs = [a[name][blk + b] if g is None else a[name][bass.ds(g * 2 + (b + blk), 1)].rearrange("a p n -> p (a n)")
                    for name, blk in (("projL", L_QA), ("projB", B_KA), ("projB", B_VA))]
            for i, (dst, src) in enumerate(zip((M.na_q, M.na_k, M.na_v), srcs)):
                if i == 0 and (g is not None or b):
                    sp.wait_ge(na_split, v(b, g, 2))
                if i == 2 and (g is not None or b):
                    sp.wait_ge(na_vt, v(3 * b, g, 6))
                sp.dma_start(dst[:, :], src).then_inc(na_ld, 16)

        sp.wait_ge(pre_used, 10)
        sp.dma_start(M.mask[:, :, :], a["maskc"]).then_inc(mask_ld, 16)
        na_prep(0)
        with sp.Fori(0, 2) as g:
            for s in range(4):
                load_unit(N_QB + 8 + s, g, 4)
                pre_store(32 + s, a["qT"][bass.ds(g * 4 + s, 1)].rearrange("a p n -> p (a n)"), g, 4)
        sp.wait_ge(kp_ok, 1)
        sp.dma_start(a["kp"], M.kpe[:, :]).then_inc(kp_st, 16)
        for s in range(4):
            load_unit(N_QB + 16 + s)
            pre_store(40 + s, a["qT"][8 + s])
            bias_tables(3)
        for s in range(2):
            sp.wait_ge(pre_st[s], 16 * 23)
        sp.wait_ge(kp_st, 16)
        sp.wait_ge(bf_st, 16 * 48)

        def na_bias(u, g=None):
            h, j = u // 4, u % 4
            src = a["bias"][SHIFT[j], h] if g is None else a["bias"][SHIFT[j], bass.ds(g * 4 + h, 1)].rearrange("a p n -> p (a n)")
            sp.wait_ge(na_max, v(u + 1, g, 16))
            sp.dma_start(M.bm[:, u % 4, :], src).then_inc(bm_ld[u % 4], 16)

        with sp.Fori(0, 3) as g:
            for s in range(2):
                for u in range(8):
                    na_bias(8 * s + u, g)
                    if u == 1:
                        na_prep(s + 1, g)
        for s in range(2):
            for u in range(8):
                na_bias(48 + 8 * s + u)
                if u == 1 and s == 0:
                    na_prep(7)

        sp.wait_ge(na_o, 16 + 2)
        sp.dma_start(M.ml_kp[:, :], a["kp"]).then_inc(ml_kpld, 16)

        def ml_prep(h, g=None):
            z = 64 * (h % 2)
            def at(x, n):
                return x[n] if g is None else x[bass.ds(g * 2 + n, 1)].rearrange("a p n -> p (a n)")
            qp = a["qT"][8 + h // 2, z:z + 64] if g is None else a["qT"][bass.ds(g + (8 + h // 2), 1), z:z + 64].rearrange("a p n -> p (a n)")
            vm = a["vmla"].rearrange("t p (h n) -> h p t n", n=P)
            vm = vm[h] if g is None else vm[bass.ds(g * 2 + h, 1)].rearrange("a p t n -> p (a t) n")
            q, k = at(a["qT"], h), at(a["knT"], h)
            if g is not None or h:
                sp.wait_ge(ml_lo, v(h, g, 2))
            sp.dma_start(M.ml_q[:, :], q).then_inc(ml_ld, 16)
            sp.dma_start(M.ml_k[:, :], k).then_inc(ml_ld, 16)
            sp.dma_start(M.ml_v[:, :, :], vm).then_inc(ml_ld, 16)
            sp.dma_start(M.ml_qp[z:z + 64, :], qp).then_inc(ml_ld, 16)

        ml_prep(0)
        with sp.Fori(0, 3) as g:
            for s in range(2):
                ml_prep(s + 1, g)
        ml_prep(7)

        sp.wait_ge(ml_o, 8 + 2)

        def mg_gates(n, g=None):
            srcs = [a["projL"][bass.ds(g * 2 + (n + blk), 1) if g is not None else slice(n + blk, n + blk + 1)
                               ].rearrange("a p n -> p (a n)") for blk in (L_GA, L_GB)]
            sp.wait_ge(mg_y, v(n + 1, g, 2))
            for i in range(2):
                sp.dma_start(M.sg[:, n % 2, i, :], srcs[i]).then_inc(mg_ld[n % 2], 16)

        def mg_units(n, g=None):
            for j in range(2):
                load_unit(N_MERGE + 2 * n + 8 + j, g, 4)

        mg_gates(0)
        with sp.Fori(0, 7) as g:
            for n in range(2):
                mg_gates(n + 1, g)
                mg_units(n, g)
        mg_gates(15)
        mg_units(14)
        mg_units(15)
        sp.wait_ge(unit_done, N_OUT)
        with sp.Fori(0, 8) as g:
            for j in range(4):
                load_unit(N_OUT + 8 + j, g, 4)
            sp.dma_start(M.x1[:, bass.ds(g * 2, 2), :], a["xT"][:, bass.ds(g * 2, 2), :]).then_inc(x_ld, 16)
        for q in range(4):
            sp.wait_ge(x1_ok, 4 * q + 4)
            sp.dma_start(a["x1s"][:, 4 * q:4 * q + 4, :], M.x1[:, 4 * q:4 * q + 4, :]).then_inc(x1_st, 16)

        sp.wait_ge(unit_done, N_QUERY)
        sp.dma_start(M.sk_raw[:, :, :], a["subk"]).then_inc(sk_ld, 16)
        with sp.Fori(0, 8) as g:
            for j in range(4):
                load_unit(N_QUERY + 8 + j, g, 4)
        for n in range(8):
            load_unit(N_MAIN + 8 + n)
        def store_gates(s, g):
            sp.wait_ge(g_ev, v(TCH // 4 * (s + 1) + 4, g, TCH // 2))
            sp.dma_start(a["gates"][bass.ds(g * 2 + s, 1)].rearrange("a p n -> p (a n)"),
                         M.gst[:, s, :, :].rearrange("p e t -> p (e t)")).then_inc(g_st[s], 16)

        with sp.Fori(0, T // TCH // 2) as g:
            for s in range(2):
                store_gates(s, g)
        for s in range(2):
            sp.wait_ge(g_st[s], 16 * (T // TCH // 2 + 1))

        gates_by_block = a["gates"].rearrange("c p (e t) -> e p c t", t=TCH)

        def exp_block(b, n=None, g=None):
            src = gates_by_block[b] if g is None else gates_by_block[bass.ds(g * 8 + b, 1)].rearrange("a p c t -> p (a c) t")
            sp.wait_ge(m_w, v(b + 3, g, 8))
            sp.dma_start(M.eg[:, b % 2, :].rearrange("p (c t) -> p c t", t=TCH), src).then_inc(m_eg[b % 2], 16)
            if n is not None:
                for j in range(2):
                    load_unit(n + j + 8, g, 32)

        def out_units(n, g=None, count=8):
            for j in range(count):
                load_unit(n + j + 8, g, 32)

        for b in range(4):
            exp_block(b)
        with sp.Fori(0, GROUPS // 2 - 1) as g:
            for r in range(2):
                for q in range(4):
                    exp_block(4 + 4 * r + q, N_MAIN + 8 + 16 * r + 2 * q, g)
                out_units(N_MAIN + 16 + 16 * r, g)
        for q in range(4):
            exp_block(4 * GROUPS - 4 + q, N_END - 24 + 2 * q)
        out_units(N_END - 16)
        sp.wait_ge(m_lo, 4 * GROUPS)
        sp.dma_start(M.fx[:, :, :], a["x1s"]).then_inc(x_ld, 16)
        for q in range(4):
            sp.wait_ge(x1_ok, KD + 4 * q + 4)
            sp.dma_start(a["out"][:, 4 * q:4 * q + 4, :], M.fx[:, 4 * q:4 * q + 4, :]).then_inc(x1_st, 16)
        sp.wait_ge(x1_st, 64 + 64)
        sp.wait_ge(x1_st, 64)

    @block.scalar
    def _(act):
        def w_hi(n, g=None, per=0):
            act.wait_ge(w_ld[n % RING], v(16 * (n // RING + 1), g, 16 * (per // RING)))
            if g is not None or n >= RING:
                act.wait_ge(unit_done, v(n - RING + 1, g, per))
            act.activation(M.w_hi[:, n % RING, :], M.w_raw[:, n % RING, :], ACT.Copy).then_inc(w_hi_done, 1)

        act.wait_ge(silu_ld, 16)
        act.activation(M.csig[:, :], M.cvec[:, :], ACT.Sigmoid).then_inc(csig_ok, 1)
        act.wait_ge(x_ld, 32)
        for k in range(KD):
            if k >= 2:
                act.wait_ge(sq_sum, k)
            act.activation(M.sq[:, k % 2, :], M.xin[:, k, :], ACT.Square).then_inc(sq_ok, 1)
        def mod_rows(half):
            act.wait_ge(ada1_used, 16 * (half + 1))
            act.activation(M.mrow[0:2, 2048 * half:2048 * (half + 1)], psf[0:2, 2048 * half:2048 * (half + 1)],
                           ACT.Copy).then_inc(rows_ok, 1)

        mod_rows(0)
        act.wait_ge(ss_ok, 1)
        act.wait_ge(dve0, 1)
        act.activation(M.sqr[:, 0:T], ps[:, 1, :], ACT.Sqrt, bias=M.eps[:, 0:1], scale=1.0 / D)
        act.activation(M.sqr[:, T:TC], ps[:, 2, 0:C], ACT.Sqrt, bias=M.eps[:, 0:1], scale=1.0 / D).then_inc(rt_ok, 1)
        mod_rows(1)
        for n in range(RING):
            w_hi(n)
        act.wait_ge(dve0, 6)
        for k in range(KD):
            if k == 0:
                act.wait_ge(rs_ok, 1 + KD)
            act.activation(M.h_hi[:, k, 0:T], M.xin[:, k, 0:T], ACT.Identity,
                           bias=M.mod1[:, k, 0:1], scale=M.scale1[:, k, 0:1])
            act.activation(M.h_hi[:, k, T:TC], M.xin[:, k, T:TC], ACT.Identity,
                           bias=M.mod1[:, k, 1:2], scale=M.scale1[:, k, 1:2]).then_inc(h_hi_ok, 1)
        with act.Fori(0, 5) as g:
            for s in range(8):
                w_hi(N_BOTH + RING + s, g, 8)
        for j in range(2):
            w_hi(N_BOTH + 40 + RING + j)
        with act.Fori(0, 11) as g:
            for s in range(8):
                w_hi(N_LAT + RING + s, g, 8)
        def square3(i):
            src, w = (M.ckv[:, i, :], TC) if i < 4 else (M.cq[:, i - 4, :], T)
            if i >= 2:
                act.wait_ge(pre_used, i - 1)
            act.activation(M.sq3[:, i % 2, 0:w], src, ACT.Square).then_inc(pre_sq, 1)

        for j in range(4):
            w_hi(N_LAT + 88 + RING + j)
            if j == 1:
                act.wait_ge(ckv_ld, 32)
                square3(0)
                square3(1)

        square3(2)
        square3(3)
        act.wait_ge(pre_used, 4)
        act.activation(M.sqr3[:, 0:T], ps[:, 0, :], ACT.Sqrt, bias=M.eps[:, 0:1], scale=1.0 / 512)
        act.activation(M.sqr3[:, T:TC], ps[:, 1, 0:C], ACT.Sqrt, bias=M.eps[:, 0:1], scale=1.0 / 512
                       ).then_inc(rt_ok, 1)
        for i in range(4):
            act.wait_ge(pre_n, i + 1)
            act.activation(M.ckv_hi[:, i, :], M.ckv[:, i, :], ACT.Copy).then_inc(pre_hi, 1)
        act.wait_ge(pre_ld, 64)
        square3(4)
        square3(5)
        square3(6)
        w_hi(N_KN + RING)
        square3(7)
        square3(8)
        w_hi(N_KN + RING + 1)
        square3(9)
        w_hi(N_KN + RING + 2)
        act.wait_ge(pre_used, 10)
        act.wait_ge(rs_ok, 17 + 1)
        act.activation(M.sqr3[:, 0:T], ps[:, 2, :], ACT.Sqrt, bias=M.eps[:, 0:1], scale=1.0 / 768).then_inc(rt_ok, 1)
        w_hi(N_KN + RING + 3)
        for i in range(6):
            act.wait_ge(pre_n, 4 + i + 1)
            act.activation(M.cq_hi[:, i, :], M.cq[:, i, :], ACT.Copy).then_inc(pre_hi, 1)
        for n in range(4, 8):
            w_hi(N_KN + RING + n)
        with act.Fori(0, 3) as g:
            for s in range(4):
                w_hi(N_QB + RING + s, g, 4)

        def na_prep(b, slot, g=None):
            act.wait_ge(na_ld, v(48 * (b + 1), g, 96))
            if g is not None or b:
                act.wait_ge(na_pv, v(8 * b, g, 16))
            else:
                act.wait_ge(na_zero, 1)
            for p in range(2):
                z = slice(64 * p, 64 * p + 64)
                act.activation(M.qz_hi[z, 2 * slot + p, :], M.na_q[z, :], ACT.Copy, scale=NA_SCALE)
            act.activation(M.k_hi[:, slot, :], M.na_k[:, :], ACT.Copy).then_inc(na_qkhi, 1)

        def na_vals(b, slot, part, g=None):
            n = 4 if part < 2 else 1
            act.wait_ge(na_vt, v(3 * b + part + 1, g, 6))
            if g is not None or b:
                act.wait_ge(na_pv, v(8 * b, g, 16))
            act.activation(M.v_hi[:, slot, 4 * part:4 * part + n, :],
                           ps[:, 6 + part % 2, 0:n * P].rearrange("p (c n) -> p c n", n=P), ACT.Copy).then_inc(na_vhi, 1)

        def na_exp_(u, g=None):
            act.wait_ge(na_max, v(u + 1 + 4, g, 16))
            act.activation(M.na_p[:, u % 4, :], ps[:, u % 2, :], ACT.Exp, bias=M.nmax[:, u % 4:u % 4 + 1],
                           accum_out=M.rsum[:, u % 4:u % 4 + 1]).then_inc(na_exp, 1)

        def na_out(h, g=None):
            z = slice(64 * (h % 2), 64 * (h % 2) + 64)
            act.wait_ge(na_pv, v(4 * h + 4 + 8, g, 16))
            dst = M.oa_hi[z, h // 2, :] if g is None else M.oa_hi[z, bass.ds(g * 2 + h // 2, 1), :].rearrange("p a n -> p (a n)")
            act.activation(dst, ps[z, 4 + h % 2, :], ACT.Copy).then_inc(na_ohi, 1)

        def na_pair(s, g=None, last=False, base=0):
            for u in range(8):
                uu = base + 8 * s + u
                b = uu // 8
                act.wait_ge(na_t, v(uu + 1, g, 16))
                act.wait_ge(na_pv, v(uu + 7, g, 16))
                act.activation(M.pt_hi[:, u % 2, :], ps[:, 2 + u % 2, :], ACT.Copy).then_inc(na_pthi, 1)
                if not (last and u >= 6):
                    na_exp_(uu + 2, g)
                if not last:
                    if u == 1:
                        na_prep(b + 1, (s + 1) % 2, g)
                    if u in (3, 5, 7):
                        na_vals(b + 1, (s + 1) % 2, (u - 3) // 2, g)
                if u == 5:
                    na_out(2 * b, g)
            na_out(2 * b + 1, g)

        na_prep(0, 0)
        for i in range(2):
            act.wait_ge(pre_st[i], 16 * 23)
        for part in range(3):
            na_vals(0, 0, part)
        na_exp_(0)
        na_exp_(1)
        with act.Fori(0, 3) as g:
            for s in range(2):
                na_pair(s, g)
        na_pair(0, base=48)
        na_pair(1, base=48, last=True)

        def ml_prep(h, part, g=None):
            s, z = h % 2, slice(64 * (h % 2), 64 * (h % 2) + 64)
            if part == 0:
                act.wait_ge(ml_ld, v(64 * (h + 1), g, 128))
                if g is not None or h:
                    act.wait_ge(ml_pv, v(h, g, 2))
                act.activation(M.mq_hi[:, s, :], M.ml_q[:, :], ACT.Copy)
                act.activation(M.mqp_hi[z, s, :], M.ml_qp[z, :], ACT.Copy).then_inc(ml_hi, 1)
            elif part == 1:
                act.activation(M.mk_hi[:, s, :], M.ml_k[:, :], ACT.Copy).then_inc(ml_hi, 1)
            else:
                act.activation(M.mv_hi[:, s, :, :], M.ml_v[:, :, :], ACT.Copy).then_inc(ml_hi, 1)

        def ml_exp_(u, g=None):
            act.wait_ge(ml_max, v(u + 1, g, 8))
            b = 1024 * (u % 2)
            act.activation(M.ml_p[:, u % 4, :], psf[:, b:b + TC], ACT.Exp, bias=M.nmax[:, u % 4:u % 4 + 1],
                           scale=MLA_SCALE, accum_out=M.rsum[:, u % 4:u % 4 + 1]).then_inc(na_exp, 1)

        def ml_out(h, g=None):
            s = h % 2
            act.wait_ge(ml_pv, v(h + 2, g, 2))
            dst = M.ob_hi[:, h, :] if g is None else M.ob_hi[:, bass.ds(g * 2 + h, 1), :].rearrange("p a n -> p (a n)")
            act.activation(dst, ps[:, 6 + s, :], ACT.Copy).then_inc(ml_ohi, 1)

        def ml_head(h, g=None, last=False):
            for q in range(4):
                u = 4 * h + q
                act.wait_ge(na_t, v(NA_UNITS + u + 1, g, 8))
                if q == 0:
                    act.wait_ge(ml_pv, v(h + 1, g, 2))
                act.activation(M.mpt_hi[:, :, P * q:P * (q + 1)],
                               psf[:, 2048:2048 + TC].rearrange("p (c n) -> p c n", n=P), ACT.Copy).then_inc(na_pthi, 1)
                if not (last and q >= 2):
                    ml_exp_(u + 2, g)
                if q < 2 and not last:
                    for part in ((0,), (1, 2))[q]:
                        ml_prep(h + 1, part, g)
                if q == 0 and h:
                    ml_out(h - 1, g)

        act.wait_ge(ml_kpld, 16)
        act.activation(M.kp_hi[:, :], M.ml_kp[:, :], ACT.Copy).then_inc(ml_kphi, 1)
        act.wait_ge(ml_zero, 1)
        for part in range(3):
            ml_prep(0, part)
        ml_exp_(0)
        ml_exp_(1)
        ml_head(0)
        with act.Fori(0, 3) as g:
            ml_head(1, g)
            ml_head(2, g)
        ml_head(7, last=True)
        ml_out(7)

        with act.Fori(0, 8) as g:
            for n in range(2):
                act.wait_ge(mg_ld[n], v(32, g, 32))
                act.activation(M.sg[:, n, :, :], M.sg[:, n, :, :], ACT.Sigmoid).then_inc(mg_sig, 1)
                w_hi(N_MERGE + 2 * n + RING, g, 4)
                w_hi(N_MERGE + 2 * n + 1 + RING, g, 4)
                act.wait_ge(mg_y, v(n + 1 + 2, g, 2))
                act.activation(M.y_hi[:, bass.ds(g * 2 + n, 1), :].rearrange("p a n -> p (a n)"), M.yb[:, n, :],
                               ACT.Copy).then_inc(mg_yhi, 1)
        with act.Fori(0, 8) as g:
            for n in range(2):
                w_hi(N_OUT + 2 * n + RING, g, 4)
                w_hi(N_OUT + 2 * n + 1 + RING, g, 4)
                act.wait_ge(unit_done, v(N_OUT + 2 * n + 2, g, 4))
                act.wait_ge(z_add, v(n + 1, g, 2))
                act.activation(M.zsq[:, n, :], ps[:, 4 + n, :], ACT.Square).then_inc(z_sq, 1)
        act.wait_ge(ss_ok, 1 + 1)
        act.activation(M.sqr2[:, :], ps[:, 6, :], ACT.Sqrt, bias=M.eps[:, 0:1], scale=1.0 / D).then_inc(rt_ok, 1)
        for k in range(KD):
            act.wait_ge(x1_ok, k + 1)
            if k >= 2:
                act.wait_ge(z_add, KD + 2 + k - 1)
            act.activation(M.zsq[:, k % 2, :], M.x1[:, k, :], ACT.Square).then_inc(z_sq, 1)
        act.wait_ge(ss_ok, 2 + 1)
        act.activation(M.sqr2[:, :], ps[:, 7, :], ACT.Sqrt, bias=M.eps[:, 0:1], scale=1.0 / D).then_inc(rt_ok, 1)

        act.wait_ge(x1_st, 64)
        for k in range(KD):
            act.wait_ge(zn if k % 2 else zn_even, KD // 2 + k // 2 + 1)
            act.activation(M.x1[:, k, :], M.z[:, k, :], ACT.Identity, bias=M.mod2[:, KD + k:KD + k + 1],
                           scale=M.scale2[:, k:k + 1])
            act.activation(M.h2_hi[:, k, :], M.z[:, k, :], ACT.Identity, bias=M.mod2[:, KD + k:KD + k + 1],
                           scale=M.scale2[:, k:k + 1]).then_inc(h2_hi_ok, 1)
        act.wait_ge(sk_ld, 16)
        act.activation(M.sk_hi[:, :, :], M.sk_raw[:, :, :], ACT.Copy).then_inc(sk_h, 1)
        def choice_exp(h, g=None):
            act.wait_ge(te_ok, v(h + 1, g, 1))
            act.activation(M.tex[:, :, :], M.te[:, :, :], ACT.Exp).then_inc(tex_ok, 1)

        def choice_head(g=None, first=False):
            for p in range(2):
                w_hi(N_QUERY + 2 * p + RING, g, 4)
                w_hi(N_QUERY + 2 * p + 1 + RING, g, 4)
                act.wait_ge(unit_done, v(N_QUERY + 2 * p + 2, g, 4))
                act.wait_ge(s_mm, v(p + 1, g, 2))
                act.activation(M.q_hi[:, p, :], ps[:, p, :], ACT.Copy).then_inc(q_h, 1)
            if not first:
                choice_exp(-1, g)
            for p in range(2):
                act.wait_ge(s_mm, v(p + 1 + 2, g, 2))
                if not first:
                    act.wait_ge(tk, v(CHOICE_SCORES - CHOICE_STEPS, g, CHOICE_STEPS))
                act.activation(M.sc[:, p, :, :], ps[:, 2 + p, :].rearrange("p (t n) -> p t n", n=P), ACT.Copy
                               ).then_inc(sc_cp, 1)

        choice_head(first=True)
        with act.Fori(1, 8) as g:
            choice_head(g)
        def exp_gelu(b, n, g=None):
            for j in range(2):
                w_hi(n + j + RING, g, 32)
            act.wait_ge(unit_done, v(n + 2, g, 32))
            act.wait_ge(m_w, v(b + 1, g, 8))
            act.activation(M.eact[:, b % 4, :], ps[:, b % 2, :], ACT.Gelu).then_inc(m_gelu, 1)

        for b in range(4):
            exp_gelu(b, N_MAIN + 2 * b)
            if b == 1:
                choice_exp(7)
        for x in range(3):
            act.wait_ge(sel_t, x + 1)
            act.activation(M.selT[:, x, :], ps[:, x, :], ACT.Copy).then_inc(selT_ok, 1)
        with act.Fori(0, T // TCH // 2) as g:
            for s in range(2):
                act.wait_ge(g_st[s], v(16, g, 16))
                with act.Fori(0, TCH // 16) as j:
                    for i in range(4):
                        act.wait_ge(g_mm, g * (TCH // 4) + j * 2 + (TCH // 8 * s + i // 2 + 1 + 4))
                        dst = M.gst[:, s, :, :].rearrange("p e t -> p t e")
                        act.activation(dst[:, bass.ds(j * 16 + 4 * i, 4), :],
                                       ps[:, i, :].rearrange("p (t e) -> p t e", e=P), ACT.Copy).then_inc(g_ev, 1)

        def exp_hi(b, g=None):
            act.wait_ge(m_w, v(b + 1 + 4, g, 8))
            act.activation(M.ew_hi[:, b % 8, :], M.ew[:, b % 2, :], ACT.Copy).then_inc(m_hi, 1)

        def exp_block(b, n, g=None):
            exp_gelu(b, n, g)
            exp_hi(b, g)

        def out_units(n, g=None, count=8):
            for j in range(count):
                w_hi(n + j + RING, g, 32)

        for s in range(2):
            act.wait_ge(g_st[s], 16 * (T // TCH // 2 + 1))
        for b in range(4):
            exp_hi(b)
        with act.Fori(0, GROUPS // 2 - 1) as g:
            for r in range(2):
                for q in range(4):
                    exp_block(4 + 4 * r + q, N_MAIN + 8 + 16 * r + 2 * q, g)
                out_units(N_MAIN + 16 + 16 * r, g)
        for q in range(4):
            exp_block(4 * GROUPS - 4 + q, N_END - 24 + 2 * q)
        out_units(N_END - 16)
        for k in range(KD):
            if k % 2 == 0 and k < 8:
                w_hi(N_END - 4 + k // 2)
            act.wait_ge(m_acc, 16 * GROUPS + k + 1)
            if k >= 2:
                act.wait_ge(z_add, 2 * KD + 1 + k)
            act.activation(M.fsq[:, k % 2, :], M.acc[:, k, :], ACT.Square).then_inc(z_sq, 1)
        act.wait_ge(ss_ok, 3 + 1)
        act.activation(M.fsqr[:, :], ps[:, 6, :], ACT.Sqrt, bias=M.eps[:, 0:1], scale=1.0 / D).then_inc(rt_ok, 1)

    @block.gpsimd
    def _(pool):
        def w_lo(n, g=None, per=0):
            pool.wait_ge(w_hi_done, v(n + 1, g, per))
            pool.tensor_tensor(M.w_lo[:, n % RING, :], M.w_raw[:, n % RING, :],
                               M.w_hi[:, n % RING, :].bitcast(F32), ALU.subtract).then_inc(w_lo_done, 1)

        for n in range(RING):
            w_lo(n)
        pool.wait_ge(ada1_used, 32)
        pool.memset(M.ada_sum[:, :], 0.0).then_inc(ada_zero, 1)
        with pool.Fori(0, (N_KN - 2) // 4) as g:
            for s in range(4):
                w_lo(RING + s, g, 4)
        for n in range(RING + N_KN - 2, RING + N_KN):
            w_lo(n)

        pool.wait_ge(unit_done, N_KN)
        pool.wait_ge(mod2_ps, 1)
        pool.memset(M.bpre[:, :], 0.0).then_inc(bpre_z, 1)
        for n in range(N_KN + RING, N_QB + RING):
            w_lo(n)
        with pool.Fori(0, 3) as g:
            for s in range(4):
                w_lo(N_QB + RING + s, g, 4)

        pool.wait_ge(kp_st, 16)
        pool.memset(M.qz_hi[:, :, :].bitcast(F32), 0.0)
        pool.memset(M.qz_lo[:, :, :].bitcast(F32), 0.0).then_inc(na_zero, 1)
        pool.wait_ge(mask_ld, 16)

        def na_mask(u, g=None):
            pool.wait_ge(bm_ld[u % 4], v(16 * (u // 4 + 1), g, 64))
            pool.tensor_tensor(M.bm[:, u % 4, :], M.bm[:, u % 4, :], M.mask[:, u % 4, :], ALU.add).then_inc(bm_ok, 1)

        def na_norm(u, g=None):
            pool.wait_ge(na_rinv, v(u + 1, g, 16))
            pool.tensor_tensor(M.na_p[:, u % 4, :], M.na_p[:, u % 4, :],
                               M.rinv[:, u % 4:u % 4 + 1].to_broadcast([P, T]), ALU.mult).then_inc(na_p, 1)

        for u in range(3):
            na_mask(u)
        na_norm(0)
        with pool.Fori(0, 3) as g:
            for u in range(16):
                na_norm(u + 1, g)
                na_mask(u + 3, g)
        for u in range(48, 64):
            if u + 1 < 64:
                na_norm(u + 1)
            if u + 3 < 64:
                na_mask(u + 3)

        pool.wait_ge(na_o, 16 + 2)
        pool.memset(M.mqp_hi[:, :, :].bitcast(F32), 0.0)
        pool.memset(M.mqp_lo[:, :, :].bitcast(F32), 0.0).then_inc(ml_zero, 1)

        def ml_norm(u, g=None):
            pool.wait_ge(na_rinv, v(NA_UNITS + u + 1, g, 8))
            pool.tensor_tensor(M.ml_p[:, u % 4, :], M.ml_p[:, u % 4, :],
                               M.rinv[:, u % 4:u % 4 + 1].to_broadcast([P, TC]), ALU.mult).then_inc(na_p, 1)

        ml_norm(0)
        with pool.Fori(0, 3) as g:
            for u in range(8):
                ml_norm(u + 1, g)
        for u in range(25, 32):
            ml_norm(u)

        with pool.Fori(0, 16) as g:
            for s in range(4):
                w_lo(N_MERGE + RING + s, g, 4)
        pool.wait_ge(rs_ok, 19 + 1)
        for k in range(1, KD, 2):
            pool.tensor_tensor(M.z[:, k, :], M.z[:, k, :], M.rs2[:, :], ALU.mult).then_inc(zn, 1)

        pool.wait_ge(rs_ok, 20 + 1)
        for k in range(1, KD, 2):
            pool.tensor_tensor(M.z[:, k, :], M.x1[:, k, :], M.rs2[:, :], ALU.mult).then_inc(zn, 1)
        def keys_of_matches(h, g=None):
            for x in range(2):
                if x == 0:
                    pool.wait_ge(tk, v(h * CHOICE_STEPS + CHOICE_MATCHES, g, CHOICE_STEPS))
                pool.tensor_tensor(M.eqc[:, x, :, :, :], M.eqb[:, x, :, :, :],
                                   M.topif[:, x, :, :].unsqueeze(2).to_broadcast([P, 4, 16, 16]), ALU.mult
                                   ).then_inc(eqc_ok, 1)

        for s in range(4):
            w_lo(N_QUERY + RING + s)
        with pool.Fori(1, 8) as g:
            for s in range(4):
                w_lo(N_QUERY + RING + s, g, 4)
            keys_of_matches(-1, g)
        for s in range(4):
            w_lo(N_MAIN + RING + s)
        keys_of_matches(7)
        for s in range(4, 8):
            w_lo(N_MAIN + RING + s)
        pool.wait_ge(selT_ok, 3)
        with pool.Fori(0, T // 32) as g:
            for s in range(4):
                pool.wait_ge(oh_eq, v(s + 1, g, 4))
                pool.tensor_tensor(M.oh2[:, s, :, :], M.oh2[:, s, :, :],
                                   M.selT[:, 2, bass.ds(g * 32 + 8 * s, 8)].unsqueeze(2).to_broadcast([P, 8, P]),
                                   ALU.mult).then_inc(oh2_ok, 1)

        for s in range(2):
            pool.wait_ge(g_st[s], 16 * (T // TCH // 2 + 1))
        pool.wait_ge(g_mm, T // 8 + 4)
        pool.wait_ge(oh1_ok, T // 8)
        pool.memset(M.acc[:, :, :], 0.0).then_inc(acc_zero, 1)
        with pool.Fori(1, (N_END - N_MAIN - RING - 4) // 8) as g:
            for s in range(8):
                w_lo(N_MAIN + RING + s, g, 8)
        for n in range(N_END - 4, N_END):
            w_lo(n)
        pool.wait_ge(rs_ok, 21 + 1)
        for k in range(1, KD, 2):
            pool.tensor_tensor(M.acc[:, k, :], M.acc[:, k, :], M.frs[:, :], ALU.mult).then_inc(zn, 1)

    @block.vector
    def _(dve):
        dve.sem_inc(ada2_used, 4)
        dve.sem_inc(p2_ev, 2)
        for s in range(2):
            dve.sem_inc(p2_st[s], 16)
        for s_, n in ((pre_st[0], 16), (pre_st[1], 16), (pre_ev, 2), (na_s, 8), (na_max, 4), (na_pt, 2), (na_pv, 8),
                      (na_o, 2), (ml_pt, 1), (ml_o, 2), (ml_pv, 1), (mg_y, 2), (z_add, 2),
                      (q_l, 2), (sc_cp, 2), (s_mm, 2), (g_ev, 4), (g_mm, 4), (g_st[0], 16),
                      (g_st[1], 16), (m_gelu, 2), (m_w, 4), (m_acc, 16)):
            dve.sem_inc(s_, n)
        dve.memset(M.eps[:, :], EPS).then_inc(dve0, 1)
        dve.wait_ge(csig_ok, 1)
        dve.tensor_tensor(M.csilu[:, :], M.cvec[:, :], M.csig[:, :], ALU.mult).then_inc(csilu_ok, 1)
        dve.wait_ge(csilu_ok, 1)
        dve.tensor_copy(M.c1[:, :], M.csilu[:, :].rearrange("p (k c) -> p k c", c=2)[:, :, 0]).then_inc(dve0, 1)
        dve.memset(M.xsum[:, :], 0.0).then_inc(sq_sum, 1)
        for k in range(KD):
            dve.wait_ge(sq_ok, k + 1)
            dve.wait_ge(sq_sum, k + 1)
            dve.tensor_tensor(M.xsum[:, :], M.xsum[:, :], M.sq[:, k % 2, :], ALU.add).then_inc(sq_sum, 1)
        dve.wait_ge(rt_ok, 1)
        dve.reciprocal(M.rs[:, :], M.sqr[:, :]).then_inc(rs_ok, 1)
        dve.wait_ge(rs_ok, 1)
        for k in range(KD):
            dve.tensor_tensor(M.xin[:, k, :], M.xin[:, k, :], M.rs[:, :], ALU.mult).then_inc(rs_ok, 1)
        dve.wait_ge(cols_ok, 2)
        dve.wait_ge(consts_ld, 64)
        for c in range(2):
            dve.tensor_tensor(M.mod1[:, :, c], ps[:, 0, 0:64].rearrange("p (n c) -> p n c", c=2)[:, :, c],
                              M.vecs[:, VEC_B:VEC_B + 32], ALU.add).then_inc(dve0, 1)
        dve.wait_ge(dve0, 4)
        for c in range(2):
            dve.scalar_tensor_tensor(M.scale1[:, :, c], M.mod1[:, KD:2 * KD, c], 1.0,
                                     M.vecs[:, VEC_PRE:VEC_PRE + KD], ALU.add, ALU.mult).then_inc(dve0, 1)
        dve.wait_ge(dve0, 6)
        dve.wait_ge(rs_ok, 1 + KD)
        for k in range(KD):
            dve.wait_ge(h_hi_ok, k + 1)
            for c, (t0, t1) in enumerate(((0, T), (T, TC))):
                dve.tensor_scalar(M.xin[:, k, t0:t1], M.xin[:, k, t0:t1], M.scale1[:, k, c:c + 1],
                                  M.mod1[:, k, c:c + 1], ALU.mult, ALU.add).then_inc(h_raw, 1)
            dve.wait_ge(h_raw, 2 * k + 2)
            dve.tensor_tensor(M.h_lo[:, k, :], M.xin[:, k, :], M.h_hi[:, k, :].bitcast(F32),
                              ALU.subtract).then_inc(h_ok, 1)

        def p2_block(bg, ctx, g=None, ada=None):
            dve.wait_ge(unit_done, v(2 * bg + 2, g, 8))
            dve.wait_ge(p2_st[bg % 2], v(16 * (bg // 2 + 1), g, 32))
            if ctx:
                dve.tensor_copy(M.stage[:, bg % 2, T:TC], ps[:, 2 + bg % 2, 0:C])
            dve.tensor_copy(M.stage[:, bg % 2, 0:T], ps[:, bg % 2, :]).then_inc(p2_ev, 1)
            if ada is not None:
                kk, q = ada // 4, ada % 4
                part = M.ada_sum[:, q * 2048:(q + 1) * 2048]
                dve.wait_ge(ada2_ld[ada % 2], v(16 * (ada // 2 + 1), g, 32))
                dve.wait_ge(ada2_used, v(ada + 1, g, 4))
                sc = M.c1[:, bass.ds(g + kk, 1)]
                dve.scalar_tensor_tensor(part, M.ada_raw[:, ada % 2, :], sc, part, ALU.mult, ALU.add
                                         ).then_inc(ada2_used, 1)

        dve.wait_ge(ada_zero, 1)
        with dve.Fori(0, 5) as g:
            for s in range(4):
                p2_block(s, True, g, ada=s)
        p2_block(20, True)
        with dve.Fori(0, 11) as g:
            for s in range(4):
                p2_block(21 + s, False, g, ada=20 + s)
        for b in (44, 45):
            p2_block(21 + b, False)

        dve.wait_ge(rt_ok, 1 + 1)
        dve.reciprocal(M.rs3[:, :], M.sqr3[:, :]).then_inc(rs_ok, 1)
        dve.wait_ge(rs_ok, 17 + 1)

        def norm3(i):
            x, w, gg = (M.ckv[:, i, :], TC, VEC_GKV + i) if i < 4 else (M.cq[:, i - 4, :], T, VEC_GQ + i - 4)
            dve.scalar_tensor_tensor(x, x, M.vecs[:, gg:gg + 1], M.rs3[:, 0:w], ALU.mult, ALU.mult).then_inc(pre_n, 1)

        def lo3(i):
            x, hi, lo = ((M.ckv, M.ckv_hi, M.ckv_lo) if i < 4 else (M.cq, M.cq_hi, M.cq_lo))
            k = i if i < 4 else i - 4
            dve.wait_ge(pre_hi, i + 1)
            dve.tensor_tensor(lo[:, k, :], x[:, k, :], hi[:, k, :].bitcast(F32), ALU.subtract).then_inc(pre_ok, 1)

        for i in range(4):
            norm3(i)
        for i in range(4):
            lo3(i)
        dve.wait_ge(mod2_ps, 1)
        dve.tensor_tensor(M.mod2[:, :], ps[:, 7, 0:64], M.vecs[:, VEC_B + 32:VEC_B + 96], ALU.add).then_inc(mod2_ok, 1)
        dve.wait_ge(mod2_ok, 1)
        dve.tensor_tensor(M.gate1[:, :], M.mod2[:, 0:KD], M.vecs[:, VEC_POST:VEC_POST + KD], ALU.mult)
        dve.scalar_tensor_tensor(M.scale2[:, :], M.mod2[:, 2 * KD:3 * KD], 1.0, M.vecs[:, VEC_PREF:VEC_PREF + KD],
                                 ALU.add, ALU.mult)
        dve.tensor_tensor(M.gate2[:, :], M.mod2[:, 3 * KD:4 * KD], M.vecs[:, VEC_POSTF:VEC_POSTF + KD],
                          ALU.mult).then_inc(mod2_ok, 1)

        def rope(x, rot, tmp, step, at, done):
            dve.tensor_tensor(tmp, rot, M.sin[:, :], ALU.mult).then_inc(step, 1)
            dve.tensor_tensor(x, x, M.cos[:, :], ALU.mult).then_inc(step, 1)
            dve.wait_ge(step, at + 2)
            dve.tensor_tensor(x, x, tmp, ALU.add).then_inc(done, 1)

        dve.wait_ge(kp_rot, 1)
        dve.wait_ge(pre_ld, 64)
        rope(M.kpe[:, 0:T], ps[:, 3, :], M.rope_t[:, :], rope_step, 0, kp_ok)

        def pre_evac(e, done, w=T, ctx=False, g=None, per=0, inc=pre_ev):
            dve.wait_ge(done[0], done[1])
            dve.wait_ge(pre_st[e % 2], v(16 * (e // 2 + 1), g, 16 * (per // 2)))
            if ctx:
                dve.tensor_copy(M.mst[:, e % 2, T:TC], ps[:, 6 + e % 2, 0:C])
            dve.tensor_copy(M.mst[:, e % 2, 0:w], ps[:, 4 + e % 2, 0:w]).then_inc(inc, 1)

        for b in range(8):
            pre_evac(b, (unit_done, N_KN + b // 2 + 1) if b % 2 else (kn_mm, b // 2 + 1), ctx=True)
        dve.wait_ge(rt_ok, 1 + 2)
        dve.wait_ge(pre_n, 4)
        dve.reciprocal(M.rs3[:, 0:T], M.sqr3[:, 0:T]).then_inc(rs_ok, 1)
        for t in range(24):
            if 1 <= t < 7:
                dve.wait_ge(rs_ok, 17 + 2)
                norm3(3 + t)
            if 7 <= t < 13:
                lo3(t - 3)
            pre_evac(8 + t, (unit_done, N_V + t // 6 + 1) if t % 6 == 5 else (kn_mm, 4 + t // 6 * 5 + t % 6 + 1), w=256)
        with dve.Fori(0, 2) as g:
            for s in range(4):
                pre_evac(32 + s, (unit_done, v(N_QB + s + 1, g, 4)), g=g, per=4)
        for s in range(4):
            e = 40 + s
            pre_evac(e, (unit_done, N_QB + 8 + s + 1), inc=rope_raw)
            dve.wait_ge(rope_rot, s + 1)
            rope(M.mst[:, e % 2, 0:T], ps[:, 2 + s % 2, :], M.rope_t[:, :], rope_step, 2 + 2 * s, pre_ev)

        def na_prep(b, slot, g=None):
            dve.wait_ge(na_qkhi, v(b + 1, g, 2))
            for p in range(2):
                z = slice(64 * p, 64 * p + 64)
                dve.scalar_tensor_tensor(M.qz_lo[z, 2 * slot + p, :], M.na_q[z, :], NA_SCALE,
                                         M.qz_hi[z, 2 * slot + p, :].bitcast(F32), ALU.mult, ALU.subtract)
            dve.tensor_tensor(M.k_lo[:, slot, :], M.na_k[:, :], M.k_hi[:, slot, :].bitcast(F32),
                              ALU.subtract).then_inc(na_split, 1)

        def na_vals(b, slot, part, g=None):
            n = 4 if part < 2 else 1
            dve.wait_ge(na_vhi, v(3 * b + part + 1, g, 6))
            dve.tensor_tensor(M.v_lo[:, slot, 4 * part:4 * part + n, :],
                              ps[:, 6 + part % 2, 0:n * P].rearrange("p (c n) -> p c n", n=P),
                              M.v_hi[:, slot, 4 * part:4 * part + n, :].bitcast(F32), ALU.subtract).then_inc(na_vlo, 1)

        def na_max_(u, g=None):
            dve.wait_ge(na_s, v(u + 1 + 8, g, 16))
            dve.wait_ge(bm_ok, v(u + 1, g, 16))
            dve.tensor_tensor(ps[:, u % 2, 0:256], ps[:, u % 2, 0:256], M.bm[:, u % 4, :], ALU.add).then_inc(na_add, 1)
            dve.wait_ge(na_add, v(u + 1, g, 16))
            dve.tensor_reduce(M.nmax[:, u % 4:u % 4 + 1], ps[:, u % 2, :], AX.X, ALU.max, negate=True).then_inc(na_max, 1)

        def na_rinv_(u, g=None):
            dve.wait_ge(na_exp, v(u + 1, g, 16))
            dve.reciprocal(M.rinv[:, u % 4:u % 4 + 1], M.rsum[:, u % 4:u % 4 + 1]).then_inc(na_rinv, 1)

        def na_out(h, g=None):
            z = slice(64 * (h % 2), 64 * (h % 2) + 64)
            dve.wait_ge(na_ohi, v(h + 1, g, 4))
            def at(x):
                return x[z, h // 2, :] if g is None else x[z, bass.ds(g * 2 + h // 2, 1), :].rearrange("p a n -> p (a n)")
            dve.tensor_tensor(at(M.oa_lo), ps[z, 4 + h % 2, :], at(M.oa_hi).bitcast(F32), ALU.subtract).then_inc(na_o, 1)

        def na_pair(s, g=None, last=False, base=0):
            for u in range(8):
                uu = base + 8 * s + u
                b = uu // 8
                if not (last and u == 7):
                    na_rinv_(uu + 1, g)
                if not (last and u >= 6):
                    na_max_(uu + 2, g)
                dve.wait_ge(na_pthi, v(uu + 1, g, 16))
                dve.tensor_tensor(M.pt_lo[:, u % 2, :], ps[:, 2 + u % 2, :], M.pt_hi[:, u % 2, :].bitcast(F32),
                                  ALU.subtract).then_inc(na_pt, 1)
                if not last:
                    if u == 1:
                        na_prep(b + 1, (s + 1) % 2, g)
                    if u in (3, 5, 7):
                        na_vals(b + 1, (s + 1) % 2, (u - 3) // 2, g)
                if u == 5:
                    na_out(2 * b, g)
            na_out(2 * b + 1, g)

        na_prep(0, 0)
        for part in range(3):
            na_vals(0, 0, part)
        na_max_(0)
        na_max_(1)
        na_rinv_(0)
        with dve.Fori(0, 3) as g:
            for s in range(2):
                na_pair(s, g)
        na_pair(0, base=48)
        na_pair(1, base=48, last=True)

        def ml_prep(h, part, g=None):
            s, z = h % 2, slice(64 * (h % 2), 64 * (h % 2) + 64)
            dve.wait_ge(ml_hi, v(3 * h + part + 1, g, 6))
            if part == 0:
                dve.tensor_tensor(M.mq_lo[:, s, :], M.ml_q[:, :], M.mq_hi[:, s, :].bitcast(F32), ALU.subtract)
                dve.tensor_tensor(M.mqp_lo[z, s, :], M.ml_qp[z, :], M.mqp_hi[z, s, :].bitcast(F32), ALU.subtract)
            elif part == 1:
                dve.tensor_tensor(M.mk_lo[:, s, :], M.ml_k[:, :], M.mk_hi[:, s, :].bitcast(F32), ALU.subtract)
            else:
                dve.tensor_tensor(M.mv_lo[:, s, :, :], M.ml_v[:, :, :], M.mv_hi[:, s, :, :].bitcast(F32),
                                  ALU.subtract).then_inc(ml_lo, 1)

        def ml_max_(u, g=None):
            dve.wait_ge(ml_s, v(u + 1, g, 8))
            b = 1024 * (u % 2)
            dve.tensor_reduce(M.nm0[:, u % 4:u % 4 + 1], psf[:, b:b + TC], AX.X, ALU.max, negate=True).then_inc(ml_m0, 1)
            dve.wait_ge(ml_m0, v(u + 1, g, 8))
            dve.tensor_scalar(M.nmax[:, u % 4:u % 4 + 1], M.nm0[:, u % 4:u % 4 + 1], MLA_SCALE, None,
                              ALU.mult).then_inc(ml_max, 1)

        def ml_rinv_(u, g=None):
            dve.wait_ge(na_exp, v(NA_UNITS + u + 1, g, 8))
            dve.reciprocal(M.rinv[:, u % 4:u % 4 + 1], M.rsum[:, u % 4:u % 4 + 1]).then_inc(na_rinv, 1)

        def ml_out(h, g=None):
            dve.wait_ge(ml_ohi, v(h + 1, g, 2))
            def at(x):
                return x[:, h, :] if g is None else x[:, bass.ds(g * 2 + h, 1), :].rearrange("p a n -> p (a n)")
            dve.tensor_tensor(at(M.ob_lo), ps[:, 6 + h % 2, :], at(M.ob_hi).bitcast(F32), ALU.subtract).then_inc(ml_o, 1)

        def ml_head(h, g=None, last=False):
            for q in range(4):
                u = 4 * h + q
                if not (last and q == 3):
                    ml_rinv_(u + 1, g)
                if not (last and q >= 2):
                    ml_max_(u + 2, g)
                dve.wait_ge(na_pthi, v(NA_UNITS + u + 1, g, 8))
                dve.tensor_tensor(M.mpt_lo[:, :, P * q:P * (q + 1)],
                                  psf[:, 2048:2048 + TC].rearrange("p (c n) -> p c n", n=P),
                                  M.mpt_hi[:, :, P * q:P * (q + 1)].bitcast(F32), ALU.subtract).then_inc(ml_pt, 1)
                if q < 2 and not last:
                    for part in ((0,), (1, 2))[q]:
                        ml_prep(h + 1, part, g)
                if q == 0 and h:
                    ml_out(h - 1, g)

        dve.wait_ge(ml_kphi, 1)
        dve.tensor_tensor(M.kp_lo[:, :], M.ml_kp[:, :], M.kp_hi[:, :].bitcast(F32), ALU.subtract).then_inc(ml_kplo, 1)
        dve.wait_ge(ml_zero, 1)
        for part in range(3):
            ml_prep(0, part)
        ml_max_(0)
        ml_max_(1)
        ml_rinv_(0)
        ml_head(0)
        with dve.Fori(0, 3) as g:
            ml_head(1, g)
            ml_head(2, g)
        ml_head(7, last=True)
        ml_out(7)

        with dve.Fori(0, 8) as g:
            for n in range(2):
                dve.wait_ge(unit_done, v(N_MERGE + 2 * n + 2, g, 4))
                dve.wait_ge(mg_sig, v(n + 1, g, 2))
                for i in range(2):
                    dve.tensor_tensor(M.sg[:, n, i, :], ps[:, 2 * n + i, :], M.sg[:, n, i, :], ALU.mult).then_inc(mg_part, 1)
                dve.wait_ge(mg_part, v(2 * n + 2, g, 4))
                dve.tensor_tensor(M.yb[:, n, :], M.sg[:, n, 0, :], M.sg[:, n, 1, :], ALU.add).then_inc(mg_y, 1)
                dve.wait_ge(mg_yhi, v(n + 1, g, 2))
                y = bass.ds(g * 2 + n, 1)
                dve.tensor_tensor(M.y_lo[:, y, :].rearrange("p a n -> p (a n)"), M.yb[:, n, :],
                                  M.y_hi[:, y, :].rearrange("p a n -> p (a n)").bitcast(F32),
                                  ALU.subtract).then_inc(mg_ylo, 1)
        dve.memset(M.ssum[:, :], 0.0).then_inc(z_cp, 1)
        with dve.Fori(0, 8) as g:
            for n in range(2):
                dve.wait_ge(z_sq, v(n + 1, g, 2))
                dve.tensor_copy(M.z[:, bass.ds(g * 2 + n, 1), :].rearrange("p a n -> p (a n)"), ps[:, 4 + n, :]
                                ).then_inc(z_cp, 1)
                dve.wait_ge(z_add, v(n + 2, g, 2))
                dve.wait_ge(z_cp, v(n + 2, g, 2))
                dve.tensor_tensor(M.ssum[:, :], M.ssum[:, :], M.zsq[:, n, :], ALU.add).then_inc(z_add, 1)
        dve.wait_ge(rt_ok, 3 + 1)
        dve.reciprocal(M.rs2[:, :], M.sqr2[:, :]).then_inc(rs_ok, 1)
        dve.wait_ge(x_ld, 32 + 16 * 8)
        dve.wait_ge(rs_ok, 19 + 1)

        def norm_even(k, out, x, rs):
            if k % 2 == 0 and k < KD:
                dve.tensor_tensor(out[:, k, :], x[:, k, :], rs, ALU.mult).then_inc(zn_even, 1)

        def normed(k, base):
            dve.wait_ge(zn if k % 2 else zn_even, base + k // 2 + 1)

        norm_even(0, M.z, M.z, M.rs2[:, :])
        for k in range(KD):
            norm_even(k + 2, M.z, M.z, M.rs2[:, :])
            normed(k, 0)
            dve.scalar_tensor_tensor(M.x1[:, k, :], M.z[:, k, :], M.gate1[:, k:k + 1], M.x1[:, k, :],
                                     ALU.mult, ALU.add).then_inc(x1_ok, 1)

        dve.wait_ge(rt_ok, 4 + 1)
        dve.reciprocal(M.rs2[:, :], M.sqr2[:, :]).then_inc(rs_ok, 1)
        dve.wait_ge(rs_ok, 20 + 1)
        norm_even(0, M.z, M.x1, M.rs2[:, :])
        norm_even(2, M.z, M.x1, M.rs2[:, :])
        for k in range(KD):
            norm_even(k + 4, M.z, M.x1, M.rs2[:, :])
            dve.wait_ge(h2_hi_ok, k + 1)
            dve.tensor_tensor(M.h2_lo[:, k, :], M.x1[:, k, :], M.h2_hi[:, k, :].bitcast(F32),
                              ALU.subtract).then_inc(h2_ok, 1)
        dve.wait_ge(sk_h, 1)
        dve.tensor_tensor(M.sk_lo[:, :, :], M.sk_raw[:, :, :], M.sk_hi[:, :, :].bitcast(F32), ALU.subtract).then_inc(sk_ok, 1)

        step = [0, None]

        def done(ins):
            ins.then_inc(tk, 1)
            step[0] += 1

        def after():
            h = step[1]
            if h is LAST:
                dve.wait_ge(tk, 7 * CHOICE_STEPS + step[0])
            else:
                dve.wait_ge(tk, v(step[0] - CHOICE_STEPS, h, CHOICE_STEPS))
                dve.sem_inc(waited_dve, 1)

        LAST = "last"

        def top16(vals, idx, src, tmp, tiles):
            for t in range(tiles):
                done(dve.max(vals[:, t, 0:8], src[:, t, :]))
            after()
            for t in range(tiles):
                done(dve.max_index(idx[:, t, 0:8], vals[:, t, 0:8], src[:, t, :]))
                done(dve.match_replace(tmp[:, t, :], vals[:, t, 0:8], src[:, t, :], -3.0e38))
            after()
            for t in range(tiles):
                done(dve.max(vals[:, t, 8:16], tmp[:, t, :]))
            after()
            for t in range(tiles):
                done(dve.max_index(idx[:, t, 8:16], vals[:, t, 8:16], tmp[:, t, :]))
            after()

        def choice_first(h):
            step[0], step[1] = 0, h
            dve.wait_ge(sc_cp, 14 + 2 + 2 if h is LAST else v(2, h, 2))
            dve.sem_inc(waited_dve, 1)
            halves = "p a t n -> p (a t) n"
            top16(M.topv[:, :, :, :].rearrange(halves), M.topi[:, :, :, :].rearrange(halves),
                  M.sc[:, :, :, :].rearrange(halves), M.cand2[:, :, :].rearrange("p t (a n) -> p (t a) n", n=P), 8)

        def choice_second(h):
            done(dve.tensor_copy(M.topif[:, :, :, :], M.topi[:, :, :, :]))
            done(dve.tensor_tensor(M.cand[:, :, :].rearrange("p t (a b) -> p t a b", b=16),
                                   M.topv[:, 0, :, :].unsqueeze(3).to_broadcast([P, 4, 16, 16]),
                                   M.topv[:, 1, :, :].unsqueeze(2).to_broadcast([P, 4, 16, 16]), ALU.add)); after()
            top16(M.tv[:, :, :], M.tpos[:, :, :], M.cand[:, :, :], M.cand2[:, :, :], 4)
            dve.tensor_tensor(M.te[:, :, :], M.tv[:, :, :], M.tv[:, :, 0:1].to_broadcast([P, 4, 16]),
                              ALU.subtract).then_inc(te_ok, 1)
            done(dve.tensor_scalar(M.tab[:, 0, :, :], M.tpos[:, :, :], 4, None, ALU.logical_shift_right))
            done(dve.tensor_scalar(M.tab[:, 1, :, :], M.tpos[:, :, :], 15, None, ALU.bitwise_and)); after()
            done(dve.tensor_copy(M.tabf[:, :, :, :], M.tab[:, :, :, :])); after()
            at = slice(7 * 16, 8 * 16) if h is LAST else bass.ds(h * 16 - 16, 16)
            for x in range(2):
                done(dve.tensor_tensor(M.eqb[:, x, :, :, :], M.tabf[:, x, :, :].unsqueeze(3).to_broadcast([P, 4, 16, 16]),
                                       M.iota[:, 0:16].unsqueeze(1).unsqueeze(1).to_broadcast([P, 4, 16, 16]),
                                       ALU.is_equal))
            assert step[0] == CHOICE_MATCHES
            dve.wait_ge(tex_ok, 8 if h is LAST else v(0, h, 1))
            done(dve.tensor_reduce(M.tsum[:, :], M.tex[:, :, :], AX.X, ALU.add)); after()
            done(dve.reciprocal(M.tinv[:, :], M.tsum[:, :])); after()
            done(dve.tensor_tensor(M.sel[:, 2, :, at], M.tex[:, :, :], M.tinv[:, :].unsqueeze(2).to_broadcast([P, 4, 16]),
                                   ALU.mult))
            for x in range(2):
                dve.wait_ge(eqc_ok, 14 + x + 1 if h is LAST else v(x - 1, h, 2))
                done(dve.tensor_reduce(M.sel[:, x, :, at], M.eqc[:, x, :, :, :], AX.X, ALU.add))
            assert step[0] == CHOICE_STEPS, step[0]

        def query_lo(p, g=None):
            dve.wait_ge(q_h, v(p + 1, g, 2))
            dve.tensor_tensor(M.q_lo[:, p, :], ps[:, p, :], M.q_hi[:, p, :].bitcast(F32), ALU.subtract).then_inc(q_l, 1)

        query_lo(0)
        query_lo(1)
        with dve.Fori(1, 8) as g:
            query_lo(0, g)
            choice_first(g)
            query_lo(1, g)
            choice_second(g)
        choice_first(LAST)
        choice_second(LAST)

        dve.wait_ge(selT_ok, 3)
        with dve.Fori(0, T // 32) as g:
            for s in range(4):
                dve.wait_ge(g_mm, v(s + 1, g, 4))
                for x, rows, ready in ((1, M.oh2, oh_eq), (0, M.oh1, oh1_ok)):
                    dve.tensor_tensor(rows[:, s, :, :], M.iota[:, :].unsqueeze(1).to_broadcast([P, 8, P]),
                                      M.selT[:, x, bass.ds(g * 32 + 8 * s, 8)].unsqueeze(2).to_broadcast([P, 8, P]),
                                      ALU.is_equal).then_inc(ready, 1)

        def exp_block(b, g=None):
            dve.wait_ge(m_gelu, v(b + 1 + 2, g, 8))
            dve.wait_ge(m_eg[b % 2], v(16 * (b // 2 + 1), g, 64))
            dve.tensor_tensor(M.ew[:, b % 2, :], M.eact[:, b % 4, :], M.eg[:, b % 2, :], ALU.mult).then_inc(m_w, 1)
            dve.wait_ge(m_hi, v(b + 1, g, 8))
            dve.tensor_tensor(M.ew_lo[:, b % 8, :], M.ew[:, b % 2, :], M.ew_hi[:, b % 8, :].bitcast(F32),
                              ALU.subtract).then_inc(m_lo, 1)

        def add_square(k):
            dve.wait_ge(z_sq, 2 * KD + k + 1)
            dve.wait_ge(z_add, 2 * KD + 1 + k + 1)
            dve.tensor_tensor(M.fsum[:, :], M.fsum[:, :], M.fsq[:, k % 2, :], ALU.add).then_inc(z_add, 1)

        def out_blocks(i, n, g=None, squares=False):
            for k in range(KD):
                if k % 2:
                    dve.wait_ge(unit_done, v(n + k // 2 + 1, g, 32))
                else:
                    dve.wait_ge(m_v, v((i + k) // 2 + 1, g, 16))
                dve.wait_ge(m_acc, v(i + k + 1, g, 32))
                dve.tensor_tensor(M.acc[:, k, :], M.acc[:, k, :], ps[:, 2 + k % 4, :], ALU.add).then_inc(m_acc, 1)
                if squares and k:
                    add_square(k - 1)
            if squares:
                add_square(KD - 1)

        dve.wait_ge(acc_zero, 1)
        for b in range(4):
            exp_block(b)
        with dve.Fori(0, GROUPS // 2 - 1) as g:
            for r in range(2):
                for q in range(4):
                    exp_block(4 + 4 * r + q, g)
                out_blocks(16 * r, N_MAIN + 16 + 16 * r, g)
        for q in range(4):
            exp_block(4 * GROUPS - 4 + q)
        out_blocks(16 * (GROUPS - 2), N_END - 16)
        dve.memset(M.fsum[:, :], 0.0).then_inc(z_add, 1)
        out_blocks(16 * (GROUPS - 1), N_END - 8, squares=True)
        dve.wait_ge(rt_ok, 5 + 1)
        dve.reciprocal(M.frs[:, :], M.fsqr[:, :]).then_inc(rs_ok, 1)
        dve.wait_ge(x_ld, 32 + 16 * 8 + 16)
        dve.wait_ge(rs_ok, 21 + 1)
        norm_even(0, M.acc, M.acc, M.frs[:, :])
        for k in range(KD):
            norm_even(k + 2, M.acc, M.acc, M.frs[:, :])
            normed(k, KD)
            dve.scalar_tensor_tensor(M.fx[:, k, :], M.acc[:, k, :], M.gate2[:, k:k + 1], M.fx[:, k, :],
                                     ALU.mult, ALU.add).then_inc(x1_ok, 1)

    @block.tensor
    def _(pe):
        def mm3(out, stat, mov, first, last):
            pe.matmul(out, stat[0], mov[0], start=first, stop=False)
            pe.matmul(out, stat[0], mov[1], start=False, stop=False)
            return pe.matmul(out, stat[1], mov[0], start=False, stop=last)

        def w_at(n, k, w=P):
            return M.w_hi[:, n % RING, k * w:(k + 1) * w], M.w_lo[:, n % RING, k * w:(k + 1) * w]

        def w_ready(n, g=None, per=0):
            pe.wait_ge(w_lo_done, v(n + 1, g, per))

        pe.wait_ge(csilu_ok, 1)

        for half in range(2):
            for k0 in range(4):
                for s in range(4):
                    k = 4 * k0 + s
                    pe.wait_ge(ada1_ld[s], 16 * (4 * half + k0 + 1))
                    for b in range(4):
                        last = pe.matmul(ps[0:2, 4 * half + b, :], M.csilu[:, 2 * k:2 * k + 2],
                                         M.ada1_raw[:, s, 512 * b:512 * (b + 1)], start=(k == 0), stop=(k == KD - 1))
                    last.then_inc(ada1_used, 1)
                if half == 1 and k0 == 1:
                    pe.wait_ge(rows_ok, 1)
                    pe.wait_ge(sq_sum, KD + 1)
                    pe.matmul(ps[:, 1, :], M.ones[:, :], M.xsum[:, 0:T], start=True, stop=True)
                    pe.matmul(ps[:, 2, 0:C], M.ones[:, :], M.xsum[:, T:TC], start=True, stop=True).then_inc(ss_ok, 1)
            if half == 0:
                pe.wait_ge(consts_ld, 64)
        for half in range(2):
            pe.wait_ge(rows_ok, half + 1)
            for n in range(KD):
                last = pe.matmul(ps[:, 0, 32 * half + 2 * n:32 * half + 2 * n + 2],
                                 M.mrow[0:2, (KD * half + n) * P:(KD * half + n + 1) * P], M.ident[0:2, 0:2],
                                 start=True, stop=True)
            last.then_inc(cols_ok, 1)


        def p2_block(bg, ctx, g=None):
            pe.wait_ge(p2_ev, v(bg + 1, g, 4))
            for u in range(2):
                w_ready(2 * bg + u, g, 8)
                for j in range(8):
                    k, w = 8 * u + j, w_at(2 * bg + u, j)
                    if bg == 0:
                        pe.wait_ge(h_ok, k + 1)
                    f, z = k == 0, k == KD - 1
                    last = mm3(ps[:, bg % 2, :], w, (M.h_hi[:, k, 0:T], M.h_lo[:, k, 0:T]), f, z)
                    if ctx:
                        last = mm3(ps[:, 2 + bg % 2, 0:C], w, (M.h_hi[:, k, T:TC], M.h_lo[:, k, T:TC]), f, z)
                last.then_inc(unit_done, 1)

        with pe.Fori(0, 5) as g:
            for s in range(4):
                p2_block(s, True, g)
        p2_block(20, True)
        with pe.Fori(0, 11) as g:
            for s in range(4):
                p2_block(21 + s, False, g)
        for b in (44, 45):
            p2_block(21 + b, False)

        def sum3(i):
            pe.wait_ge(pre_sq, i + 1)
            if i < 4:
                pe.matmul(ps[:, 0, :], M.ones[:, :], M.sq3[:, i % 2, 0:T], start=(i == 0), stop=(i == 3))
                pe.matmul(ps[:, 1, 0:C], M.ones[:, :], M.sq3[:, i % 2, T:TC], start=(i == 0), stop=(i == 3)
                          ).then_inc(pre_used, 1)
            else:
                pe.matmul(ps[:, 2, :], M.ones[:, :], M.sq3[:, i % 2, 0:T], start=(i == 4), stop=(i == 9)
                          ).then_inc(pre_used, 1)

        pe.wait_ge(p2_ev, 67 + 2)
        sum3(0)
        sum3(1)
        pe.wait_ge(ada2_used, 64 + 4)
        for j in range(64):
            if j in (6, 12):
                sum3(2 + j // 12)
            last = pe.matmul(ps[:, 7, j:j + 1], M.ada_sum[:, j * P:(j + 1) * P], M.ones[:, 0:1], start=True, stop=True)
        last.then_inc(mod2_ps, 1)
        pe.wait_ge(pre_ld, 64)
        pe.matmul(ps[:, 3, :], M.rotm[:, :], M.kpe[:, 0:T], start=True, stop=True).then_inc(kp_rot, 1)
        pe.wait_ge(pre_ok, 4)
        pe.wait_ge(mod2_ok, 1)
        for b in range(8):
            n = N_KN + b // 2
            w_ready(n)
            pe.wait_ge(pre_ev, b + 1)
            for k in range(4):
                w = w_at(n, 4 * (b % 2) + k)
                mm3(ps[:, 4 + b % 2, :], w, (M.ckv_hi[:, k, 0:T], M.ckv_lo[:, k, 0:T]), k == 0, k == 3)
                last = mm3(ps[:, 6 + b % 2, 0:C], w, (M.ckv_hi[:, k, T:TC], M.ckv_lo[:, k, T:TC]), k == 0, k == 3)
            last.then_inc(unit_done if b % 2 else kn_mm, 1)
            if b < 6:
                sum3(4 + b)
        for u in range(4):
            n = N_V + u
            w_ready(n)
            for t in range(6):
                e = 8 + 6 * u + t
                pe.wait_ge(pre_ev, e + 1)
                for k in range(4):
                    last = mm3(ps[:, 4 + e % 2, 0:256],
                               (M.ckv_hi[:, k, t * P:(t + 1) * P], M.ckv_lo[:, k, t * P:(t + 1) * P]),
                               (M.w_hi[:, n % RING, 256 * k:256 * (k + 1)], M.w_lo[:, n % RING, 256 * k:256 * (k + 1)]),
                               k == 0, k == 3)
                last.then_inc(unit_done if t == 5 else kn_mm, 1)
        pe.wait_ge(pre_ok, 10)

        def qb_block(s, base=0, g=None):
            n = N_QB + base + s
            w_ready(n, g, 4)
            pe.wait_ge(pre_ev, v(33 + base + s, g, 4))
            for k in range(6):
                last = mm3(ps[:, 4 + s % 2, :], w_at(n, k), (M.cq_hi[:, k, :], M.cq_lo[:, k, :]), k == 0, k == 5)
            last.then_inc(unit_done, 1)

        with pe.Fori(0, 2) as g:
            for s in range(4):
                qb_block(s, 0, g)
        for s in range(4):
            qb_block(s, 8)
            pe.wait_ge(rope_raw, s + 1)
            pe.matmul(ps[:, 2 + s % 2, :], M.rotm[:, :], M.mst[:, s % 2, 0:T], start=True, stop=True).then_inc(rope_rot, 1)

        pe.wait_ge(pre_ev, 44 + 2)
        def na_vt_(b, part, g=None):
            if part == 0:
                pe.wait_ge(na_ld, v(48 * (b + 1), g, 96))
            if g is not None or 3 * b + part >= 2:
                need = 3 * b + part - (1 if part == 2 else (1 if part == 0 else 2))
                pe.wait_ge(na_vlo, v(need, g, 6))
            for i in range(4 if part < 2 else 1):
                t = V_CHUNKS[4 * part + i]
                last = pe.transpose(ps[:, 6 + part % 2, i * P:(i + 1) * P], M.na_v[:, t:t + P], M.ident[:, :])
            last.then_inc(na_vt, 1)

        def na_s_(u, slot, g=None):
            h, j = u // 4, u % 4
            if u % 8 == 0:
                pe.wait_ge(na_split, v(u // 8 + 1, g, 2))
            if g is not None or u >= 2:
                pe.wait_ge(na_exp, v(u - 1, g, 16))
            qq = tuple(q[:, 2 * slot + h % 2, j * P:(j + 1) * P] for q in (M.qz_hi, M.qz_lo))
            mm3(ps[:, u % 2, 0:256], qq, tuple(k[:, slot, BAND[j]:BAND[j] + 256] for k in (M.k_hi, M.k_lo)), True, True)
            mm3(ps[:, u % 2, 256:512], qq, tuple(k[:, slot, T:TC] for k in (M.k_hi, M.k_lo)), True, True
                ).then_inc(na_s, 1)

        def na_pv_(u, slot, g=None):
            h, j = u // 4, u % 4
            if u % 8 == 0:
                pe.wait_ge(na_vlo, v(3 * (u // 8 + 1), g, 6))
            pe.wait_ge(na_pt, v(u + 1 + 2, g, 16))
            if j == 0:
                pe.wait_ge(na_o, v(h + 1, g, 4))
            for c in range(4):
                ch = V_OF[j][c] if c < 2 else 5 + c
                last = mm3(ps[:, 4 + h % 2, j * P:(j + 1) * P],
                           (M.v_hi[:, slot, ch, :], M.v_lo[:, slot, ch, :]),
                           (M.pt_hi[:, u % 2, c * P:(c + 1) * P], M.pt_lo[:, u % 2, c * P:(c + 1) * P]), c == 0, c == 3)
            last.then_inc(na_pv, 1)

        def na_pair(s, g=None, last=False, base=0):
            for u in range(8):
                uu = base + 8 * s + u
                if not (last and u >= 6):
                    na_s_(uu + 2, s if u < 6 else (s + 1) % 2, g)
                pe.wait_ge(na_p, v(uu + 1, g, 16))
                pe.wait_ge(na_pt, v(uu + 1, g, 16))
                for c in range(4):
                    t = pe.transpose(ps[:, 2 + u % 2, c * P:(c + 1) * P], M.na_p[:, u % 4, c * P:(c + 1) * P],
                                     M.ident[:, :])
                t.then_inc(na_t, 1)
                if u:
                    na_pv_(uu - 1, s, g)
                if not last and u in (2, 4, 6):
                    na_vt_(uu // 8 + 1, (u - 2) // 2, g)
            na_pv_(uu, s, g)

        for part in range(3):
            na_vt_(0, part)
        na_s_(0, 0)
        na_s_(1, 0)
        with pe.Fori(0, 3) as g:
            for s in range(2):
                na_pair(s, g)
        na_pair(0, base=48)
        na_pair(1, base=48, last=True)

        pe.wait_ge(ml_kplo, 1)
        pe.wait_ge(na_o, 16 + 2)

        def ml_s_(u, g=None):
            h, q = u // 4, u % 4
            if q == 0:
                pe.wait_ge(ml_lo, v(h + 1, g, 2))
            if g is not None or u >= 2:
                pe.wait_ge(na_exp, v(NA_UNITS + u - 1, g, 8))
            s = h % 2
            cols = slice(q * P, (q + 1) * P)
            for t0, t1, bank in ((0, T, 2 * (u % 2)), (T, TC, 2 * (u % 2) + 1)):
                out = ps[:, bank, 0:t1 - t0]
                mm3(out, (M.mq_hi[:, s, cols], M.mq_lo[:, s, cols]), (M.mk_hi[:, s, t0:t1], M.mk_lo[:, s, t0:t1]), True, False)
                last = mm3(out, (M.mqp_hi[:, s, cols], M.mqp_lo[:, s, cols]), (M.kp_hi[:, t0:t1], M.kp_lo[:, t0:t1]),
                           False, True)
            last.then_inc(ml_s, 1)

        def ml_pv_(h, g=None):
            s = h % 2
            pe.wait_ge(ml_pt, v(4 * h + 4 + 1, g, 8))
            pe.wait_ge(ml_o, v(h + 1, g, 2))
            for c in range(6):
                t = mm3(ps[:, 6 + s, :], (M.mv_hi[:, s, c, :], M.mv_lo[:, s, c, :]),
                        (M.mpt_hi[:, c, :], M.mpt_lo[:, c, :]), c == 0, c == 5)
            t.then_inc(ml_pv, 1)

        def ml_head(h, g=None, last=False):
            for q in range(4):
                u = 4 * h + q
                if not (last and q >= 2):
                    ml_s_(u + 2, g)
                pe.wait_ge(na_p, v(NA_UNITS + u + 1, g, 8))
                pe.wait_ge(ml_pt, v(u + 1, g, 8))
                for c in range(6):
                    t = pe.transpose(psf[:, 2048 + c * P:2048 + (c + 1) * P], M.ml_p[:, u % 4, c * P:(c + 1) * P],
                                     M.ident[:, :])
                t.then_inc(na_t, 1)
                if q == 0 and h:
                    ml_pv_(h - 1, g)

        ml_s_(0)
        ml_s_(1)
        ml_head(0)
        with pe.Fori(0, 3) as g:
            ml_head(1, g)
            ml_head(2, g)
        ml_head(7, last=True)
        ml_pv_(7)

        pe.wait_ge(ml_o, 8 + 2)
        with pe.Fori(0, 8) as g:
            for n in range(2):
                pe.wait_ge(mg_y, v(n + 1, g, 2))
                for i, (hi, lo) in enumerate(((M.oa_hi, M.oa_lo), (M.ob_hi, M.ob_lo))):
                    w_ready(N_MERGE + 2 * n + i, g, 4)
                    for k in range(8):
                        last = mm3(ps[:, 2 * n + i, :], w_at(N_MERGE + 2 * n + i, k), (hi[:, k, :], lo[:, k, :]),
                                   k == 0, k == 7)
                    last.then_inc(unit_done, 1)
        pe.wait_ge(mg_ylo, KD)

        def block16(n, bank, xh, xl, g, per, chunk_ready=None):
            for k in range(KD):
                if chunk_ready is not None:
                    pe.wait_ge(chunk_ready, k + 1)
                if k % 8 == 0:
                    w_ready(n + k // 8, g, per)
                last = mm3(ps[:, bank, :], w_at(n + k // 8, k % 8), (xh[:, k, :], xl[:, k, :]), k == 0, k == KD - 1)
                if k % 8 == 7:
                    last.then_inc(unit_done, 1)

        with pe.Fori(0, 8) as g:
            for n in range(2):
                pe.wait_ge(z_add, v(n + 1, g, 2))
                block16(N_OUT + 2 * n, 4 + n, M.y_hi, M.y_lo, g, 4)
        pe.wait_ge(z_add, KD + 2)
        pe.matmul(ps[:, 6, :], M.ones[:, :], M.ssum[:, :], start=True, stop=True).then_inc(ss_ok, 1)
        for k in range(KD):
            pe.wait_ge(z_sq, KD + k + 1)
            pe.matmul(ps[:, 7, :], M.ones[:, :], M.zsq[:, k % 2, :], start=(k == 0), stop=(k == KD - 1)
                      ).then_inc(z_add if k < KD - 1 else ss_ok, 1)


        with pe.Fori(0, 8) as g:
            for p in range(2):
                pe.wait_ge(q_l, v(p + 1, g, 2))
                block16(N_QUERY + 2 * p, p, M.h2_hi, M.h2_lo, g, 4, None if p else h2_ok)
            pe.wait_ge(sk_ok, 1)
            for p in range(2):
                pe.wait_ge(q_l, v(p + 1 + 2, g, 2))
                pe.wait_ge(sc_cp, v(p + 1, g, 2))
                keys = tuple(k[:, bass.ds(g * 2 + p, 1), :].rearrange("p a n -> p (a n)") for k in (M.sk_hi, M.sk_lo))
                for t in range(4):
                    last = mm3(ps[:, 2 + p, t * P:(t + 1) * P],
                               (M.q_hi[:, p, t * P:(t + 1) * P], M.q_lo[:, p, t * P:(t + 1) * P]), keys, True, True)
                last.then_inc(s_mm, 1)
        def exp_block(b, n, g=None):
            pe.wait_ge(m_gelu, v(b + 1, g, 8))
            block16(n, b % 2, M.h2_hi, M.h2_lo, g, 32)

        pe.wait_ge(q_l, 16 + 2)
        for b in range(4):
            exp_block(b, N_MAIN + 2 * b)
        pe.wait_ge(m_gelu, 4 + 2)
        pe.wait_ge(tk, 8 * CHOICE_STEPS)
        for x in range(3):
            for t in range(4):
                last = pe.transpose(ps[:, x, t * P:(t + 1) * P], M.sel[:, x, t, :], M.ident[:, :])
            last.then_inc(sel_t, 1)
        pe.wait_ge(selT_ok, 3)
        with pe.Fori(0, T // 32) as g:
            for s in range(4):
                pe.wait_ge(oh1_ok, v(s + 1, g, 4))
                pe.wait_ge(oh2_ok, v(s + 1, g, 4))
                for i in range(8):
                    if i % 4 == 0:
                        pe.wait_ge(g_ev, v(2 * s + i // 4 + 1, g, 8))
                    last = pe.matmul(ps[:, 2 * (s % 2) + i // 4, P * (i % 4):P * (i % 4 + 1)], M.oh2[:, s, i, :],
                                     M.oh1[:, s, i, :], start=True, stop=True)
                last.then_inc(g_mm, 1)

        def out_blocks(i, n, grp, g=None):
            pe.wait_ge(m_lo, v(i // 4 + 4, g, 8))
            for k in range(KD):
                if k % 2 == 0:
                    w_ready(n + k // 2, g, 32)
                pe.wait_ge(m_acc, v(i + k - 4 + 1 + 16, g, 32))
                for c in range(4):
                    last = mm3(ps[:, 2 + k % 4, :], w_at(n + k // 2, 4 * (k % 2) + c),
                               (M.ew_hi[:, 4 * grp + c, :], M.ew_lo[:, 4 * grp + c, :]), c == 0, c == 3)
                last.then_inc(unit_done if k % 2 else m_v, 1)

        pe.wait_ge(g_ev, T // 4 + 4)
        with pe.Fori(0, GROUPS // 2 - 1) as g:
            for r in range(2):
                for q in range(4):
                    exp_block(4 + 4 * r + q, N_MAIN + 8 + 16 * r + 2 * q, g)
                out_blocks(16 * r, N_MAIN + 16 + 16 * r, r, g)
        for q in range(4):
            exp_block(4 * GROUPS - 4 + q, N_END - 24 + 2 * q)
        out_blocks(16 * (GROUPS - 2), N_END - 16, 0)
        out_blocks(16 * (GROUPS - 1), N_END - 8, 1)
        pe.wait_ge(z_add, 2 * KD + 1 + KD + 1)
        pe.matmul(ps[:, 6, :], M.ones[:, :], M.fsum[:, :], start=True, stop=True).then_inc(ss_ok, 1)

    block.__exit__(None, None, None)


SCRATCH = {
    "projB": (BOTH_BLOCKS, P, TC), "projL": (LAT_BLOCKS, P, T), "bias_rows": (ROWS, 16, 512),
    "bias": (3, 16, P, 256), "qT": (12, P, T), "knT": (8, P, TC), "vmla": (6, P, 1024), "kp": (P, TC), "x1s": (P, KD, T),
    "gates": (T // TCH, P, P * TCH),
}


def layout(x, c, ctx, c_ctx, w_ada, b_ada, g_pre_mix, g_post_mix, g_pre_ffn, g_post_ffn, w_in, na_rpb,
           mla_g_q, mla_w_q_b, mla_g_kv, mla_w_kv_b, w_branch_a, w_branch_b, w_out,
           peer_w_query, peer_subkeys, peer_u, peer_v):
    f = np.float32

    def cols(w):
        k, n = w.shape
        return w.reshape(k // P, P, n // P, P).transpose(2, 1, 0, 3)

    def feat(x):
        return np.ascontiguousarray(x.T.reshape(-1, P, x.shape[0]).transpose(1, 0, 2))

    w = w_in[0]
    e = np.cumsum([0, 1024, 1024, 1024, 768, 512, 64, D, D])
    qa, ka, va, cq, ckv, kpe, ga, gb = (w[:, e[i]:e[i + 1]] for i in range(8))
    w2 = np.concatenate([ckv, kpe, kpe, ka, va, cq, qa, ga, gb], axis=1)
    units = [cols(w2).reshape(-1, P, 2, UW).transpose(0, 2, 1, 3).reshape(-1, P, UW)]
    wq = mla_w_q_b[0].reshape(768, 8, 192)
    wq = np.concatenate([wq[:, :, :128].reshape(768, 1024), wq[:, :, 128:].reshape(768, 512)], axis=1)
    wkv = mla_w_kv_b[0].reshape(512, 8, 256)
    units.append(cols(wkv[:, :, :128].reshape(512, 1024)).reshape(4, 2, P, 512).transpose(0, 2, 1, 3).reshape(4, P, UW))
    units.append(wkv[:, :, 128:].reshape(4, P, 4, 256).transpose(2, 1, 0, 3).reshape(4, P, UW))
    units.append(np.concatenate([cols(wq).reshape(12, P, 768), np.zeros((12, P, 256), f)], axis=2))
    ab = np.stack([cols(w_branch_a[0]).reshape(16, P, UW), cols(w_branch_b[0]).reshape(16, P, UW)], axis=1)
    units.append(ab.reshape(32, P, UW))
    for w in (w_out[0], peer_w_query[0]):
        units.append(cols(w).reshape(-1, P, 2, UW).transpose(0, 2, 1, 3).reshape(-1, P, UW))
    u = cols(peer_u[0].T).reshape(P, P, 2, UW).transpose(0, 2, 1, 3).reshape(GROUPS, 8, P, UW)
    vv = peer_v[0].reshape(GROUPS, 4, P, 8, 2, P).transpose(0, 3, 2, 4, 1, 5).reshape(GROUPS, 8, P, UW)
    body = [u[0]]
    for g in range(1, GROUPS):
        body += [u[g], vv[g - 1]]
    body.append(vv[GROUPS - 1])
    units += body
    wall = np.concatenate(units, axis=0)
    assert wall.shape[0] == N_END, wall.shape
    wa = w_ada[0]
    tok = x[0].reshape(ROWS, GRID_W, D).transpose(1, 0, 2).reshape(T, D)
    vec = np.concatenate([b_ada[0].reshape(96, P), g_pre_mix[0].reshape(KD, P), g_post_mix[0].reshape(KD, P),
                          g_pre_ffn[0].reshape(KD, P), g_post_ffn[0].reshape(KD, P), mla_g_q[0].reshape(6, P),
                          mla_g_kv[0].reshape(4, P)], axis=0)
    t = np.arange(T)
    row, col = (t % ROWS).astype(f), (t // ROWS).astype(f)
    inv = (10000.0 ** (-np.arange(16, dtype=f) / f(16))).astype(f)
    ang = np.concatenate([row[:, None] * inv, col[:, None] * inv], axis=1).T
    cos, sin = np.cos(ang).astype(f), np.sin(ang).astype(f)
    rot = np.zeros((P, P), f)
    for b in range(2):
        for i in range(32):
            rot[64 * b + 32 + i, 64 * b + i] = -1.0
            rot[64 * b + i, 64 * b + 32 + i] = 1.0
    mask = np.zeros((P, 4, 256), f)
    for j in range(4):
        qc = 16 * j + np.arange(P) // ROWS
        kc = BAND[j] // ROWS + np.arange(256) // ROWS
        off = kc[None, :] - np.clip(qc - 8, 0, GRID_W - 16)[:, None]
        mask[:, j] = np.where((off >= 0) & (off < 16), 0.0, -1e30)
    return {
        "wall": wall,
        "ada1": np.ascontiguousarray(wa[:, :4096].reshape(KD, P, 2, 2048).transpose(2, 0, 1, 3)).reshape(32, P, 2048),
        "ada2": np.ascontiguousarray(wa[:, 4096:].reshape(KD, P, 4, 2048).transpose(0, 2, 1, 3)),
        "xT": feat(tok), "ctxT": feat(ctx[0]),
        "cvec": np.ascontiguousarray(np.stack([c[0], c_ctx], axis=1).reshape(KD, P, 2).transpose(1, 0, 2).reshape(P, 32)),
        "vecs": np.ascontiguousarray(vec.T),
        "rpb": np.ascontiguousarray(na_rpb[0].transpose(0, 2, 1)),
        "subk": np.ascontiguousarray(peer_subkeys[0].transpose(3, 0, 1, 2).reshape(P, 16, P)),
        "consts": np.stack([np.ones((P, P), f), np.eye(P, dtype=f), np.tile(np.arange(P, dtype=f), (P, 1)), rot]),
        "rope": np.stack([np.tile(cos, (4, 1)), np.tile(sin, (4, 1))]),
        "maskc": mask,
    }


def kernel(**inputs):
    from concourse.bass_utils import run_bass_kernel_spmd as run
    import concourse.bacc as bacc

    arrays = layout(**{k: np.asarray(x) for k, x in inputs.items()})
    nc = bacc.Bacc("TRN2", target_bir_lowering=False, num_devices=1)
    a = {k: nc.dram_tensor(k, x.shape, F32, kind="ExternalInput").ap() for k, x in arrays.items()}
    for k, shape in SCRATCH.items():
        a[k] = nc.dram_tensor(k, shape, F32, kind="Internal").ap()
    a["out"] = nc.dram_tensor("out", (P, KD, T), F32, kind="ExternalOutput").ap()
    build(nc, a)
    r = run(nc, [arrays], core_ids=[0]).results[0]
    o = r["out"].transpose(1, 0, 2).reshape(D, GRID_W, ROWS).transpose(2, 1, 0).reshape(1, T, D)
    return np.ascontiguousarray(o)
```
